# Optimizing a Trainium2 kernel written in Bass

```python
import jax
import jax.numpy as jnp
from jax import lax
import numpy as np

D_MODEL = 1024
BATCH = 1
SEQ = 256
DEPTH = 2
DEC_BATCH = 8
DEC_SEQ = 8
PAST_LEN = 256
PAGE_SIZE = 128

HEAD_DIM = 64
N_HEADS = (D_MODEL // 2) // HEAD_DIM
KV_HEADS = 2
IDX_HEADS = 8
IDX_DIM = 64
TOPK_MAX = 256
Q_BLOCK = 128
HG_KDIM = 128
HG_VDIM = 128
HG_HEADS = (D_MODEL // 2) // HG_VDIM
HG_CHUNK = 64
D_FF = 2816
P_DIM = 256
ROPE_THETA = 10000.0
EPS = 1e-6
ATT_WIDTH = N_HEADS * HEAD_DIM
HG_WIDTH = HG_HEADS * HG_VDIM
MIX_WIDTH = ATT_WIDTH + HG_WIDTH
SPLITS = (ATT_WIDTH, KV_HEADS * HEAD_DIM, KV_HEADS * HEAD_DIM,
          IDX_HEADS * IDX_DIM, IDX_DIM, IDX_HEADS,
          HG_HEADS * HG_KDIM, HG_HEADS * HG_KDIM, HG_WIDTH, HG_WIDTH)
IN_WIDTH = sum(SPLITS)

kernel_name = 'hymba_hgrn2_dsa_macaron_step'

def rmsnorm(x, g):
    xf = x.astype(jnp.float32)
    y = xf * lax.rsqrt(jnp.mean(xf * xf, axis=-1, keepdims=True) + EPS)
    return (y * g.astype(jnp.float32)).astype(x.dtype)

def swiglu(x, w_gate, w_up, w_down):
    return (jax.nn.silu(x @ w_gate) * (x @ w_up)) @ w_down

def rope(x, pos):
    half = x.shape[-1] // 2
    inv_freq = ROPE_THETA ** (-jnp.arange(half, dtype=jnp.float32) / half)
    ang = pos.astype(jnp.float32)[:, None] * inv_freq[None, :]
    cos = jnp.cos(ang)[None, :, None, :]
    sin = jnp.sin(ang)[None, :, None, :]
    xf = x.astype(jnp.float32)
    x1, x2 = xf[..., :half], xf[..., half:]
    return jnp.concatenate([x1 * cos - x2 * sin, x2 * cos + x1 * sin], axis=-1).astype(x.dtype)

def gather_pages(pool, page_table):
    g = pool[page_table]
    return g.reshape((g.shape[0], g.shape[1] * g.shape[2]) + g.shape[3:])

def hgrn_lower_bounds(logits):
    sm = jax.nn.softmax(logits.astype(jnp.float32), axis=0)
    return jnp.cumsum(sm, axis=0) - sm[0:1]

def hgrn2(q, f_logit, i, lb, s0):
    B, T, _ = q.shape
    f = lb + (1.0 - lb) * jax.nn.sigmoid(f_logit.astype(jnp.float32))
    logf = jnp.log(f)
    k = 1.0 - f
    qf = jax.nn.silu(q.astype(jnp.float32)) * (HG_KDIM ** -0.5)
    v = i.astype(jnp.float32)
    C = min(HG_CHUNK, T)
    nc = -(-T // C)
    pad = nc * C - T

    def heads(a, d):
        a = a.reshape(B, T, HG_HEADS, d)
        a = jnp.pad(a, ((0, 0), (0, pad), (0, 0), (0, 0)))
        return a.reshape(B, nc, C, HG_HEADS, d).transpose(1, 0, 3, 2, 4)

    qs, ks, gs, vs = heads(qf, HG_KDIM), heads(k, HG_KDIM), heads(logf, HG_KDIM), heads(v, HG_VDIM)
    causal = jnp.tril(jnp.ones((C, C), dtype=bool))[:, :, None]

    def step(S, xs):
        qc, kc, gc, vc = xs
        b = jnp.cumsum(gc, axis=2)
        o_inter = jnp.einsum('bhtd,bhde->bhte', qc * jnp.exp(b), S)
        diff = b[:, :, :, None, :] - b[:, :, None, :, :]
        decay = jnp.where(causal, jnp.exp(jnp.where(causal, diff, 0.0)), 0.0)
        att = jnp.einsum('bhtd,bhsd,bhtsd->bhts', qc, kc, decay)
        o = o_inter + jnp.einsum('bhts,bhse->bhte', att, vc)
        b_last = b[:, :, -1:, :]
        S_new = jnp.exp(b_last[:, :, 0, :])[..., None] * S + jnp.einsum(
            'bhsd,bhse->bhde', kc * jnp.exp(b_last - b), vc)
        return S_new, o

    s_fin, outs = lax.scan(step, s0, (qs, ks, gs, vs))
    o = outs.transpose(1, 0, 3, 2, 4).reshape(B, nc * C, HG_HEADS, HG_VDIM)[:, :T]
    return o, s_fin

def dsa_attention(q, k_all, v_all, iq, ik_all, iw, q_pos):
    B, Tq = q.shape[:2]
    L = k_all.shape[1]
    topk = min(TOPK_MAX, L // 4)
    qb = min(Q_BLOCK, Tq)
    nb = -(-Tq // qb)
    pad = nb * qb - Tq
    key_pos = jnp.arange(L, dtype=jnp.int32)
    bidx = jnp.arange(B)[:, None, None]
    ikf = ik_all.astype(jnp.float32)
    group = N_HEADS // KV_HEADS

    def blocks(a):
        a = jnp.pad(a, [(0, 0), (0, pad)] + [(0, 0)] * (a.ndim - 2))
        return jnp.moveaxis(a.reshape((B, nb, qb) + a.shape[2:]), 1, 0)

    pos_b = jnp.pad(q_pos, (0, pad), mode='edge').reshape(nb, qb)

    def one_block(xs):
        qx, iqx, iwx, px = xs
        logits = jnp.einsum('bqhd,bsd->bqhs', iqx.astype(jnp.float32), ikf) * (IDX_DIM ** -0.5)
        score = jnp.einsum('bqh,bqhs->bqs', iwx.astype(jnp.float32), jax.nn.relu(logits))
        admissible = key_pos[None, None, :] <= px[None, :, None]
        score = jnp.where(admissible, score, -jnp.inf)
        _, sel = lax.top_k(score, topk)
        valid = sel <= px[None, :, None]
        k_sel = k_all[bidx, sel].astype(jnp.float32)
        v_sel = v_all[bidx, sel].astype(jnp.float32)
        qg = qx.astype(jnp.float32).reshape(B, qb, KV_HEADS, group, HEAD_DIM)
        s = jnp.einsum('bqhgd,bqjhd->bqhgj', qg, k_sel) * (HEAD_DIM ** -0.5)
        s = jnp.where(valid[:, :, None, None, :], s, -jnp.inf)
        p = jax.nn.softmax(s, axis=-1)
        o = jnp.einsum('bqhgj,bqjhd->bqhgd', p, v_sel)
        return o.reshape(B, qb, ATT_WIDTH).astype(q.dtype)

    out = lax.map(one_block, (blocks(q), blocks(iq), blocks(iw), pos_b))
    return jnp.moveaxis(out, 0, 1).reshape(B, nb * qb, ATT_WIDTH)[:, :Tq]

def decoder_layer(x, p_emb, q_pos, past_k, past_v, past_ik, s0, lb,
                  n_f1_pre, n_f1_post, w_f1_gate, w_f1_up, w_f1_down,
                  n_mix_pre, n_mix_post, w_in, hg_norm, w_out,
                  n_f2_pre, n_f2_post, w_f2_gate, w_f2_up, w_f2_down,
                  n_ple_pre, n_ple_post, w_ple_proj, w_ple_gate):
    B, T, _ = x.shape
    h = x + 0.5 * rmsnorm(swiglu(rmsnorm(x, n_f1_pre), w_f1_gate, w_f1_up, w_f1_down), n_f1_post)
    u = rmsnorm(h, n_mix_pre)
    proj = u @ w_in
    cuts = []
    acc = 0
    for width in SPLITS[:-1]:
        acc += width
        cuts.append(acc)
    q, k, v, iq, ik, iw, hq, hf, hi, hgate = jnp.split(proj, cuts, axis=-1)
    q = rope(q.reshape(B, T, N_HEADS, HEAD_DIM), q_pos)
    k = rope(k.reshape(B, T, KV_HEADS, HEAD_DIM), q_pos)
    v = v.reshape(B, T, KV_HEADS, HEAD_DIM)
    iq = rope(iq.reshape(B, T, IDX_HEADS, IDX_DIM), q_pos)
    ik = rope(ik.reshape(B, T, 1, IDX_DIM), q_pos)[:, :, 0]
    iw = iw * (IDX_HEADS ** -0.5)
    if past_k is None:
        k_all, v_all, ik_all = k, v, ik
    else:
        k_all = jnp.concatenate([past_k.astype(k.dtype), k], axis=1)
        v_all = jnp.concatenate([past_v.astype(v.dtype), v], axis=1)
        ik_all = jnp.concatenate([past_ik.astype(ik.dtype), ik], axis=1)
    att = dsa_attention(q, k_all, v_all, iq, ik_all, iw, q_pos)
    o_hg, s_fin = hgrn2(hq, hf, hi, lb, s0)
    o_hg = rmsnorm(o_hg, hg_norm) * jax.nn.silu(hgate.reshape(B, T, HG_HEADS, HG_VDIM).astype(jnp.float32))
    mix = jnp.concatenate([att, o_hg.reshape(B, T, HG_WIDTH).astype(att.dtype)], axis=-1) @ w_out
    h = h + rmsnorm(mix, n_mix_post)
    h = h + 0.5 * rmsnorm(swiglu(rmsnorm(h, n_f2_pre), w_f2_gate, w_f2_up, w_f2_down), n_f2_post)
    gate = jax.nn.sigmoid(rmsnorm(h, n_ple_pre) @ w_ple_gate)
    h = h + rmsnorm((p_emb.astype(h.dtype) @ w_ple_proj) * gate, n_ple_post)
    return h, k, v, ik, s_fin

def _normal(k, shape, scale):
    return scale * jax.random.normal(k, shape, jnp.float32)

def _gain(k, shape):
    return 1.0 + 0.02 * jax.random.normal(k, shape, jnp.float32)

def setup_inputs(seed: int = 0) -> dict:
    key = jax.random.key(seed)
    k = jax.random.split(key, 32)
    n_pages = PAST_LEN // PAGE_SIZE
    n_used = DEC_BATCH * n_pages
    n_pool = n_used + max(1, n_used // 4)
    page_table = jax.random.permutation(k[8], n_pool)[:n_used].reshape(DEC_BATCH, n_pages).astype(jnp.int32)
    d = D_MODEL
    return {
        'x_prompt': _normal(k[0], (BATCH, SEQ, d), 1.0),
        'x_sample': _normal(k[1], (DEC_BATCH, DEC_SEQ, d), 1.0),
        'p_prompt': _normal(k[2], (DEPTH, BATCH, SEQ, P_DIM), 1.0),
        'p_sample': _normal(k[3], (DEPTH, DEC_BATCH, DEC_SEQ, P_DIM), 1.0),
        'cache_k': _normal(k[4], (DEPTH, n_pool, PAGE_SIZE, KV_HEADS, HEAD_DIM), 1.0),
        'cache_v': _normal(k[5], (DEPTH, n_pool, PAGE_SIZE, KV_HEADS, HEAD_DIM), 1.0),
        'cache_idx_k': _normal(k[6], (DEPTH, n_pool, PAGE_SIZE, IDX_DIM), 1.0),
        'state_hgrn': _normal(k[7], (DEPTH, DEC_BATCH, HG_HEADS, HG_KDIM, HG_VDIM), 1.0),
        'page_table': page_table,
        'n_f1_pre': _gain(k[9], (DEPTH, d)),
        'n_f1_post': _gain(k[10], (DEPTH, d)),
        'w_f1_gate': _normal(k[11], (DEPTH, d, D_FF), d ** -0.5),
        'w_f1_up': _normal(k[12], (DEPTH, d, D_FF), d ** -0.5),
        'w_f1_down': _normal(k[13], (DEPTH, D_FF, d), D_FF ** -0.5),
        'n_mix_pre': _gain(k[14], (DEPTH, d)),
        'n_mix_post': _gain(k[15], (DEPTH, d)),
        'w_in': _normal(k[16], (DEPTH, d, IN_WIDTH), d ** -0.5),
        'hg_lb_logits': _normal(k[17], (DEPTH, HG_HEADS * HG_KDIM), 0.5),
        'hg_norm': _gain(k[18], (DEPTH, HG_VDIM)),
        'w_out': _normal(k[19], (DEPTH, MIX_WIDTH, d), MIX_WIDTH ** -0.5),
        'n_f2_pre': _gain(k[20], (DEPTH, d)),
        'n_f2_post': _gain(k[21], (DEPTH, d)),
        'w_f2_gate': _normal(k[22], (DEPTH, d, D_FF), d ** -0.5),
        'w_f2_up': _normal(k[23], (DEPTH, d, D_FF), d ** -0.5),
        'w_f2_down': _normal(k[24], (DEPTH, D_FF, d), D_FF ** -0.5),
        'n_ple_pre': _gain(k[25], (DEPTH, d)),
        'n_ple_post': _gain(k[26], (DEPTH, d)),
        'w_ple_proj': _normal(k[27], (DEPTH, P_DIM, d), P_DIM ** -0.5),
        'w_ple_gate': _normal(k[28], (DEPTH, d, d), d ** -0.5),
    }

def reference(x_prompt, x_sample, p_prompt, p_sample, cache_k, cache_v, cache_idx_k, state_hgrn, page_table,
              n_f1_pre, n_f1_post, w_f1_gate, w_f1_up, w_f1_down,
              n_mix_pre, n_mix_post, w_in, hg_lb_logits, hg_norm, w_out,
              n_f2_pre, n_f2_post, w_f2_gate, w_f2_up, w_f2_down,
              n_ple_pre, n_ple_post, w_ple_proj, w_ple_gate):
    bp, tp = x_prompt.shape[:2]
    ts = x_sample.shape[1]
    past_len = page_table.shape[1] * cache_k.shape[2]
    pos_p = jnp.arange(tp, dtype=jnp.int32)
    pos_s = past_len + jnp.arange(ts, dtype=jnp.int32)
    lbs = hgrn_lower_bounds(hg_lb_logits)
    s0_prompt = jnp.zeros((bp, HG_HEADS, HG_KDIM, HG_VDIM), jnp.float32)
    hp, hs = x_prompt, x_sample
    kp_l, vp_l, ikp_l, sp_l = [], [], [], []
    ks_l, vs_l, iks_l, ss_l = [], [], [], []
    for i in range(DEPTH):
        lw = (n_f1_pre[i], n_f1_post[i], w_f1_gate[i], w_f1_up[i], w_f1_down[i],
              n_mix_pre[i], n_mix_post[i], w_in[i], hg_norm[i], w_out[i],
              n_f2_pre[i], n_f2_post[i], w_f2_gate[i], w_f2_up[i], w_f2_down[i],
              n_ple_pre[i], n_ple_post[i], w_ple_proj[i], w_ple_gate[i])
        hp, k1, v1, ik1, s1 = decoder_layer(hp, p_prompt[i], pos_p, None, None, None,
                                            s0_prompt, lbs[i], *lw)
        hs, k2, v2, ik2, s2 = decoder_layer(hs, p_sample[i], pos_s,
                                            gather_pages(cache_k[i], page_table),
                                            gather_pages(cache_v[i], page_table),
                                            gather_pages(cache_idx_k[i], page_table),
                                            state_hgrn[i].astype(jnp.float32), lbs[i], *lw)
        kp_l.append(k1); vp_l.append(v1); ikp_l.append(ik1); sp_l.append(s1.astype(x_prompt.dtype))
        ks_l.append(k2); vs_l.append(v2); iks_l.append(ik2); ss_l.append(s2.astype(state_hgrn.dtype))
    k_prompt = jnp.stack(kp_l)
    v_prompt = jnp.stack(vp_l)
    idx_k_prompt = jnp.stack(ikp_l)
    hgrn_prompt = jnp.stack(sp_l)
    k_sample = jnp.stack(ks_l)
    v_sample = jnp.stack(vs_l)
    idx_k_sample = jnp.stack(iks_l)
    hgrn_sample = jnp.stack(ss_l)
    return (hp, hs, k_prompt, v_prompt, idx_k_prompt, hgrn_prompt, k_sample, v_sample, idx_k_sample, hgrn_sample)


_drawn_inputs = setup_inputs


def setup_inputs(seed=0):
    import zlib

    import numpy as np

    out = dict(_drawn_inputs(seed))
    spreads = {}
    factors = {'n_f2_pre': 3.059, 'n_f2_post': 3.668, 'n_ple_pre': 17.627, 'n_ple_post': 3.544}
    for name, (base, spread) in spreads.items():
        noise = np.random.default_rng([zlib.crc32(name.encode()), seed]).standard_normal(out[name].shape)
        drawn = base * np.exp(spread * noise) if base else spread * noise
        out[name] = jnp.asarray(drawn.astype(out[name].dtype))
    for name, factor in factors.items():
        out[name] = (out[name] * factor).astype(out[name].dtype)
    return out
```

```python
import numpy as np
import concourse.bass as bass
from concourse import mybir
from contextlib import ExitStack

F32 = mybir.dt.float32
F32R = mybir.dt.float32r
U8 = mybir.dt.uint8
I32 = mybir.dt.int32
ALU = mybir.AluOpType
ACT = mybir.ActivationFunctionType
AX = mybir.AxisListType

P = 128
LAYERS = 2
DM, KT = 1024, 8
TP, TS = 256, 64
T = TP + TS
SEQS, STEP = 8, 8
TOK_TILES = [(0, 128), (128, 128), (256, 64)]
FF = 2816
FT = FF // P
HD, NH, KVH, GROUP = 64, 8, 2, 4
PAGE, NPAGES = 128, 2
PAST = PAGE * NPAGES
HG = 4
PD = 256
EPS = 1e-6
NEG = -1e30
TAKEN = -3e38
SENTINEL = 3e38
TOPK_P, TOPK_S = TP // 4, (PAST + STEP) // 4
ROUNDS_P = TOPK_P // 8
ROUNDS_S = -(-TOPK_S // 8)
PADS = ROUNDS_S * 8 - TOPK_S
KEYS_S = PAST + TS
CHUNK = 128
LEVELS = [1, 2, 4, 8, 16, 32, 64]

C_Q, C_K, C_V, C_IQ, C_IK, C_IW = 0, 512, 640, 768, 1280, 1344
C_HQ, C_HF, C_HI, C_HG = 1352, 1864, 2376, 2888

LOADS = []
for t in range(FT):
    LOADS.append(("gateup1", t, 1))
for j in range(KT):
    LOADS.append(("down1", j, 1))
for kind, count, tiles in (("iq", 2, 2), ("kv", 1, 3), ("ikiw", 1, 3), ("hf", 2, 2), ("hq", 2, 2),
                           ("q", 2, 2), ("hi", 2, 3), ("hgate", 2, 2), ("out", 4, 2)):
    for i in range(count):
        LOADS.append((kind, i, tiles))
for t in range(FT):
    LOADS.append(("gateup2", t, 1))
for j in range(KT):
    LOADS.append(("down2", j, 1))
for i in range(4):
    LOADS.append(("ple", i, 2))
assert len(LOADS) % 2 == 0
LOAD_AT = {(k, i): n for n, (k, i, _) in enumerate(LOADS)}
TILES_BEFORE = [sum(x[2] for x in LOADS[:n]) for n in range(len(LOADS) + 1)]
TILES = TILES_BEFORE[-1]
SLOT = FT * P


def tile_at(kind, i, k=0):
    return TILES_BEFORE[LOAD_AT[kind, i]] + k


def dmas_of(kind):
    return {"gateup1": 2, "gateup2": 2, "iq": 4, "q": 4, "out": 3, "ple": 2}.get(kind, 1)


SPLIT_KINDS = ("gateup1", "down1", "gateup2", "down2")
SPLITS = FT + KT
assert FT % 2 == 0 and KT % 2 == 0


def splits_before(n):
    return sum(LOADS[m][0] in SPLIT_KINDS for m in range(n))


def dma_count_before(n):
    return sum(16 * dmas_of(LOADS[m][0]) for m in range(n % 2, n, 2))


def DMAS(n):
    return dmas_of(LOADS[n][0])


def _order(names):
    return {name: n for n, name in enumerate(names)}


AUXD = _order(["r_tok", "rot_iq0", "rot_iq1", "rot_iq2", "rot_iq3", "iwT", "iwrow", "score_s",
               "rot_q0", "rot_q1", "rot_q2", "rot_q3", "state0", "state1"]
              + [f"ms_o{h}" for h in range(HG)]
              + [f"state_s{h}{c}" for h in range(HG) for c in "ab"] + ["pv1", "pv0", "pvs"])
AUXA = _order(["p0", "p1"] + [f"kpages{k}" for k in range(4)] + [f"ipages{k}" for k in range(4)]
              + ["kT", "ikT", "key0", "key1", "key2"] + [f"o{h}" for h in range(HG)]
              + ["pT1_00", "pT1_01", "pT1_10", "pT1_11", "pT0_00", "pT0_01", "pTs0", "pTs1", "pTs2"])
LEVEL_BIG, _n = [], 10 + 3
for _h in LEVELS:
    LEVEL_BIG.append(list(range(_n, _n + (3 if 2 * _h <= STEP else 2))))
    _n = LEVEL_BIG[-1][-1] + 1
BIG = {"idx": 0, "levels": 10, "att": _n, "att_s": _n + 4, "att0": _n + 8}


def BIGD_BEFORE(n):
    return n - BIG["levels"]


EV = {"score1": 1, "score0": 2}
MIX_LAST = {kind: tile_at(kind, *last) - tile_at("iq", 0) + 1 for kind, last in (
    ("kv", (0, 2)), ("ikiw", (0, 2)), ("hf", (1, 1)), ("hq", (1, 1)), ("hi", (1, 2)), ("hgate", (1, 1)))}
HGD = {"f": 1, "silu": 2, "scan": 3}


def level_view(t, h):
    if 2 * h <= STEP:
        v = t[:, :, :].rearrange("p g (n two s) -> p (g n) two s", two=2, s=h)
        return v[:, :, 0, :], v[:, :, 1, :]
    v = t[:, :, 0:TP].rearrange("p g (n two s) -> p g n two s", two=2, s=h)
    return v[:, :, :, 0, :], v[:, :, :, 1, :]


def constants():
    f = np.float32
    pos = np.concatenate([np.arange(TP), np.tile(PAST + np.arange(STEP), SEQS)]).astype(f)
    half = HD // 2
    inv = (f(10000.0) ** (-np.arange(half, dtype=f) / f(half))).astype(f)
    ang = (pos[:, None] * inv[None, :]).astype(f).astype(np.float64)
    cos, sin = np.cos(ang).astype(f), np.sin(ang).astype(f)
    c = {}
    c["cos_f"] = np.tile(cos.T, (4, 1))
    c["sin_f"] = np.tile(sin.T, (4, 1))
    tok = np.zeros((2, P, 3, half), f)
    for i, (a, n) in enumerate(TOK_TILES):
        tok[0, :n, i], tok[1, :n, i] = cos[a:a + n], sin[a:a + n]
    c["cos_t"], c["sin_t"] = tok[0].reshape(P, -1), tok[1].reshape(P, -1)
    rot = np.zeros((P, P), f)
    for m in range(P):
        if m % HD < half:
            rot[m + half, m] = -1
        else:
            rot[m - half, m] = 1
    c["rotate"] = rot
    c["identity"] = np.eye(P, dtype=f)
    c["mean_model"] = np.full((P, P), 1.0 / DM, f)
    c["mean_head"] = np.full((P, P), 1.0 / P, f)
    s, t = np.arange(P)[:, None], np.arange(P)[None, :]
    c["level_masks"] = np.stack(
        [((s // (2 * h) == t // (2 * h)) & (s % (2 * h) < h) & (t % (2 * h) >= h)) for h in LEVELS],
        1).astype(f).reshape(P, -1)
    fill = np.zeros((P, 128 + 256), f)
    fill[:, :128] = np.where(t > s, f(NEG), f(0))
    fill[:, 256:] = np.where(t > s, f(NEG), f(0))
    c["causal"] = fill
    a, b = np.arange(TS)[:, None], np.arange(TS)[None, :]
    c["causal_s"] = np.where((a // STEP == b // STEP) & (b % STEP <= a % STEP), f(0), f(NEG)).astype(f)
    spread = np.zeros((TS, 4, P), f)
    for pair in range(4):
        for r in range(P):
            spread[(2 * pair + r // 64) * STEP + r % STEP, pair, r] = 1
    c["spread"] = spread.reshape(TS, -1)
    c["own_token"] = spread.transpose(2, 1, 0).reshape(P, -1).copy()
    head = np.zeros((NH, P), f)
    for r in range(P):
        head[(r % 64) // STEP, r] = 1
    c["head_row"] = head
    reset = np.ones((P, T), f)
    reset[:, 0:TP:CHUNK] = 0
    reset[:, TP::STEP] = 0
    c["carry"] = reset
    own = np.zeros((TS, SEQS), f)
    for r in range(TS):
        own[r, r // STEP] = 1
    c["own_seq"] = own
    return c


class Signal:

    def __init__(self, nc, ctx, name, totals):
        self.sem = ctx.enter_context(nc.semaphore(name))
        self.name = name
        self.before, self.each, _ = totals.get(name, (0, 0, 0))
        self.seen = [0, 0, 0]

    def at(self, layer, n):
        assert self.each == 0 or self.before + n >= 1, (self.name, n)
        return layer * self.each + (self.before + n)


CONST_NAMES = list(constants())


class Counts:

    def __init__(self):
        self.in_layer, self.times = 0, 1

    def inc(self, sig, by=1):
        sig.seen[self.in_layer] += by * self.times
        return sig.sem, by


def build(nc, A, O, totals):
    ctx = ExitStack()
    counts = Counts()
    signals = {}

    def sig(name):
        signals[name] = Signal(nc, ctx, name, totals)
        return signals[name]

    def once(s):
        return counts.inc(s, 1)

    def dma(s):
        return counts.inc(s, 16)

    with ctx:
        pool_pages = A["cache_k"].shape[1]
        base = -(-nc.sbuf_base // 32) * 32
        cursor = [base]

        def place(name, shape, dt=F32, at=None):
            size = int(np.prod(shape[1:])) * (1 if dt == U8 else 4)
            size = -(-size // 32) * 32
            off = at
            if at is None:
                off = cursor[0]
                cursor[0] += size
            return nc.alloc_sbuf_tensor_at(name, list(shape), dt, offset=off)

        x = place("x", [P, KT, T])
        u_at = cursor[0]
        u = place("u", [P, KT, T])
        slots = [place(f"slot{i}", [P, SLOT]) for i in range(2)]
        cos_f, sin_f = place("cos_f", [P, T]), place("sin_f", [P, T])
        cos_t, sin_t = place("cos_t", [P, 3, 32]), place("sin_t", [P, 3, 32])
        rotate, identity = place("rotate", [P, P]), place("identity", [P, P])
        mean_model, mean_head = place("mean_model", [P, P]), place("mean_head", [P, P])
        level_masks = place("level_masks", [P, len(LEVELS), P], U8)
        causal, causal_s = place("causal", [P, 384]), place("causal_s", [TS, TS])
        spread, own_token = place("spread", [TS, 4, P]), place("own_token", [P, 4, TS])
        head_row, carry = place("head_row", [NH, P]), place("carry", [P, T])
        own_seq = place("own_seq", [TS, SEQS])
        gains = place("gains", [P, 8, LAYERS, KT])
        small = place("small", [P, 10])
        bounds = place("bounds", [P, LAYERS, HG])
        bounds_tmp = place("bounds_tmp", [P, 5, HG])
        gain = place("gain", [P, 8, KT])
        bound = place("bound", [P, 3, HG])
        pT = place("pT", [P, 2, T])
        r_pre, r_post = place("r_pre", [P, T]), place("r_post", [P, T])
        inv_pre, inv_post = r_pre, r_post
        sq, sumsq = place("sq", [P, 2, T]), place("sumsq", [P, T])
        sqx, sumsqx = place("sqx", [P, 2, T]), place("sumsqx", [P, T])
        ffn_small = cursor[0]
        kT, ikT = place("kT", [P, T]), place("ikT", [P, T])
        rope_tmp = place("rope_tmp", [P, 2, T])
        iw_mask = place("iw_mask", [P, 4, TS])
        score0, score1 = place("score0", [P, 128]), place("score1", [P, 256])
        score_s = place("score_s", [TS, PADS + KEYS_S])
        assert cursor[0] - ffn_small >= 4 * 6 * T
        kv_tok = place("kv_tok", [P, 3, 256])
        ik_tok, iw_tok = place("ik_tok", [P, 3, 128]), place("iw_tok", [P, 3, NH])
        r_tok = place("r_tok", [P, 3])
        iwT = place("iwT", [NH, TS])
        top8 = place("top8", [P, 8])
        peak, total = place("peak", [P, 3, NH]), place("total", [P, 3, NH])
        mixed_at = cursor[0]
        mixed = place("mixed", [P, KT, T])
        shared = cursor[0]
        hidden_hi, hidden_lo = (place(f"hidden_{a}", [P, FT, T], F32R) for a in ("hi", "lo"))
        y = place("y", [P, KT, T])
        hidden_tmp = place("hidden_tmp", [P, 2, T])
        slot_hi = [place(f"slot{i}_hi", [P, SLOT], F32R) for i in range(2)]
        slot_lo = [place(f"slot{i}_lo", [P, SLOT], F32R) for i in range(2)]
        gate_in = place("gate_in", [P, 2, T], at=ffn_small)
        gate_out = place("gate_out", [P, 2, T], at=ffn_small + 4 * 2 * T)
        up_out = place("up_out", [P, 2, T], at=ffn_small + 4 * 4 * T)
        u_hi = place("u_hi", [P, KT, T], F32R, at=u_at)
        u_lo = place("u_lo", [P, KT, T], F32R, at=mixed_at)
        ffn_end = cursor[0]
        tokens = place("tokens", [P, 3, DM], at=shared)
        rows_a = place("rows_a", [P, P], at=shared + 4 * 3 * DM)
        rows_b = place("rows_b", [10, P], at=shared + 4 * (3 * DM + P))
        masks_in = place("masks_in", [P, len(LEVELS), P], at=shared + 4 * (3 * DM + 2 * P))
        cursor[0] = shared
        hk, hb, hq = (place(n, [P, HG, T]) for n in ("hk", "hb", "hq"))
        v_tok = place("v_tok", [P, 3, 512])
        att_p, att_s = place("att_p", [P, 2, HG, P]), place("att_s", [TS, HG, TS])
        work_at = cursor[0]
        decay = [place(f"decay{i}", [P, HG, T]) for i in range(2)]
        scaled = [place(f"scaled{i}", [P, HG, T]) for i in range(2)]
        iq_at = cursor[0]
        iq, iq_s = place("iq", [P, 4, TP]), place("iq_s", [P, SEQS, 4, STEP])
        q, q_s = place("q", [P, 4, TP]), place("q_s", [P, SEQS, 4, STEP])
        cache_at = cursor[0]
        k_pages, i_pages = place("k_pages", [P, 16, P]), place("i_pages", [P, 16, 2, HD])
        v_pages = place("v_pages", [P, 16, P])
        kT_past, ikT_past = place("kT_past", [P, 16, P]), place("ikT_past", [P, 16, P])
        state = place("state", [P, SEQS, HG, P])
        s_end = place("s_end", [P, HG, P])
        assert max(cursor[0], ffn_end) <= nc.sbuf_usable_end, (cursor[0], ffn_end)
        p_tok = place("p_tok", [P, 3, PD], at=work_at)
        relu_p = place("relu_p", [P, NH, 256], at=work_at)
        relu_s = place("relu_s", [P, 4, KEYS_S], at=work_at + 4 * 2 * HG * T)
        probs = place("probs", [P, NH, 256], at=work_at)
        probsT = place("probsT", [P, 2, NH, P], at=work_at + 4 * 2 * HG * T)
        hgate = place("hgate", [P, HG, T], at=iq_at)
        raw_iq = place("raw_iq", [P, 4, T], at=work_at + 4 * 2 * HG * T)
        raw_q = place("raw_q", [P, 4, T], at=work_at + 4 * 3 * HG * T)
        rope_tok = place("rope_tok", [P, 4, 3 * 2 * 32], at=work_at + 4 * 3 * HG * T)
        s_mid = place("s_mid", [P, HG, P], at=cache_at + 4 * 7 * HG * P)
        key_tok = place("key_tok", [P, 3, HG, P], at=cache_at)
        v_own = place("v_own", [TS, 2, SEQS, P], at=cache_at + 4 * 3 * HG * P)
        probs_s = place("probs_s", [P, 4, KEYS_S], at=shared + 4 * HG * T)
        probsT_s = place("probsT_s", [P, 3, 4, P], at=cache_at)
        o_hg = place("o_hg", [P, HG, T], at=shared)

        ps = ctx.enter_context(nc.psum_tensor("ps", [P, 8, 512], F32))

        constants_in = sig("constants_in")
        tokens_in = sig("tokens_in")
        slot_in = [sig("slot0_in"), sig("slot1_in")]
        caches_in, states_in, embeddings_in = sig("caches_in"), sig("states_in"), sig("embeddings_in")
        slot_hi_ready, slot_lo_ready = sig("slot_hi_ready"), sig("slot_lo_ready")
        u_lo_ready = sig("u_lo_ready")
        squarex_ready, squarex_added = sig("squarex_ready"), sig("squarex_added")
        hidden_hi_ready = sig("hidden_hi_ready")
        tile_done = sig("tile_done")
        pair_read = sig("pair_read")
        mix_read = sig("mix_read")
        turned = sig("turned")
        turned_read = sig("turned_read")
        setup_done = sig("setup_done")
        bounds_exp = sig("bounds_exp")
        x_ready = sig("x_ready")
        u_ready = sig("u_ready")
        gain_ready = sig("gain_ready")
        msx_ready = sig("msx_ready")
        invx_ready, r_pre_ready = sig("invx_ready"), sig("r_pre_ready")
        square_ready, square_added, ms_ready = sig("square_ready"), sig("square_added"), sig("ms_ready")
        inv_ready, r_post_ready = sig("inv_ready"), sig("r_post_ready")
        gate_scaled, gate_acted, hidden_ready = sig("gate_scaled"), sig("gate_acted"), sig("hidden_ready")
        ple_y_ready = sig("ple_y_ready")
        auxd_done, auxd_read = sig("auxd_done"), sig("auxd_read")
        auxa_done, auxa_read = sig("auxa_done"), sig("auxa_read")
        big_done = sig("big_done")
        big_read_act, big_read_dve = sig("big_read_act"), sig("big_read_dve")
        scored = sig("scored")
        roped = sig("roped")
        relu_ready = sig("relu_ready")
        iw_ready = sig("iw_ready")
        hg_exp, hg_dve = sig("hg_exp"), sig("hg_dve")
        diff_ready, decay_ready, scaled_ready = sig("diff_ready"), sig("decay_ready"), sig("scaled_ready")
        att_ready = sig("att_ready")
        v_own_ready = sig("v_own_ready")
        o_ready, inv_o_ready, r_o_ready = sig("o_ready"), sig("inv_o_ready"), sig("r_o_ready")
        state_decayed, states_done = sig("state_decayed"), sig("states_done")
        masked, exped, normed = sig("masked"), sig("exped"), sig("normed")
        attended = sig("attended")
        stored = sig("stored")
        y_stored = sig("y_stored")
        final_turned, final_copied = sig("final_turned"), sig("final_copied")
        passed = sig("passed")
        dve_steps, act_steps, pool_steps = sig("dve_steps"), sig("act_steps"), sig("pool_steps")

        block = ctx.enter_context(nc.Block())
        N_CONST = len(CONST_NAMES) + 10
        NAMES_A = ["n_f1_pre", "n_f1_post", "n_mix_pre", "n_mix_post", "n_f2_pre", "n_f2_post",
                   "n_ple_pre", "n_ple_post"]

        def apart(eng):
            eng.sem_inc(passed.sem, 1)

        class Chain:

            def __init__(self, eng, s):
                self.eng, self.sig, self.layer, self.n = eng, s, None, 0

            def enter(self, layer):
                self.layer, self.n = layer, 0

            def add(self, ins):
                ins.then_inc(*once(self.sig))
                self.n += 1

            def settle(self, but=0):
                if self.layer is None:
                    self.eng.wait_ge(self.sig.sem, self.n)
                else:
                    self.eng.wait_ge(self.sig.sem, self.sig.at(self.layer, self.n - but))
                    apart(self.eng)

            def __call__(self, ins):
                self.add(ins)
                self.settle()

        @block.sync
        def _(sp):
            counts.in_layer = 0
            def load(L, n, parts, i=None):
                before = n - 2 if i is None else n
                if before >= 0 and LOADS[before][0] in SPLIT_KINDS:
                    v = slot_lo_ready.at(L, splits_before(before) + 1)
                    sp.wait_ge(slot_lo_ready.sem, v if i is None else v + (i * 2 - 2))
                else:
                    sp.wait_ge(tile_done.sem, tile_done.at(L, TILES_BEFORE[n - 1] if n else -1))
                apart(sp)
                for dst, src in parts:
                    sp.dma_start(dst, src).then_inc(*dma(slot_in[n % 2]))

            def w(name, L):
                return A[name][bass.ds(L, 1)]

            def cols(name, L, at, n, kt=KT):
                return w(name, L)[:, :, at:at + n].rearrange("a (k p) n -> p (a k) n", p=P)

            def ffn(L, which):
                g, up, down = f"w_f{which}_gate", f"w_f{which}_up", f"w_f{which}_down"
                n0 = LOAD_AT[f"gateup{which}", 0]

                def gateup(half, at, i=None):
                    n = n0 + half
                    s = slots[n % 2][:, 0:2 * KT * P].rearrange("p (a k n) -> p a k n", a=2, k=KT)
                    load(L, n, [
                        (s[:, a], w(name, L)[:, :, at].rearrange("a (k p) n -> p (a k) n", p=P))
                        for a, name in enumerate((g, up))], i)

                for half in range(2):
                    gateup(half, slice(half * P, half * P + P))
                counts.times = FT // 2 - 1
                with sp.Fori(1, FT // 2) as i:
                    for half in range(2):
                        gateup(half, bass.ds(i * (2 * P) + half * P, P), i)
                n0 = LOAD_AT[f"down{which}", 0]
                counts.times = KT // 2
                with sp.Fori(0, KT // 2) as i:
                    for half in range(2):
                        n = n0 + half
                        s = slots[n % 2][:, :].rearrange("p (f n) -> p f n", f=FT)
                        at = bass.ds(i * (2 * P) + half * P, P)
                        load(L, n, [(s, w(down, L)[:, :, at].rearrange("a (f p) n -> p (a f) n", p=P))],
                             i)
                counts.times = 1

            for n, name in enumerate(NAMES_A):
                sp.dma_start(rows_a[16 * n:16 * n + 16, :],
                             A[name].rearrange("l (k p) -> (l k) p", p=P)).then_inc(*dma(constants_in))
            sp.dma_start(rows_b[0:8, :], A["hg_lb_logits"].rearrange("l (h p) -> (l h) p", p=P)
                         ).then_inc(*dma(constants_in))
            sp.dma_start(rows_b[8:10, :], A["hg_norm"]).then_inc(*dma(constants_in))
            for name, t in (("identity", identity), ("mean_model", mean_model)):
                sp.dma_start(t[:, :], A[name]).then_inc(*dma(constants_in))
            sp.dma_start(tokens[:, 0:2, :], A["x_prompt"].rearrange("a (t p) d -> p (a t) d", p=P)
                         ).then_inc(*dma(tokens_in))
            sp.dma_start(tokens[0:TS, 2, :], A["x_sample"].rearrange("b t d -> (b t) d")
                         ).then_inc(*dma(tokens_in))
            for name, t in (("cos_f", cos_f), ("sin_f", sin_f), ("rotate", rotate),
                            ("mean_head", mean_head), ("causal", causal), ("causal_s", causal_s),
                            ("head_row", head_row), ("carry", carry), ("own_seq", own_seq)):
                sp.dma_start(t[:, :], A[name]).then_inc(*dma(constants_in))
            for name, t in (("cos_t", cos_t), ("sin_t", sin_t), ("level_masks", masks_in),
                            ("spread", spread), ("own_token", own_token)):
                sp.dma_start(t[:, :, :], A[name].rearrange("p (a b) -> p a b", a=t.shape[1])
                             ).then_inc(*dma(constants_in))
            pages = [sp.value_load(A["page_table"][b:b + 1, n:n + 1], min_val=0, max_val=pool_pages - 1)
                     for b in range(SEQS) for n in range(NPAGES)]
            sp.wait_ge(turned_read.sem, KT + 2)
            counts.in_layer = 1
            with sp.Fori(0, LAYERS) as L:
                ffn(L, 1)
                def mix_load(kind, i, parts):
                    load(L, LOAD_AT[kind, i], parts)

                def slot_of(kind, i, width):
                    return slots[LOAD_AT[kind, i] % 2][:, 0:KT * width].rearrange("p (k n) -> p k n", k=KT)

                def head_pairs(kind, at):
                    for i in range(2):
                        dst = slot_of(kind, i, 256).rearrange("p k (j g n) -> p j g k n", j=2, g=2)
                        mix_load(kind, i, [
                            (dst[:, j, g], cols("w_in", L, at + g * 256 + (2 * i + j) * HD, HD))
                            for j in range(2) for g in range(2)])

                head_pairs("iq", C_IQ)
                sp.wait_ge(x_ready.sem, x_ready.at(L, KT))
                apart(sp)
                pool_k = w("cache_k", L).rearrange("a n t h d -> (a n) t (h d)")
                pool_v = w("cache_v", L).rearrange("a n t h d -> (a n) t (h d)")
                pool_i = w("cache_idx_k", L).rearrange("a n t d -> (a n) t d")
                sp.dma_start(p_tok[:, 0:2, :], w("p_prompt", L).rearrange("l a (t p) d -> p (l a t) d", p=P)
                             ).then_inc(*dma(embeddings_in))
                sp.dma_start(p_tok[0:TS, 2, :], w("p_sample", L).rearrange("l b t d -> (l b t) d")
                             ).then_inc(*dma(embeddings_in))

                for n in range(16):
                    sp.dma_start(k_pages[:, n, :], pool_k[bass.ds(pages[n], 1)].rearrange("a t d -> t (a d)")
                                 ).then_inc(*dma(caches_in))
                mix_load("kv", 0, [(slot_of("kv", 0, 256), cols("w_in", L, C_K, 256))])
                for n in range(16):
                    for twice in range(2):
                        sp.dma_start(i_pages[:, n, twice, :],
                                     pool_i[bass.ds(pages[n], 1)].rearrange("a t d -> t (a d)")
                                     ).then_inc(*dma(caches_in))
                mix_load("ikiw", 0, [(slot_of("ikiw", 0, 72), cols("w_in", L, C_IK, 72))])
                for kind, at in (("hf", C_HF), ("hq", C_HQ)):
                    for i in range(2):
                        mix_load(kind, i, [(slot_of(kind, i, 256), cols("w_in", L, at + 256 * i, 256))])
                head_pairs("q", C_Q)
                for n in range(16):
                    sp.dma_start(v_pages[:, n, :], pool_v[bass.ds(pages[n], 1)].rearrange("a t d -> t (a d)")
                                 ).then_inc(*dma(states_in))
                st = w("state_hgrn", L).rearrange("l b h d e -> d (l b) h e")
                for b in range(0, SEQS, 2):
                    sp.dma_start(state[:, b:b + 2], st[:, b:b + 2]).then_inc(*dma(states_in))
                for kind, at in (("hi", C_HI), ("hgate", C_HG)):
                    for i in range(2):
                        mix_load(kind, i, [(slot_of(kind, i, 256), cols("w_in", L, at + 256 * i, 256))])
                wo = w("w_out", L)
                for i in range(4):
                    dst = slot_of("out", i, 256)
                    c = slice(256 * i, 256 * i + 256)
                    mix_load("out", i, [
                        (dst[0:64, 0:4], wo[:, 0:256, c].rearrange("a (j d) n -> d (a j) n", d=HD)),
                        (dst[64:128, 0:4], wo[:, 256:512, c].rearrange("a (j d) n -> d (a j) n", d=HD)),
                        (dst[:, 4:8], wo[:, 512:1024, c].rearrange("a (h e) n -> e (a h) n", e=P))])
                ffn(L, 2)
                for i in range(4):
                    s = slots[LOAD_AT["ple", i] % 2][:, 0:(KT + 2) * 256].rearrange("p (k n) -> p k n", k=KT + 2)
                    mix_load("ple", i, [(s[:, 0:KT], cols("w_ple_gate", L, 256 * i, 256)),
                                        (s[:, KT:], cols("w_ple_proj", L, 256 * i, 256))])
            counts.in_layer = 2
            sp.wait_ge(final_copied.sem, 6)
            yt = tokens
            sp.dma_start(O["y_prompt"].rearrange("a (t p) d -> p (a t) d", p=P), yt[:, 0:2, :]
                         ).then_inc(*dma(y_stored))
            sp.dma_start(O["y_sample"].rearrange("b t d -> (b t) d"), yt[0:TS, 2, :]
                         ).then_inc(*dma(y_stored))
            sp.wait_ge(y_stored.sem, 32)
            sp.wait_ge(stored.sem, stored.at(LAYERS - 1, 16 * 8))

        @block.gpsimd
        def _(pool):
            counts.in_layer = 0
            ch = Chain(pool, pool_steps)
            ch(pool.memset(kv_tok[:, :, :], 0.0))
            ch(pool.memset(ik_tok[:, :, :], 0.0))
            pool.wait_ge(constants_in.sem, 16 * N_CONST)

            def squares_of_x(L, stage):
                pool.wait_ge(msx_ready.sem, msx_ready.at(L, stage))
                apart(pool)
                for j in range(KT):
                    pool.wait_ge(squarex_ready.sem, squarex_ready.at(L, stage * KT + j + 1))
                    apart(pool)
                    if j == 0:
                        ins = pool.tensor_copy(sumsqx[:, :], sqx[:, 0, :])
                    else:
                        ins = pool.tensor_tensor(sumsqx[:, :], sumsqx[:, :], sqx[:, j % 2, :], ALU.add)
                    ins.then_inc(*once(squarex_added))
                    pool.wait_ge(squarex_added.sem, squarex_added.at(L, stage * KT + j + 1))
                    apart(pool)

            def hidden_rest(L, which):
                m = FT * (which - 1)
                counts.times = FT // 2
                with pool.Fori(0, FT // 2) as i:
                    for half in range(2):
                        pool.wait_ge(gate_acted.sem, gate_acted.at(L, m + half + 1) + i * 2)
                        apart(pool)
                        pool.wait_ge(pair_read.sem, pair_read.at(L, m + half + 1) + i * 2)
                        apart(pool)
                        ch.add(pool.tensor_tensor(hidden_tmp[:, half, :], gate_out[:, half, :],
                                                  up_out[:, half, :], ALU.mult))
                        pool.wait_ge(hidden_hi_ready.sem, hidden_hi_ready.at(L, m + half + 1) + i * 2)
                        apart(pool)
                        pool.wait_ge(pool_steps.sem, pool_steps.at(L, ch.n) + i * 2)
                        apart(pool)
                        at = bass.ds(i * 2 + half, 1)
                        pool.tensor_tensor(hidden_lo[:, at, :].rearrange("p a t -> p (a t)"),
                                           hidden_tmp[:, half, :],
                                           hidden_hi[:, at, :].bitcast(F32).rearrange("p a t -> p (a t)"),
                                           ALU.subtract).then_inc(*once(hidden_ready))
                counts.times = 1
                ch.n += 2 * (FT // 2 - 1)

            def squares_of_y(L, stage):
                pool.wait_ge(ms_ready.sem, ms_ready.at(L, stage))
                apart(pool)
                for j in range(KT):
                    pool.wait_ge(square_ready.sem, square_ready.at(L, stage * KT + j + 1))
                    apart(pool)
                    if j == 0:
                        ins = pool.tensor_copy(sumsq[:, :], sq[:, 0, :])
                    else:
                        ins = pool.tensor_tensor(sumsq[:, :], sumsq[:, :], sq[:, j % 2, :], ALU.add)
                    ins.then_inc(*once(square_added))
                    pool.wait_ge(square_added.sem, square_added.at(L, stage * KT + j + 1))
                    apart(pool)

            def rope_tokens(tile, dst_heads, heads):
                v = tile.rearrange("p t (h two c) -> p t h two c", h=heads, two=2)
                a, b = v[:, :, :, 0, :], v[:, :, :, 1, :]
                n = 3 * heads * 32
                tmp = [rope_tok[:, i, 0:n].rearrange("p (t h c) -> p t h c", t=3, h=heads) for i in range(4)]
                for h in range(heads):
                    pool_ops = ((0, a, cos_t), (1, b, sin_t), (2, b, cos_t), (3, a, sin_t))
                    for i, src, tab in pool_ops:
                        ch.add(pool.tensor_tensor(tmp[i][:, :, h, :], src[:, :, h, :], tab[:, :, :], ALU.mult))
                ch.settle()
                for h in range(heads):
                    ch.add(pool.tensor_tensor(a[:, :, h, :], tmp[0][:, :, h, :], tmp[1][:, :, h, :], ALU.subtract))
                    ch.add(pool.tensor_tensor(b[:, :, h, :], tmp[2][:, :, h, :], tmp[3][:, :, h, :], ALU.add))
                ch.settle()

            def store(L, dst, src, rearrange):
                pool.dma_start(dst, src).then_inc(*dma(stored))

            counts.in_layer = 1
            with pool.Fori(0, LAYERS) as L:
                ch.enter(L)
                squares_of_x(L, 0)
                hidden_rest(L, 1)
                squares_of_y(L, 0)
                squares_of_x(L, 1)
                pool.wait_ge(mix_read.sem, mix_read.at(L, MIX_LAST["kv"]))
                apart(pool)
                rope_tokens(kv_tok[:, :, 0:128], None, 2)
                pool.wait_ge(mix_read.sem, mix_read.at(L, MIX_LAST["ikiw"]))
                apart(pool)
                rope_tokens(ik_tok[:, :, 0:64], None, 1)
                pool.tensor_copy(ik_tok[:, :, 64:128], ik_tok[:, :, 0:64]).then_inc(*once(roped))
                pool.wait_ge(roped.sem, roped.at(L, 1))
                apart(pool)
                for name, src in (("k", kv_tok[:, :, 0:128]), ("v", kv_tok[:, :, 128:256]),
                                  ("idx_k", ik_tok[:, :, 0:64])):
                    d = O[f"{name}_prompt"][bass.ds(L, 1)]
                    e = O[f"{name}_sample"][bass.ds(L, 1)]
                    if name == "idx_k":
                        d = d.rearrange("l a (t p) d -> p (l a t) d", p=P)
                        e = e.rearrange("l b t d -> (l b t) d")
                    else:
                        d = d.rearrange("l a (t p) h d -> p (l a t) (h d)", p=P)
                        e = e.rearrange("l b t h d -> (l b t) (h d)")
                    pool.dma_start(d, src[:, 0:2]).then_inc(*dma(stored))
                    pool.dma_start(e, src[0:TS, 2]).then_inc(*dma(stored))
                pool.wait_ge(hg_dve.sem, hg_dve.at(L, HGD["scan"]))
                apart(pool)
                for n, h in enumerate(LEVELS):
                    if n >= 2:
                        pool.wait_ge(scaled_ready.sem, scaled_ready.at(L, n - 1))
                        apart(pool)
                    src, dst = level_view(hb, h), level_view(decay[n % 2], h)
                    ref = src[0][:, :, h - 1:h] if 2 * h <= STEP else src[0][:, :, :, h - 1:h]
                    ref = ref.to_broadcast(list(src[1].shape))
                    pool.tensor_tensor(dst[1], src[1], ref, ALU.subtract)
                    pool.tensor_tensor(dst[0], ref, src[0], ALU.subtract).then_inc(*once(diff_ready))
                n = len(LEVELS)
                pool.wait_ge(scaled_ready.sem, scaled_ready.at(L, n))
                apart(pool)
                for a, b in (((0, TP), CHUNK), ((TP, T), STEP)):
                    for hh in range(HG):
                        v = hb[:, hh, a[0]:a[1]].rearrange("p (c s) -> p c s", s=b)
                        d = decay[1][:, hh, a[0]:a[1]].rearrange("p (c s) -> p c s", s=b)
                        ins = pool.tensor_tensor(d, v[:, :, b - 1:b].to_broadcast(list(v.shape)), v, ALU.subtract)
                ins.then_inc(*once(diff_ready))
                pool.wait_ge(mix_read.sem, mix_read.at(L, MIX_LAST["hi"]))
                apart(pool)
                def own_values(h):
                    vv = v_tok[0:TS, 2, h * P:(h + 1) * P].rearrange("p (a e) -> p a e", a=1)
                    oo = own_seq[:, :].rearrange("p (b a) -> p b a", a=1)
                    pool.tensor_tensor(v_own[:, h % 2], vv.to_broadcast([TS, SEQS, P]),
                                       oo.to_broadcast([TS, SEQS, P]), ALU.mult).then_inc(*once(v_own_ready))

                pool.wait_ge(auxa_done.sem, auxa_done.at(L, AUXA["ipages3"] + 1))
                apart(pool)
                own_values(0)
                own_values(1)
                for h in range(HG):
                    pool.wait_ge(auxa_done.sem, auxa_done.at(L, AUXA[f"o{h}"] + 1))
                    apart(pool)
                    last = decay[0][:, h, TP + STEP - 1::STEP].rearrange("p (b a) -> p b a", a=1)
                    pool.tensor_tensor(state[:, :, h, :], state[:, :, h, :], last.to_broadcast([P, SEQS, P]),
                                       ALU.mult).then_inc(*once(state_decayed))
                for h in (2, 3):
                    pool.wait_ge(auxd_done.sem, auxd_done.at(L, AUXD[f"state_s{h - 2}b"] + 1))
                    apart(pool)
                    own_values(h)
                pool.wait_ge(states_done.sem, states_done.at(L, 1))
                apart(pool)
                pool.dma_start(O["hgrn_prompt"][bass.ds(L, 1)].rearrange("l a h d e -> d (l a h) e"),
                               s_end[:, :, :]).then_inc(*dma(stored))
                pool.wait_ge(states_done.sem, states_done.at(L, 2))
                apart(pool)
                pool.dma_start(O["hgrn_sample"][bass.ds(L, 1)].rearrange("l b h d e -> d (l b h) e"),
                               state[:, :, :, :].rearrange("p b h e -> p (b h) e")).then_inc(*dma(stored))
                squares_of_y(L, 1)
                squares_of_x(L, 2)
                hidden_rest(L, 2)
                squares_of_y(L, 2)
                squares_of_x(L, 3)
                squares_of_y(L, 3)
            counts.in_layer = 2

        @block.scalar
        def _(act):
            counts.in_layer = 0
            ch = Chain(act, act_steps)
            act.wait_ge(bounds_exp.sem, 1)
            act.activation(bounds_tmp[:, 1, :], bounds_tmp[:, 1, :], ACT.Exp)
            act.activation(bounds_tmp[:, 2, :], bounds_tmp[:, 2, :], ACT.Exp).then_inc(*once(bounds_exp))
            act.wait_ge(constants_in.sem, 16 * N_CONST)

            def make_u(L, stage, norm):
                dst = u_hi if stage in (0, 2) else u
                for j in range(KT):
                    act.wait_ge(x_ready.sem, x_ready.at(L, stage * KT + j + 1 - KT))
                    apart(act)
                    if j == 0:
                        act.wait_ge(gain_ready.sem, gain_ready.at(L, 1))
                        apart(act)
                    act.activation(dst[:, j, :], x[:, j, :], ACT.Copy, scale=gain[:, norm, j:j + 1]
                                   ).then_inc(*once(u_ready))
                    act.wait_ge(squarex_added.sem, squarex_added.at(L, stage * KT + j - 1))
                    apart(act)
                    act.activation(sqx[:, j % 2, :], x[:, j, :], ACT.Square).then_inc(*once(squarex_ready))

            def split_hi(L, n, i=None):
                size = 2 * KT * P if LOADS[n][0].startswith("gateup") else SLOT
                full = slot_in[n % 2]
                value = full.at(L, dma_count_before(n) + 16 * DMAS(n))
                act.wait_ge(full.sem, value if i is None else value + i * (16 * DMAS(n)))
                apart(act)
                act.activation(slot_hi[n % 2][:, 0:size], slots[n % 2][:, 0:size], ACT.Copy
                               ).then_inc(*once(slot_hi_ready))

            def root(L, n, ready, inv, dst, out):
                act.wait_ge(ready.sem, ready.at(L, n))
                act.activation(dst, inv, ACT.Sqrt).then_inc(*once(out))

            def tiles_out(L, kind, stage):
                per = dict(down1=1, out=2, down2=1)[kind]
                for j in range(KT):
                    act.wait_ge(tile_done.sem, tile_done.at(L, tile_at(kind, j // per, j % per) + 1))
                    apart(act)
                    if kind != "out" and j + 2 < KT:
                        split_hi(L, LOAD_AT[kind, j + 2])
                    if j >= 2:
                        act.wait_ge(square_added.sem, square_added.at(L, stage * KT + j - 1))
                        apart(act)
                    act.activation(y[:, j, :], ps[:, 4 + j % 2, 0:T], ACT.Copy)
                    act.activation(sq[:, j % 2, :], ps[:, 4 + j % 2, 0:T], ACT.Square
                                   ).then_inc(*once(square_ready))

            def ple_square(L, j):
                act.wait_ge(pair_read.sem, pair_read.at(L, 2 * FT + j + 1))
                apart(act)
                if j >= 2:
                    act.wait_ge(square_added.sem, square_added.at(L, 3 * KT + j - 1))
                act.activation(sq[:, j % 2, :], y[:, j, :], ACT.Square).then_inc(*once(square_ready))

            def soft(L, t):
                keys = 256 if t else 128
                act.wait_ge(masked.sem, masked.at(L, 2 - t))
                apart(act)
                for h in range(NH):
                    ins = act.activation(probs[:, h, 0:keys], probs[:, h, 0:keys], ACT.Exp,
                                         bias=peak[:, t, h:h + 1], scale=HD ** -0.5,
                                         accum_out=total[:, t, h:h + 1])
                ins.then_inc(*once(exped))

            def ffn(L, which):
                m = FT * (which - 1)
                n0 = LOAD_AT[f"gateup{which}", 0]
                t0 = tile_at(f"gateup{which}", 0)

                def step(n, i=None):
                    v = tile_done.at(L, t0 + n + 1)
                    act.wait_ge(tile_done.sem, v if i is None else v + i * 2)
                    apart(act)
                    split_hi(L, n0 + n + 2, i)
                    v = gate_scaled.at(L, m + n + 1)
                    act.wait_ge(gate_scaled.sem, v if i is None else v + i * 2)
                    act.activation(gate_out[:, n % 2, :], gate_in[:, n % 2, :], ACT.Silu
                                   ).then_inc(*once(gate_acted))

                counts.times = FT // 2 - 1
                with act.Fori(0, FT // 2 - 1) as i:
                    step(0, i)
                    step(1, i)
                counts.times = 1
                step(FT - 2)
                step(FT - 1)

            def auxa(L, name, dst, src, func=ACT.Copy, done=None):
                k = AUXA[name]
                act.wait_ge(auxa_done.sem, auxa_done.at(L, k + 1))
                apart(act)
                act.activation(dst, src(ps[:, (3, 6)[k % 2], :]), func).then_inc(*once(auxa_read))

            counts.in_layer = 1
            with act.Fori(0, LAYERS) as L:
                ch.enter(L)
                split_hi(L, 0)
                make_u(L, 0, 0)
                split_hi(L, 1)
                root(L, 1, invx_ready, inv_pre[:, :], r_pre[:, :], r_pre_ready)
                ffn(L, 1)
                tiles_out(L, "down1", 0)
                root(L, 1, inv_ready, inv_post[:, :], r_post[:, :], r_post_ready)
                make_u(L, 1, 2)
                root(L, 2, invx_ready, inv_pre[:, :], r_pre[:, :], r_pre_ready)
                for k in range(2):
                    auxa(L, f"p{k}", pT[:, k, :], lambda b: b[:, 0:T])
                for k in range(4):
                    auxa(L, f"kpages{k}", kT_past[:, 4 * k:4 * k + 4, :],
                         lambda b: b.rearrange("p (n t) -> p n t", n=4))
                for k in range(4):
                    auxa(L, f"ipages{k}", ikT_past[:, 4 * k:4 * k + 4, :],
                         lambda b: b.rearrange("p (n t) -> p n t", n=4))
                act.wait_ge(mix_read.sem, mix_read.at(L, MIX_LAST["hf"]))
                act.activation(hb[:, :, :], hk[:, :, :], ACT.Sigmoid).then_inc(*once(hg_exp))
                auxa(L, "kT", kT[:, :], lambda b: b[:, 0:T])
                auxa(L, "ikT", ikT[:, :], lambda b: b[:, 0:T])
                act.wait_ge(mix_read.sem, mix_read.at(L, MIX_LAST["hq"]))
                act.activation(scaled[1][:, :, :], hq[:, :, :], ACT.Silu).then_inc(*once(hg_exp))
                for n in range(4):
                    g, j = n % 2, n // 2 * 2
                    act.wait_ge(big_done.sem, big_done.at(L, BIG["idx"] + n + 1))
                    apart(act)
                    act.activation(relu_p[:, 4 * g + j:4 * g + j + 2, :],
                                   ps[:, 4 + n % 2, :].rearrange("p (h k) -> p h k", h=2),
                                   ACT.Relu, scale=HD ** -0.5).then_inc(*once(big_read_act))
                act.wait_ge(scored.sem, scored.at(L, EV["score1"]))
                for n in range(2):
                    act.wait_ge(big_done.sem, big_done.at(L, BIG["idx"] + 5 + n))
                    apart(act)
                    act.activation(relu_p[:, 4 * n:4 * n + 4, 0:128],
                                   ps[:, 4 + n % 2, :].rearrange("p (h k) -> p h k", h=4),
                                   ACT.Relu, scale=HD ** -0.5).then_inc(*once(big_read_act))
                for n in range(4):
                    act.wait_ge(big_done.sem, big_done.at(L, BIG["idx"] + 7 + n))
                    apart(act)
                    act.activation(relu_s[:, n, :], ps[:, 4 + n % 2, 0:KEYS_S],
                                   ACT.Relu, scale=HD ** -0.5).then_inc(*once(big_read_act))
                act.wait_ge(hg_dve.sem, hg_dve.at(L, HGD["f"]))
                apart(act)
                act.wait_ge(scored.sem, scored.at(L, EV["score0"]))
                act.activation(decay[0][:, :, :], hb[:, :, :], ACT.Ln).then_inc(*once(hg_exp))
                act.wait_ge(mix_read.sem, mix_read.at(L, MIX_LAST["hgate"]))
                apart(act)
                act.wait_ge(auxd_done.sem, auxd_done.at(L, AUXD["score_s"] + 1))
                act.activation(scaled[0][:, :, :], hgate[:, :, :], ACT.Silu).then_inc(*once(hg_exp))
                for n, h in enumerate(LEVELS):
                    act.wait_ge(diff_ready.sem, diff_ready.at(L, n + 1))
                    c = T if 2 * h <= STEP else TP
                    act.activation(decay[n % 2][:, :, 0:c], decay[n % 2][:, :, 0:c], ACT.Exp
                                   ).then_inc(*once(decay_ready))
                n = len(LEVELS)
                act.wait_ge(scaled_ready.sem, scaled_ready.at(L, n))
                act.activation(decay[0][:, :, :], hb[:, :, :], ACT.Exp).then_inc(*once(decay_ready))
                act.wait_ge(diff_ready.sem, diff_ready.at(L, n + 1))
                act.activation(decay[1][:, :, :], decay[1][:, :, :], ACT.Exp).then_inc(*once(decay_ready))
                for n in range(3):
                    m = TOK_TILES[n][1]
                    auxa(L, f"key{n}", key_tok[0:m, n, :, :],
                         lambda b, m=m: b[0:m, :].rearrange("p (h d) -> p h d", h=HG))
                for h in range(HG):
                    k = AUXA[f"o{h}"]
                    act.wait_ge(auxa_done.sem, auxa_done.at(L, k + 1))
                    apart(act)
                    bank = ps[:, (3, 6)[k % 2], 0:T]
                    ch.add(act.activation(o_hg[:, h, :], bank, ACT.Copy))
                    act.activation(scaled[1][:, h, :], bank, ACT.Square).then_inc(*once(auxa_read))
                act.wait_ge(inv_o_ready.sem, inv_o_ready.at(L, 1))
                act.activation(decay[1][:, :, :], decay[1][:, :, :], ACT.Sqrt).then_inc(*once(r_o_ready))
                soft(L, 1)
                for k in range(2):
                    for g in range(2):
                        auxa(L, f"pT1_{k}{g}", probsT[:, k, 4 * g:4 * g + 4, :],
                             lambda b: b.rearrange("p (h t) -> p h t", h=4))
                soft(L, 0)
                for g in range(2):
                    auxa(L, f"pT0_0{g}", probsT[:, 0, 4 * g:4 * g + 4, :],
                         lambda b: b.rearrange("p (h t) -> p h t", h=4))
                act.wait_ge(masked.sem, masked.at(L, 3))
                apart(act)
                for pair in range(4):
                    ins = act.activation(probs_s[:, pair, :], probs_s[:, pair, :], ACT.Exp,
                                         bias=peak[:, 2, pair:pair + 1], scale=HD ** -0.5,
                                         accum_out=total[:, 2, pair:pair + 1])
                ins.then_inc(*once(exped))
                for k in range(3):
                    m = TOK_TILES[k][1]
                    auxa(L, f"pTs{k}", probsT_s[0:m, k, :, :],
                         lambda b, m=m: b[0:m, :].rearrange("p (n t) -> p n t", n=4))
                tiles_out(L, "out", 1)
                act.wait_ge(stored.sem, stored.at(L, 16 * 8))
                apart(act)
                split_hi(L, LOAD_AT["gateup2", 0])
                root(L, 2, inv_ready, inv_post[:, :], r_post[:, :], r_post_ready)
                make_u(L, 2, 4)
                split_hi(L, LOAD_AT["gateup2", 1])
                root(L, 3, invx_ready, inv_pre[:, :], r_pre[:, :], r_pre_ready)
                ffn(L, 2)
                tiles_out(L, "down2", 2)
                root(L, 3, inv_ready, inv_post[:, :], r_post[:, :], r_post_ready)
                make_u(L, 3, 6)
                root(L, 4, invx_ready, inv_pre[:, :], r_pre[:, :], r_pre_ready)
                for j in range(KT):
                    act.wait_ge(gate_scaled.sem, gate_scaled.at(L, 2 * FT + j + 1))
                    act.activation(gate_out[:, j % 2, :], gate_in[:, j % 2, :], ACT.Sigmoid
                                   ).then_inc(*once(gate_acted))
                    if j:
                        ple_square(L, j - 1)
                ple_square(L, KT - 1)
                root(L, 4, inv_ready, inv_post[:, :], r_post[:, :], r_post_ready)
            counts.in_layer = 2

        @block.vector
        def _(dve):
            counts.in_layer = 0
            ch = Chain(dve, dve_steps)
            for k in range(KT):
                dve.wait_ge(turned.sem, k + 1)
                dve.tensor_copy(x[:, k, :], ps[:, k, 0:T]).then_inc(*once(turned_read))
            dve.wait_ge(turned.sem, KT + 1)
            dve.tensor_copy(gains[:, :, :, :].rearrange("p a l k -> p (a l k)"), ps[:, 0, 320:448]
                            ).then_inc(*once(turned_read))
            dve.wait_ge(turned.sem, KT + 2)
            dve.tensor_copy(small[:, :], ps[:, 1, 320:330]).then_inc(*once(turned_read))
            dve.wait_ge(turned_read.sem, KT + 2)
            for a in (1, 5):
                ch(dve.tensor_scalar(gains[:, a], gains[:, a], 0.5, None, ALU.mult))
            lg = small[:, 0:8].rearrange("p (l h) -> p l h", l=LAYERS)
            ch(dve.tensor_tensor(bounds_tmp[:, 0, :], lg[:, 0], lg[:, 1], ALU.max))
            ch(dve.tensor_tensor(bounds_tmp[:, 1, :], lg[:, 0], bounds_tmp[:, 0, :], ALU.subtract))
            dve.tensor_tensor(bounds_tmp[:, 2, :], lg[:, 1], bounds_tmp[:, 0, :], ALU.subtract
                              ).then_inc(*once(bounds_exp))
            dve.wait_ge(bounds_exp.sem, 2)
            ch(dve.tensor_tensor(bounds_tmp[:, 3, :], bounds_tmp[:, 1, :], bounds_tmp[:, 2, :], ALU.add))
            ch(dve.reciprocal(bounds_tmp[:, 4, :], bounds_tmp[:, 3, :]))
            for a in (1, 2):
                ch(dve.tensor_tensor(bounds_tmp[:, a, :], bounds_tmp[:, a, :], bounds_tmp[:, 4, :], ALU.mult))
            ch(dve.tensor_tensor(bounds_tmp[:, 3, :], bounds_tmp[:, 1, :], bounds_tmp[:, 2, :], ALU.add))
            ch(dve.tensor_tensor(bounds[:, 0, :], bounds_tmp[:, 1, :], bounds_tmp[:, 1, :], ALU.subtract))
            ch(dve.tensor_tensor(bounds[:, 1, :], bounds_tmp[:, 3, :], bounds_tmp[:, 1, :], ALU.subtract))
            for s in (pair_read, mix_read, square_ready, squarex_added, hidden_ready, tile_done,
                      auxd_read, auxa_read):
                dve.sem_inc(*counts.inc(s, 2))
            for s in (msx_ready, ms_ready):
                dve.sem_inc(*once(s))
            dve.sem_inc(*counts.inc(x_ready, KT))
            dve.wait_ge(constants_in.sem, 16 * N_CONST)
            ch(dve.tensor_copy(level_masks[:, :, :], masks_in[:, :, :]))
            dve.sem_inc(*once(setup_done))

            def norm_in(L, stage):
                dve.wait_ge(msx_ready.sem, msx_ready.at(L, stage + 1))
                ch(dve.tensor_scalar(inv_pre[:, :], ps[:, 7, 0:T], EPS, None, ALU.add))
                dve.reciprocal(inv_pre[:, :], inv_pre[:, :]).then_inc(*once(invx_ready))

            def split_lo(L, n, i=None):
                size = 2 * KT * P if LOADS[n][0].startswith("gateup") else SLOT
                v = slot_hi_ready.at(L, splits_before(n) + 1)
                dve.wait_ge(slot_hi_ready.sem, v if i is None else v + i * 2)
                apart(dve)
                dve.tensor_tensor(slot_lo[n % 2][:, 0:size], slots[n % 2][:, 0:size],
                                  slot_hi[n % 2][:, 0:size].bitcast(F32), ALU.subtract
                                  ).then_inc(*once(slot_lo_ready))

            def rest_of_u(L, stage, norm, j):
                dve.wait_ge(u_ready.sem, u_ready.at(L, stage * KT + j + 1))
                apart(dve)
                dve.scalar_tensor_tensor(out=u_lo[:, j, :], in0=x[:, j, :], scalar=gain[:, norm, j:j + 1],
                                         in1=u_hi[:, j, :].bitcast(F32), op0=ALU.mult, op1=ALU.subtract
                                         ).then_inc(*once(u_lo_ready))

            def norm_out(L, stage, norm, u_norm=None):
                dve.wait_ge(ms_ready.sem, ms_ready.at(L, stage + 1))
                ch(dve.tensor_scalar(inv_post[:, :], ps[:, 6, 0:T], EPS, None, ALU.add))
                dve.reciprocal(inv_post[:, :], inv_post[:, :]).then_inc(*once(inv_ready))
                dve.wait_ge(r_post_ready.sem, r_post_ready.at(L, stage + 1))
                apart(dve)

                def add(j):
                    dve.scalar_tensor_tensor(out=x[:, j, :], in0=y[:, j, :], scalar=gain[:, norm, j:j + 1],
                                             in1=x[:, j, :], op0=ALU.mult, op1=ALU.add
                                             ).then_inc(*once(x_ready))

                ch.add(dve.tensor_tensor(y[:, 0, :], y[:, 0, :], r_post[:, :], ALU.mult))
                for j in range(KT):
                    if j + 1 < KT:
                        ch.add(dve.tensor_tensor(y[:, j + 1, :], y[:, j + 1, :], r_post[:, :], ALU.mult))
                    ch.settle(0 if j + 1 == KT else 1)
                    add(j)
                    if u_norm is not None and j:
                        rest_of_u(L, stage + 1, u_norm, j - 1)
                if u_norm is not None:
                    rest_of_u(L, stage + 1, u_norm, KT - 1)

            def ffn(L, which):
                m = FT * (which - 1)
                dve.wait_ge(r_pre_ready.sem, r_pre_ready.at(L, 1 if which == 1 else 3))
                apart(dve)
                t0 = tile_at(f"gateup{which}", 0)
                n0 = LOAD_AT[f"gateup{which}", 0]

                def at(sig, n, i):
                    v = sig.at(L, n)
                    return v if i is None else v + i * 2

                def step(n, i=None):
                    h = n % 2
                    dve.wait_ge(tile_done.sem, at(tile_done, t0 + n + 1, i))
                    apart(dve)
                    dve.wait_ge(hidden_ready.sem, at(hidden_ready, m + n - 1, i))
                    apart(dve)
                    dve.tensor_tensor(gate_in[:, h, :], ps[:, 2 * h, 0:T], r_pre[:, :], ALU.mult
                                      ).then_inc(*once(gate_scaled))
                    dve.tensor_tensor(up_out[:, h, :], ps[:, 2 * h + 1, 0:T], r_pre[:, :], ALU.mult
                                      ).then_inc(*once(pair_read))
                    split_lo(L, n0 + n + 2, i)
                    dve.wait_ge(pair_read.sem, at(pair_read, m + n + 1, i))
                    apart(dve)
                    dve.wait_ge(gate_acted.sem, at(gate_acted, m + n + 1, i))
                    apart(dve)
                    if i is None:
                        tile = hidden_hi[:, n, :]
                    else:
                        tile = hidden_hi[:, bass.ds(i * 2 + h, 1), :].rearrange("p a t -> p (a t)")
                    dve.tensor_tensor(tile, gate_out[:, h, :], up_out[:, h, :], ALU.mult
                                      ).then_inc(*once(hidden_hi_ready))

                counts.times = FT // 2 - 1
                with dve.Fori(0, FT // 2 - 1) as i:
                    step(0, i)
                    step(1, i)
                counts.times = 1
                step(FT - 2)
                step(FT - 1)
                for j in range(2, KT):
                    split_lo(L, LOAD_AT[f"down{which}", j])

            def mix_tile(L, kind, i, k):
                n = tile_at(kind, i, k)
                dve.wait_ge(tile_done.sem, tile_done.at(L, n + 1))
                apart(dve)
                return ps[:, (n - tile_at("iq", 0)) % 2, :]

            def auxd(L, name):
                k = AUXD[name]
                dve.wait_ge(auxd_done.sem, auxd_done.at(L, k + 1))
                apart(dve)
                return ps[:, (2, 7)[k % 2], :]

            def mark(name, ins):
                ins.then_inc(*once(scored))
                assert totals == {} or scored.seen[1] == EV[name], (name, scored.seen)

            def own(s, L, n):
                dve.wait_ge(s.sem, s.at(L, n))
                apart(dve)

            def rope_feature(L, raw, dst, dst_s, j, name):
                bank = auxd(L, name)
                ch.add(dve.tensor_tensor(rope_tmp[:, 0, :], bank[:, 0:T], sin_f[:, :], ALU.mult))
                ch.add(dve.tensor_tensor(rope_tmp[:, 1, :], raw[:, j, :], cos_f[:, :], ALU.mult))
                ch.settle()
                dve.tensor_tensor(dst[:, j, :], rope_tmp[:, 0, 0:TP], rope_tmp[:, 1, 0:TP], ALU.add)
                a, b = (rope_tmp[:, n, TP:T].rearrange("p (b t) -> p b t", b=SEQS) for n in range(2))
                dve.tensor_tensor(dst_s[:, :, j, :], a, b, ALU.add).then_inc(*once(auxd_read))
                own(auxd_read, L, AUXD[name] + 1)

            def top_k(score, rounds, m):
                for _ in range(rounds):
                    ch(dve.max(top8[0:m, :], score))
                    ch(dve.match_replace(score, top8[0:m, :], score, TAKEN))
                ch(dve.tensor_scalar(score, score, TAKEN / 2, NEG, ALU.is_gt, ALU.mult))

            counts.in_layer = 1
            with dve.Fori(0, LAYERS) as L:
                ch.enter(L)
                own(x_ready, L, 0)
                ch.add(dve.tensor_copy(gain[:, :, :], gains[:, :, bass.ds(L, 1), :].rearrange("p a l k -> p a (l k)")))
                ch.add(dve.tensor_copy(bound[:, 0, :], bounds[:, bass.ds(L, 1), :].rearrange("p l h -> p (l h)")))
                ch.add(dve.tensor_copy(bound[:, 2, 0:1], small[:, bass.ds(L + 8, 1)]))
                ch.settle()
                dve.tensor_scalar(bound[:, 1, :], bound[:, 0, :], -1.0, 1.0, ALU.mult, ALU.add
                                  ).then_inc(*once(gain_ready))
                split_lo(L, 0)
                for j in range(KT):
                    rest_of_u(L, 0, 0, j)
                split_lo(L, 1)
                norm_in(L, 0)
                ffn(L, 1)
                norm_out(L, 0, 1)
                norm_in(L, 1)
                dve.wait_ge(r_pre_ready.sem, r_pre_ready.at(L, 2))
                apart(dve)

                def feature_tile(kind, i, k, dst):
                    bank = mix_tile(L, kind, i, k)
                    dve.tensor_tensor(dst[:, 2 * i + k, :], bank[:, 0:T], r_pre[:, :], ALU.mult
                                      ).then_inc(*once(mix_read))

                def tile_no(kind, i, k):
                    return tile_at(kind, i, k) - tile_at("iq", 0) + 1

                feature_tile("iq", 0, 0, raw_iq)
                feature_tile("iq", 0, 1, raw_iq)
                bank = auxd(L, "r_tok")
                dve.tensor_copy(r_tok[:, 0:2], bank[:, 0:2])
                dve.tensor_copy(r_tok[0:TS, 2:3], bank[0:TS, 2:3]).then_inc(*once(auxd_read))
                own(auxd_read, L, AUXD["r_tok"] + 1)
                feature_tile("iq", 1, 0, raw_iq)
                feature_tile("iq", 1, 1, raw_iq)
                for t, (_, m) in enumerate(TOK_TILES):
                    bank = mix_tile(L, "kv", 0, t)
                    dve.tensor_scalar(kv_tok[0:m, t, :], bank[0:m, 0:256], r_tok[0:m, t:t + 1], None, ALU.mult
                                      ).then_inc(*once(mix_read))
                for j in range(4):
                    rope_feature(L, raw_iq, iq, iq_s, j, f"rot_iq{j}")
                for t, (_, m) in enumerate(TOK_TILES):
                    bank = mix_tile(L, "ikiw", 0, t)
                    ch.add(dve.tensor_scalar(iw_tok[0:m, t, :], bank[0:m, 64:72], r_tok[0:m, t:t + 1],
                                             NH ** -0.5, ALU.mult, ALU.mult))
                    dve.tensor_scalar(ik_tok[0:m, t, 0:64], bank[0:m, 0:64], r_tok[0:m, t:t + 1], None, ALU.mult
                                      ).then_inc(*once(mix_read))
                for i in range(2):
                    for k in range(2):
                        feature_tile("hf", i, k, hk)
                bank = auxd(L, "iwT")
                dve.tensor_copy(iwT[:, :], bank[0:NH, 0:TS]).then_inc(*once(auxd_read))
                bank = auxd(L, "iwrow")
                dve.tensor_tensor(iw_mask[:, :, :],
                                  bank[:, 0:TS].rearrange("p (a t) -> p a t", a=1).to_broadcast([P, 4, TS]),
                                  own_token[:, :, :], ALU.mult).then_inc(*once(auxd_read))
                dve.wait_ge(hg_exp.sem, hg_exp.at(L, 1))
                apart(dve)
                for h in range(HG):
                    ch.add(dve.tensor_scalar(hb[:, h, :], hb[:, h, :], bound[:, 1, h:h + 1], bound[:, 0, h:h + 1],
                                             ALU.mult, ALU.add))
                ch.settle()
                dve.tensor_scalar(hk[:, :, :], hb[:, :, :], -1.0, 1.0, ALU.mult, ALU.add).then_inc(*once(hg_dve))
                assert hg_dve.seen[1] == HGD["f"]
                for i in range(2):
                    for k in range(2):
                        feature_tile("hq", i, k, hq)
                fills = {1: (score1, causal[:, 128:384], 256), 0: (score0, causal[:, 0:128], 128)}
                for t in (1, 0):
                    score, fill, keys = fills[t]
                    order = [0, 1, 4, 5, 2, 3, 6, 7] if t else range(NH)
                    for m, h in enumerate(order):
                        n = BIG["idx"] + (m // 2 + 1 if t else 5 + m // 4)
                        if m % (2 if t else 4) == 0:
                            dve.wait_ge(big_read_act.sem, big_read_act.at(L, n))
                            apart(dve)
                        ins = dve.scalar_tensor_tensor(out=score[:, :], in0=relu_p[:, h, 0:keys],
                                                       scalar=iw_tok[:, t, h:h + 1],
                                                       in1=fill if m == 0 else score[:, :],
                                                       op0=ALU.mult, op1=ALU.add)
                        if m == NH - 1:
                            mark(f"score{t}", ins)
                            own(scored, L, EV[f"score{t}"])
                        else:
                            ch(ins)
                bank = auxd(L, "score_s")
                ch.add(dve.memset(score_s[:, 0:PADS], SENTINEL))
                ch.add(dve.tensor_copy(score_s[:, PADS:PADS + PAST], bank[0:TS, 0:PAST]))
                dve.tensor_tensor(score_s[:, PADS + PAST:], bank[0:TS, PAST:KEYS_S], causal_s[:, :], ALU.add
                                  ).then_inc(*once(auxd_read))
                own(auxd_read, L, AUXD["score_s"] + 1)
                dve.wait_ge(hg_exp.sem, hg_exp.at(L, 2))
                apart(dve)
                dve.tensor_scalar(hq[:, :, :], scaled[1][:, :, :], P ** -0.5, None, ALU.mult
                                  ).then_inc(*once(hg_dve))
                own(hg_dve, L, HGD["silu"])
                dve.wait_ge(hg_exp.sem, hg_exp.at(L, 3))
                apart(dve)
                for h in range(HG):
                    ins = dve.tensor_tensor_scan(hb[:, h, :], carry[:, :], decay[0][:, h, :], 0.0, ALU.mult, ALU.add)
                ins.then_inc(*once(hg_dve))
                assert hg_dve.seen[1] == HGD["scan"]
                for i in range(2):
                    for k in range(2):
                        feature_tile("q", i, k, raw_q)
                for i in range(2):
                    for t, (_, m) in enumerate(TOK_TILES):
                        bank = mix_tile(L, "hi", i, t)
                        dve.tensor_scalar(v_tok[0:m, t, 256 * i:256 * i + 256], bank[0:m, 0:256],
                                          r_tok[0:m, t:t + 1], None, ALU.mult).then_inc(*once(mix_read))
                for j in range(4):
                    rope_feature(L, raw_q, q, q_s, j, f"rot_q{j}")
                for i in range(2):
                    for k in range(2):
                        feature_tile("hgate", i, k, hgate)
                dve.wait_ge(hg_exp.sem, hg_exp.at(L, 4))
                apart(dve)
                ch(dve.tensor_copy(hgate[:, :, :], scaled[0][:, :, :]))

                def big(n):
                    dve.wait_ge(big_done.sem, big_done.at(L, n + 1))
                    apart(dve)
                    return ps[:, 4 + n % 2, :]

                n = BIG["levels"]
                for c in range(2):
                    b = big(n)
                    dve.tensor_tensor(att_p[:, c], b.rearrange("p (h t) -> p h t", h=HG),
                                      identity[:, :].rearrange("p (a t) -> p a t", a=1).to_broadcast([P, HG, P]),
                                      ALU.mult).then_inc(*once(big_read_dve))
                    n += 1
                b = big(n)
                dve.tensor_tensor(att_s[:, :, :], b[0:TS, 0:HG * TS].rearrange("p (h t) -> p h t", h=HG),
                                  identity[0:TS, 0:TS].rearrange("p (a t) -> p a t", a=1).to_broadcast([TS, HG, TS]),
                                  ALU.mult).then_inc(*once(big_read_dve))
                n += 1

                def products(lv):
                    h = LEVELS[lv]
                    dve.wait_ge(decay_ready.sem, decay_ready.at(L, lv + 1))
                    apart(dve)
                    if lv >= 2:
                        dve.wait_ge(big_done.sem, big_done.at(L, LEVEL_BIG[lv - 2][-1] + 1))
                        apart(dve)
                    e, s = level_view(decay[lv % 2], h), level_view(scaled[lv % 2], h)
                    a, b = level_view(hk, h), level_view(hq, h)
                    dve.tensor_tensor(s[0], a[0], e[0], ALU.mult)
                    dve.tensor_tensor(s[1], b[1], e[1], ALU.mult).then_inc(*once(scaled_ready))

                def keep(lv):
                    own(big_read_dve, L, BIGD_BEFORE(LEVEL_BIG[lv][0]))
                    for c, k in enumerate(LEVEL_BIG[lv]):
                        b = big(k)
                        if c < 2:
                            m = level_masks[:, lv, :].rearrange("p (a t) -> p a t", a=1).to_broadcast([P, HG, P])
                            dve.copy_predicated(att_p[:, c], m, b.rearrange("p (h t) -> p h t", h=HG)
                                                ).then_inc(*once(big_read_dve))
                        else:
                            m = level_masks[0:TS, lv, 0:TS].rearrange("p (a t) -> p a t", a=1)
                            dve.copy_predicated(att_s[:, :, :], m.to_broadcast([TS, HG, TS]),
                                                b[0:TS, 0:HG * TS].rearrange("p (h t) -> p h t", h=HG)
                                                ).then_inc(*once(big_read_dve))

                products(0)
                for lv in range(len(LEVELS)):
                    if lv + 1 < len(LEVELS):
                        products(lv + 1)
                    keep(lv)
                own(big_read_dve, L, BIGD_BEFORE(BIG["att"]))
                nl = len(LEVELS)
                dve.wait_ge(decay_ready.sem, decay_ready.at(L, nl + 1))
                apart(dve)
                ch(dve.tensor_tensor(hq[:, :, :], hq[:, :, :], decay[0][:, :, :], ALU.mult))
                dve.wait_ge(decay_ready.sem, decay_ready.at(L, nl + 2))
                apart(dve)
                dve.tensor_tensor(scaled[0][:, :, :], hk[:, :, :], decay[1][:, :, :], ALU.mult
                                  ).then_inc(*once(att_ready))
                own(att_ready, L, 1)
                bank = auxd(L, "state0")
                dve.tensor_copy(s_mid[:, :, :].rearrange("p h e -> p (h e)"), bank).then_inc(*once(auxd_read))
                own(auxd_read, L, AUXD["state0"] + 1)
                bank = auxd(L, "state1")
                for h in range(HG):
                    ins = dve.scalar_tensor_tensor(out=s_end[:, h, :], in0=s_mid[:, h, :],
                                                   scalar=decay[0][:, h, TP - 1:TP],
                                                   in1=bank[:, h * P:(h + 1) * P], op0=ALU.mult, op1=ALU.add)
                ins.then_inc(*once(auxd_read))
                own(auxd_read, L, AUXD["state1"] + 1)
                dve.sem_inc(*once(states_done))
                top_k(score1[:, :], ROUNDS_P, P)
                ch(dve.tensor_tensor(score1[:, :], score1[:, :], causal[:, 128:384], ALU.add))
                top_k(score0[:, :], ROUNDS_P, P)
                ch(dve.tensor_tensor(score0[:, :], score0[:, :], causal[:, 0:128], ALU.add))
                top_k(score_s[:, :], ROUNDS_S, TS)
                dve.tensor_tensor(score_s[:, PADS + PAST:], score_s[:, PADS + PAST:], causal_s[:, :], ALU.add
                                  ).then_inc(*once(att_ready))
                own(att_ready, L, 2)
                for h in range(HG):
                    bank = auxd(L, f"ms_o{h}")
                    dve.tensor_scalar(decay[1][:, h, :], bank[:, 0:T], EPS, None, ALU.add
                                      ).then_inc(*once(auxd_read))
                own(auxd_read, L, AUXD["ms_o3"] + 1)
                dve.reciprocal(decay[1][:, :, :], decay[1][:, :, :]).then_inc(*once(inv_o_ready))
                for h in range(HG):
                    dve.wait_ge(state_decayed.sem, state_decayed.at(L, h + 1))
                    apart(dve)
                    for half in range(2):
                        bank = auxd(L, f"state_s{h}{'ab'[half]}")
                        v = state[:, 4 * half:4 * half + 4, h, :]
                        dve.tensor_tensor(v, v, bank.rearrange("p (b e) -> p b e", b=4), ALU.add
                                          ).then_inc(*once(auxd_read))
                own(auxd_read, L, AUXD["state_s3b"] + 1)
                dve.sem_inc(*once(states_done))
                dve.wait_ge(r_o_ready.sem, r_o_ready.at(L, 1))
                apart(dve)
                for h in range(HG):
                    ch.add(dve.scalar_tensor_tensor(out=o_hg[:, h, :], in0=o_hg[:, h, :], scalar=bound[:, 2, 0:1],
                                                    in1=decay[1][:, h, :], op0=ALU.mult, op1=ALU.mult))
                ch.settle()
                dve.tensor_tensor(mixed[:, 4:8, :], o_hg[:, :, :], hgate[:, :, :], ALU.mult
                                  ).then_inc(*once(attended))
                own(attended, L, 1)

                def mask_scores(t):
                    score, _, keys = fills[t]
                    per = 512 // keys
                    b0 = BIG["att"] if t else BIG["att0"]
                    order = [(0, 0), (1, 0), (0, 2), (1, 2)] if t else [(0, 0), (1, 0)]
                    for k, (g, j) in enumerate(order):
                        b = big(b0 + k)
                        for a in range(per):
                            h = 4 * g + j + a
                            ins = dve.tensor_tensor_reduce(probs[:, h, 0:keys], b[:, a * keys:(a + 1) * keys],
                                                           score[:, :], 1.0, TAKEN, ALU.add, ALU.max,
                                                           peak[:, t, h:h + 1])
                        ins.then_inc(*once(big_read_dve))
                    own(big_read_dve, L, BIGD_BEFORE(b0 + len(order)))
                    dve.tensor_scalar(peak[:, t, :], peak[:, t, :], -(HD ** -0.5), None, ALU.mult
                                      ).then_inc(*once(masked))
                    own(masked, L, 2 - t)

                def normalise(t):
                    keys = fills[t][2]
                    dve.wait_ge(exped.sem, exped.at(L, 2 - t))
                    apart(dve)
                    ch(dve.reciprocal(total[:, t, :], total[:, t, :]))
                    for h in range(NH):
                        ins = dve.tensor_scalar(probs[:, h, 0:keys], probs[:, h, 0:keys], total[:, t, h:h + 1],
                                                None, ALU.mult)
                    ins.then_inc(*once(normed))

                def keep_attended(name, t0, m):
                    bank = auxd(L, name)
                    dve.tensor_copy(mixed[:, 0:4, t0:t0 + m], bank.rearrange("p (j t) -> p j t", j=4)
                                    ).then_inc(*once(auxd_read))

                mask_scores(1)
                for pair in range(4):
                    b = big(BIG["att_s"] + pair)
                    dve.tensor_copy(probs_s[:, pair, :], b[:, 0:KEYS_S]).then_inc(*once(big_read_dve))
                own(big_read_dve, L, BIGD_BEFORE(BIG["att_s"] + 4))
                ch(dve.tensor_reduce(peak[:, 2, 0:4], probs_s[:, :, :], AX.X, ALU.max))
                normalise(1)
                dve.wait_ge(auxa_done.sem, auxa_done.at(L, AUXA["pT1_11"] + 1))
                apart(dve)
                mask_scores(0)
                dve.tensor_scalar(peak[:, 2, 0:4], peak[:, 2, 0:4], -(HD ** -0.5), None, ALU.mult
                                  ).then_inc(*once(masked))
                keep_attended("pv1", 128, 128)
                normalise(0)
                dve.wait_ge(exped.sem, exped.at(L, 3))
                apart(dve)
                ch(dve.reciprocal(total[:, 2, 0:4], total[:, 2, 0:4]))
                for pair in range(4):
                    ins = dve.tensor_scalar(probs_s[:, pair, :], probs_s[:, pair, :], total[:, 2, pair:pair + 1],
                                            None, ALU.mult)
                ins.then_inc(*once(normed))
                keep_attended("pv0", 0, 128)
                bank = auxd(L, "pvs").rearrange("p (b g j t) -> p j b g t", b=SEQS, g=2, j=4)
                for g in range(2):
                    rows = slice(64 * g, 64 * g + 64)
                    dst = mixed[rows, 0:4, TP:T].rearrange("p j (b t) -> p j b t", b=SEQS)
                    ins = dve.tensor_copy(dst, bank[rows, :, :, g, :])
                ins.then_inc(*once(auxd_read))
                own(auxd_read, L, AUXD["pvs"] + 1)
                dve.sem_inc(*once(attended))
                split_lo(L, LOAD_AT["gateup2", 0])
                norm_out(L, 1, 3, 4)
                split_lo(L, LOAD_AT["gateup2", 1])
                norm_in(L, 2)
                ffn(L, 2)
                norm_out(L, 2, 5)
                norm_in(L, 3)
                dve.wait_ge(r_pre_ready.sem, r_pre_ready.at(L, 4))
                apart(dve)
                for j in range(KT):
                    b = 2 * (j % 2)
                    dve.wait_ge(tile_done.sem, tile_done.at(L, tile_at("ple", j // 2, j % 2) + 1))
                    dve.tensor_tensor(gate_in[:, j % 2, :], ps[:, b, 0:T], r_pre[:, :], ALU.mult
                                      ).then_inc(*once(gate_scaled))
                    dve.wait_ge(gate_acted.sem, gate_acted.at(L, 2 * FT + j + 1))
                    dve.tensor_tensor(y[:, j, :], ps[:, b + 1, 0:T], gate_out[:, j % 2, :], ALU.mult
                                      ).then_inc(*once(pair_read))
                norm_out(L, 3, 7)
            counts.in_layer = 2
            for n in range(6):
                dve.wait_ge(final_turned.sem, n + 1)
                t, half = n // 2, n % 2
                m = TOK_TILES[t][1]
                dve.tensor_copy(tokens[0:m, t, 512 * half:512 * half + 512], ps[0:m, n, :]
                                ).then_inc(*once(final_copied))

        @block.tensor
        def _(pe):
            counts.in_layer = 0
            pe.wait_ge(tokens_in.sem, 32)
            pe.wait_ge(constants_in.sem, 16 * N_CONST)
            for k in range(KT):
                for t, (a, m) in enumerate(TOK_TILES):
                    ins = pe.transpose(ps[:, k, a:a + m], tokens[0:m, t, k * P:(k + 1) * P], identity[0:m, 0:m])
                ins.then_inc(*once(turned))
            pe.wait_ge(turned_read.sem, 1)
            pe.transpose(ps[:, 0, 320:448], rows_a[:, :], identity[:, :]).then_inc(*once(turned))
            pe.wait_ge(turned_read.sem, 2)
            pe.transpose(ps[:, 1, 320:330], rows_b[:, :], identity[0:10, 0:10]).then_inc(*once(turned))
            pe.wait_ge(turned_read.sem, KT + 2)
            pe.wait_ge(setup_done.sem, 1)

            def wait(s, value):
                pe.wait_ge(s.sem, value)
                apart(pe)

            def slot_full(L, n, i=None):
                full = slot_in[n % 2]
                value = full.at(L, dma_count_before(n) + 16 * DMAS(n))
                if i is not None:
                    value = value + i * (16 * DMAS(n))
                pe.wait_ge(full.sem, value)

            def mean_x(L, stage):
                wait(squarex_added, squarex_added.at(L, (stage + 1) * KT))
                pe.matmul(ps[:, 7, 0:T], mean_model[:, :], sumsqx[:, :], start=True, stop=True
                          ).then_inc(*once(msx_ready))

            def mean_y(L, stage):
                wait(square_added, square_added.at(L, (stage + 1) * KT))
                pe.matmul(ps[:, 6, 0:T], mean_model[:, :], sumsq[:, :], start=True, stop=True
                          ).then_inc(*once(ms_ready))

            def product(bank, weights, rhs, last=None):
                n = len(rhs)
                for k in range(n):
                    ins = pe.matmul(bank, weights(k), rhs[k], start=(k == 0), stop=(k == n - 1))
                if last is not None:
                    ins.then_inc(*last)

            def product_split(bank, hi, lo, rhs_hi, rhs_lo, last=None, first=0, end=None):
                n = len(rhs_hi)
                for k in range(first, n if end is None else end):
                    pe.matmul(bank, hi(k), rhs_hi[k], start=(k == 0), stop=False)
                    pe.matmul(bank, hi(k), rhs_lo[k], start=False, stop=False)
                    ins = pe.matmul(bank, lo(k), rhs_hi[k], start=False, stop=(k == n - 1))
                if last is not None:
                    ins.then_inc(*last)

            def us(a=0, b=T):
                return [u[:, k, a:b] for k in range(KT)]

            def ffn(L, which, stage):
                n0 = LOAD_AT[f"gateup{which}", 0]
                m = FT * (which - 1)

                u_parts = [[t[:, k, :] for k in range(KT)] for t in (u_hi, u_lo)]

                def tile(half, i=None):
                    v = slot_lo_ready.at(L, splits_before(n0) + half + 1)
                    pe.wait_ge(slot_lo_ready.sem, v if i is None else v + i * 2)
                    apart(pe)
                    hi, lo = (t[(n0 + half) % 2][:, 0:2 * KT * P].rearrange("p (a k n) -> p a k n", a=2, k=KT)
                              for t in (slot_hi, slot_lo))
                    v = pair_read.at(L, m + half - 1)
                    pe.wait_ge(pair_read.sem, v if i is None else v + i * 2)
                    product_split(ps[:, 2 * half, 0:T], lambda k: hi[:, 0, k, :], lambda k: lo[:, 0, k, :],
                                  *u_parts)
                    product_split(ps[:, 2 * half + 1, 0:T], lambda k: hi[:, 1, k, :], lambda k: lo[:, 1, k, :],
                                  *u_parts, once(tile_done))

                wait(u_lo_ready, u_lo_ready.at(L, stage // 2 * KT + KT))
                tile(0)
                mean_x(L, stage)
                tile(1)
                apart(pe)
                counts.times = FT // 2 - 1
                with pe.Fori(1, FT // 2) as i:
                    for half in range(2):
                        tile(half, i)
                counts.times = 1
                n0 = LOAD_AT[f"down{which}", 0]
                wait(hidden_ready, hidden_ready.at(L, m + FT - 2))
                y0 = (0 if which == 1 else 2) * KT
                counts.times = KT // 2
                with pe.Fori(0, KT // 2) as i:
                    for half in range(2):
                        pe.wait_ge(slot_lo_ready.sem,
                                   slot_lo_ready.at(L, splits_before(n0) + half + 1) + i * 2)
                        apart(pe)
                        hi, lo = (t[(n0 + half) % 2][:, :].rearrange("p (f n) -> p f n", f=FT)
                                  for t in (slot_hi, slot_lo))
                        pe.wait_ge(square_ready.sem, square_ready.at(L, y0 + half - 1) + i * 2)
                        parts = (ps[:, 4 + half, 0:T], lambda k: hi[:, k, :], lambda k: lo[:, k, :],
                                 [hidden_hi[:, k, :] for k in range(FT)],
                                 [hidden_lo[:, k, :] for k in range(FT)])
                        product_split(*parts, end=FT - 2)
                        if half == 0:
                            wait(hidden_ready, hidden_ready.at(L, m + FT))
                        product_split(*parts, once(tile_done), first=FT - 2)
                counts.times = 1
                mean_y(L, 0 if which == 1 else 2)

            def mix_bank(L, n):
                wait(mix_read, mix_read.at(L, n - 1))
                return ps[:, n % 2, :]

            base = tile_at("iq", 0)

            def feature_tile(L, kind, i, k):
                if k == 0:
                    slot_full(L, LOAD_AT[kind, i])
                    apart(pe)
                bank = mix_bank(L, tile_at(kind, i, k) - base)
                s = slots[LOAD_AT[kind, i] % 2][:, 0:KT * 256].rearrange("p (k n) -> p k n", k=KT)
                product(bank[:, 0:T], lambda c: s[:, c, 128 * k:128 * k + 128], us(), once(tile_done))

            def token_tiles(L, kind, i, width):
                slot_full(L, LOAD_AT[kind, i])
                apart(pe)
                s = slots[LOAD_AT[kind, i] % 2][:, 0:KT * width].rearrange("p (k n) -> p k n", k=KT)
                for t, (a, m) in enumerate(TOK_TILES):
                    bank = mix_bank(L, tile_at(kind, i, t) - base)
                    product(bank[0:m, 0:width], lambda c: u[:, c, a:a + m],
                            [s[:, c, :] for c in range(KT)], once(tile_done))

            def aux(L, table, name, done, read):
                k = table[name]
                wait(read, read.at(L, k - 1))
                return ps[:, ((2, 7) if table is AUXD else (3, 6))[k % 2], :]

            def auxd(L, name):
                return aux(L, AUXD, name, auxd_done, auxd_read)

            def auxa(L, name):
                return aux(L, AUXA, name, auxa_done, auxa_read)

            def big(L, n):
                return ps[:, 4 + n % 2, :]

            def sample_scores(bank, queries, new, past, b, start):
                for g in range(2):
                    rows = slice(64 * g, 64 * g + 64)
                    out = bank[64 * (b % 2) + 32 * g:64 * (b % 2) + 32 * g + 32]
                    lhs = queries[rows, b].rearrange("p j t -> p (j t)")
                    pe.matmul(out[:, 0:PAST], lhs,
                              past[rows, 2 * b:2 * b + 2, :].rearrange("p n t -> p (n t)"),
                              start=start, stop=True, skip_group_check=True)
                    ins = pe.matmul(out[:, PAST:KEYS_S], lhs, new[rows, TP:T], start=start, stop=True,
                                    skip_group_check=True)
                return ins

            counts.in_layer = 1
            with pe.Fori(0, LAYERS) as L:
                ffn(L, 1, 0)
                wait(u_ready, u_ready.at(L, 2 * KT))
                feature_tile(L, "iq", 0, 0)
                mean_x(L, 1)
                feature_tile(L, "iq", 0, 1)
                wait(r_pre_ready, r_pre_ready.at(L, 2))
                bank = auxd(L, "r_tok")
                for t, (a, m) in enumerate(TOK_TILES):
                    ins = pe.matmul(bank[0:m, t:t + 1], r_pre[0:1, a:a + m], identity[0:1, 0:1],
                                    start=True, stop=True)
                ins.then_inc(*once(auxd_done))
                feature_tile(L, "iq", 1, 0)
                feature_tile(L, "iq", 1, 1)
                wait(embeddings_in, embeddings_in.at(L, 32))
                for k in range(2):
                    bank = auxa(L, f"p{k}")
                    for t, (a, m) in enumerate(TOK_TILES):
                        ins = pe.transpose(bank[:, a:a + m], p_tok[0:m, t, k * P:(k + 1) * P], identity[0:m, 0:m])
                    ins.then_inc(*once(auxa_done))
                token_tiles(L, "kv", 0, 256)
                for j in range(4):
                    bank = auxd(L, f"rot_iq{j}")
                    if j == 0:
                        wait(mix_read, mix_read.at(L, tile_at("iq", 1, 1) - base + 1))
                    pe.matmul(bank[:, 0:T], rotate[:, :], raw_iq[:, j, :], start=True, stop=True
                              ).then_inc(*once(auxd_done))
                token_tiles(L, "ikiw", 0, 72)
                wait(caches_in, caches_in.at(L, 16 * 48))
                for src, name in ((k_pages[:, :, :], "kpages"),
                                  (i_pages[:, :, :, :].rearrange("p n a d -> p n (a d)"), "ipages")):
                    for k in range(4):
                        bank = auxa(L, f"{name}{k}")
                        for n in range(4):
                            ins = pe.transpose(bank[:, n * P:(n + 1) * P], src[:, 4 * k + n, :], identity[:, :])
                        ins.then_inc(*once(auxa_done))
                for i in range(2):
                    for k in range(2):
                        feature_tile(L, "hf", i, k)
                wait(roped, roped.at(L, 1))
                for name, src in (("kT", kv_tok), ("ikT", ik_tok)):
                    bank = auxa(L, name)
                    for t, (a, m) in enumerate(TOK_TILES):
                        ins = pe.transpose(bank[:, a:a + m], src[0:m, t, 0:P], identity[0:m, 0:m])
                    ins.then_inc(*once(auxa_done))
                bank = auxd(L, "iwT")
                pe.transpose(bank[0:NH, 0:TS], iw_tok[0:TS, 2, :], identity[0:TS, 0:TS]
                             ).then_inc(*once(auxd_done))
                wait(auxd_read, auxd_read.at(L, AUXD["iwT"] + 1))
                bank = auxd(L, "iwrow")
                pe.matmul(bank[:, 0:TS], head_row[:, :], iwT[:, :], start=True, stop=True
                          ).then_inc(*once(auxd_done))
                for i in range(2):
                    for k in range(2):
                        feature_tile(L, "hq", i, k)
                wait(auxa_read, auxa_read.at(L, AUXA["ikT"] + 1))
                n = BIG["idx"]

                for kk, q0, order in ((256, 128, [(0, 0), (1, 0), (0, 2), (1, 2)]), (128, 0, [(0, 0), (1, 0)])):
                    for g, j in order:
                        if n >= BIG["idx"] + 2:
                            wait(big_read_act, big_read_act.at(L, n - BIG["idx"] - 1))
                        bank = big(L, n)
                        for a in range(512 // kk):
                            ins = pe.matmul(bank[:, a * kk:(a + 1) * kk],
                                            iq[64 * g:64 * g + 64, j + a, q0:q0 + 128],
                                            ikT[64 * g:64 * g + 64, 0:kk], start=True, stop=True)
                        ins.then_inc(*once(big_done))
                        n += 1
                for pair in range(4):
                    wait(big_read_act, big_read_act.at(L, n - BIG["idx"] - 1))
                    bank = big(L, n)
                    for b2 in range(2):
                        b = 2 * pair + b2
                        ins = sample_scores(bank, iq_s, ikT, ikT_past, b, True)
                    ins.then_inc(*once(big_done))
                    n += 1
                bank = auxd(L, "score_s")
                wait(auxd_read, auxd_read.at(L, AUXD["iwrow"] + 1))
                for pair in range(4):
                    wait(big_read_act, big_read_act.at(L, 7 + pair))
                    ins = pe.matmul(bank[0:TS, 0:KEYS_S], iw_mask[:, pair, :], relu_s[:, pair, :],
                                    start=(pair == 0), stop=(pair == 3))
                ins.then_inc(*once(auxd_done))
                for i in range(2):
                    for k in range(2):
                        feature_tile(L, "q", i, k)
                for i in range(2):
                    token_tiles(L, "hi", i, 256)
                for j in range(4):
                    bank = auxd(L, f"rot_q{j}")
                    pe.matmul(bank[:, 0:T], rotate[:, :], raw_q[:, j, :], start=True, stop=True
                              ).then_inc(*once(auxd_done))
                for i in range(2):
                    for k in range(2):
                        feature_tile(L, "hgate", i, k)
                n = BIG["levels"]
                wait(hg_dve, hg_dve.at(L, HGD["scan"]))

                use = [n]

                def chunk(c, a, b):
                    n = use[0]
                    use[0] += 1
                    if n - BIG["levels"] >= 2:
                        wait(big_read_dve, big_read_dve.at(L, BIGD_BEFORE(n - 1)))
                    bank = big(L, n)
                    t0, m = TOK_TILES[c]
                    for h in range(HG):
                        ins = pe.matmul(bank[0:m, h * m:(h + 1) * m], a[:, h, t0:t0 + m], b[:, h, t0:t0 + m],
                                        start=True, stop=True)
                    ins.then_inc(*once(big_done))

                for c in range(3):
                    chunk(c, hk, hq)
                for lv, h in enumerate(LEVELS):
                    wait(scaled_ready, scaled_ready.at(L, lv + 1))
                    for c in range(3 if 2 * h <= STEP else 2):
                        assert use[0] == LEVEL_BIG[lv][c]
                        chunk(c, scaled[lv % 2], scaled[lv % 2])
                wait(att_ready, att_ready.at(L, 1))
                for t, (a, m) in enumerate(TOK_TILES):
                    bank = auxa(L, f"key{t}")
                    for h in range(HG):
                        ins = pe.transpose(bank[0:m, h * P:(h + 1) * P], scaled[0][:, h, a:a + m], identity[:, :])
                    ins.then_inc(*once(auxa_done))
                for t in range(2):
                    wait(auxa_read, auxa_read.at(L, AUXA[f"key{t}"] + 1))
                    bank = auxd(L, f"state{t}")
                    for h in range(HG):
                        ins = pe.matmul(bank[:, h * P:(h + 1) * P], key_tok[:, t, h, :],
                                        v_tok[:, t, h * P:(h + 1) * P], start=True, stop=True)
                    ins.then_inc(*once(auxd_done))
                wait(states_in, states_in.at(L, 16 * 20))
                wait(auxd_read, auxd_read.at(L, AUXD["state0"] + 1))
                for h in range(HG):
                    bank = auxa(L, f"o{h}")
                    v = lambda t, m: v_tok[0:m, t, h * P:(h + 1) * P]
                    pe.matmul(bank[:, 0:128], v(0, P), att_p[:, 0, h, :], start=True, stop=True)
                    pe.matmul(bank[:, 128:256], v(1, P), att_p[:, 1, h, :], start=True, stop=False)
                    pe.matmul(bank[:, 128:256], s_mid[:, h, :], hq[:, h, 128:256], start=False, stop=True)
                    pe.matmul(bank[:, TP:T], v(2, TS), att_s[:, h, :], start=True, stop=True,
                              skip_group_check=True)
                    for b in range(SEQS):
                        ins = pe.matmul(bank[:, TP + b * STEP:TP + (b + 1) * STEP], state[:, b, h, :],
                                        hq[:, h, TP + b * STEP:TP + (b + 1) * STEP], start=False,
                                        stop=True, skip_group_check=True)
                    ins.then_inc(*once(auxa_done))
                for h in range(HG):
                    wait(auxa_read, auxa_read.at(L, AUXA[f"o{h}"] + 1))
                    bank = auxd(L, f"ms_o{h}")
                    pe.matmul(bank[:, 0:T], mean_head[:, :], scaled[1][:, h, :], start=True, stop=True
                              ).then_inc(*once(auxd_done))
                wait(auxa_read, auxa_read.at(L, AUXA["key2"] + 1))
                for h in range(HG):
                    wait(v_own_ready, v_own_ready.at(L, h + 1))
                    for half in range(2):
                        bank = auxd(L, f"state_s{h}{'ab'[half]}")
                        pe.matmul(bank, key_tok[0:TS, 2, h, :],
                                  v_own[:, h % 2, 4 * half:4 * half + 4, :].rearrange("p b e -> p (b e)"),
                                  start=True, stop=True).then_inc(*once(auxd_done))
                def att_scores(t):
                    n = BIG["att"] if t else BIG["att0"]
                    kk, q0 = (256, 128) if t else (128, 0)
                    for g, j in ([(0, 0), (1, 0), (0, 2), (1, 2)] if t else [(0, 0), (1, 0)]):
                        wait(big_read_dve, big_read_dve.at(L, BIGD_BEFORE(n - 1)))
                        bank = big(L, n)
                        for a in range(512 // kk):
                            ins = pe.matmul(bank[:, a * kk:(a + 1) * kk],
                                            q[64 * g:64 * g + 64, j + a, q0:q0 + 128],
                                            kT[64 * g:64 * g + 64, 0:kk], start=True, stop=True)
                        ins.then_inc(*once(big_done))
                        n += 1

                def turn_probs(t, keys):
                    for k in range(keys):
                        for g in range(2):
                            bank = auxa(L, f"pT{t}_{k}{g}")
                            for a in range(4):
                                ins = pe.transpose(bank[:, a * P:(a + 1) * P],
                                                   probs[:, 4 * g + a, k * P:(k + 1) * P], identity[:, :])
                            ins.then_inc(*once(auxa_done))

                def weigh(t, keys):
                    bank = auxd(L, f"pv{t}")
                    for k in range(keys):
                        wait(auxa_read, auxa_read.at(L, AUXA[f"pT{t}_{k}1"] + 1))
                        for g in range(2):
                            ins = pe.matmul(bank[64 * g:64 * g + 64, :], kv_tok[:, k, 128 + 64 * g:192 + 64 * g],
                                            probsT[:, k, 4 * g:4 * g + 4, :].rearrange("p h t -> p (h t)"),
                                            start=(k == 0), stop=(k == keys - 1))
                    ins.then_inc(*once(auxd_done))

                assert use[0] == BIG["att"]
                att_scores(1)
                for pair in range(4):
                    n = BIG["att_s"] + pair
                    wait(big_read_dve, big_read_dve.at(L, BIGD_BEFORE(n - 1)))
                    wait(att_ready, att_ready.at(L, 2))
                    bank = big(L, n)
                    pe.matmul(bank[:, 0:KEYS_S], spread[:, pair, :], score_s[:, PADS:], start=True, stop=True,
                              skip_group_check=True)
                    for b2 in range(2):
                        b = 2 * pair + b2
                        ins = sample_scores(bank, q_s, kT, kT_past, b, False)
                    ins.then_inc(*once(big_done))
                wait(normed, normed.at(L, 1))
                turn_probs(1, 2)
                att_scores(0)
                weigh(1, 2)
                wait(normed, normed.at(L, 2))
                turn_probs(0, 1)
                weigh(0, 1)
                wait(normed, normed.at(L, 3))
                for k, (a, m) in enumerate(TOK_TILES):
                    bank = auxa(L, f"pTs{k}")
                    for pair in range(4):
                        ins = pe.transpose(bank[0:m, pair * P:(pair + 1) * P], probs_s[:, pair, a:a + m],
                                           identity[:, :])
                    ins.then_inc(*once(auxa_done))
                wait(auxa_read, auxa_read.at(L, AUXA["pTs2"] + 1))
                bank = auxd(L, "pvs")
                for b in range(SEQS):
                    out = bank[:, 64 * b:64 * b + 64]
                    c = slice(64 * (b % 2), 64 * (b % 2) + 64)
                    for k in range(2):
                        pe.matmul(out, v_pages[:, 2 * b + k, :], probsT_s[:, k, b // 2, c],
                                  start=(k == 0), stop=False)
                    ins = pe.matmul(out, kv_tok[0:TS, 2, 128:256], probsT_s[0:TS, 2, b // 2, c],
                                    start=False, stop=True)
                ins.then_inc(*once(auxd_done))
                wait(attended, attended.at(L, 2))
                for i in range(4):
                    slot_full(L, LOAD_AT["out", i])
                    apart(pe)
                    s = slots[LOAD_AT["out", i] % 2][:, 0:KT * 256].rearrange("p (k n) -> p k n", k=KT)
                    for k in range(2):
                        pe.wait_ge(square_ready.sem, square_ready.at(L, KT + 2 * i + k - 1))
                        apart(pe)
                        product(ps[:, 4 + k, 0:T], lambda c: s[:, c, 128 * k:128 * k + 128],
                                [mixed[:, c, :] for c in range(KT)], once(tile_done))
                mean_y(L, 1)
                ffn(L, 2, 2)
                wait(u_ready, u_ready.at(L, 4 * KT))
                for i in range(4):
                    slot_full(L, LOAD_AT["ple", i])
                    apart(pe)
                    s = slots[LOAD_AT["ple", i] % 2][:, 0:(KT + 2) * 256].rearrange("p (k n) -> p k n", k=KT + 2)
                    for k in range(2):
                        j = 2 * i + k
                        wait(pair_read, pair_read.at(L, 2 * FT + j - 1))
                        product(ps[:, 2 * k, 0:T], lambda c: s[:, c, 128 * k:128 * k + 128], us())
                        product(ps[:, 2 * k + 1, 0:T], lambda c: s[:, KT + c, 128 * k:128 * k + 128],
                                [pT[:, c, :] for c in range(2)], once(tile_done))
                        if j == 0:
                            mean_x(L, 3)
                mean_y(L, 3)
            counts.in_layer = 2
            pe.wait_ge(x_ready.sem, x_ready.at(LAYERS, 0))
            for n in range(6):
                t, half = n // 2, n % 2
                a, m = TOK_TILES[t]
                for k in range(4):
                    ins = pe.transpose(ps[0:m, n, k * P:(k + 1) * P], x[:, 4 * half + k, a:a + m], identity[:, :])
                ins.then_inc(*once(final_turned))

    return {n: tuple(s.seen) for n, s in signals.items()}


_INS = ["x_prompt", "x_sample", "p_prompt", "p_sample", "cache_k", "cache_v", "cache_idx_k", "state_hgrn",
        "page_table", "n_f1_pre", "n_f1_post", "w_f1_gate", "w_f1_up", "w_f1_down", "n_mix_pre", "n_mix_post",
        "w_in", "hg_lb_logits", "hg_norm", "w_out", "n_f2_pre", "n_f2_post", "w_f2_gate", "w_f2_up", "w_f2_down",
        "n_ple_pre", "n_ple_post", "w_ple_proj", "w_ple_gate"]
_OUTS = [("y_prompt", (1, TP, DM)), ("y_sample", (SEQS, STEP, DM)),
         ("k_prompt", (LAYERS, 1, TP, KVH, HD)), ("v_prompt", (LAYERS, 1, TP, KVH, HD)),
         ("idx_k_prompt", (LAYERS, 1, TP, HD)), ("hgrn_prompt", (LAYERS, 1, HG, P, P)),
         ("k_sample", (LAYERS, SEQS, STEP, KVH, HD)), ("v_sample", (LAYERS, SEQS, STEP, KVH, HD)),
         ("idx_k_sample", (LAYERS, SEQS, STEP, HD)), ("hgrn_sample", (LAYERS, SEQS, HG, P, P))]


def declared(nc, arrays):
    A = {name: nc.dram_tensor(f"in_{name}", a.shape, mybir.dt.from_np(a.dtype), kind="ExternalInput").ap()
         for name, a in arrays.items()}
    O = {name: nc.dram_tensor(f"out_{name}", shape, F32, kind="ExternalOutput").ap() for name, shape in _OUTS}
    return A, O


def kernel(**inputs):
    import numpy as _np
    import concourse.bacc as _bacc
    from concourse.bass_utils import run_bass_kernel_spmd as _run

    arrays = {name: _np.ascontiguousarray(inputs[name]) for name in _INS}
    arrays.update(constants())
    totals = {}
    for _ in range(2):
        nc = _bacc.Bacc("TRN2", target_bir_lowering=False, num_devices=1)
        totals = build(nc, *declared(nc, arrays), totals)
    r = _run(nc, [{f"in_{k}": v for k, v in arrays.items()}], core_ids=[0])
    return tuple(r.results[0][f"out_{name}"] for name, _ in _OUTS)
```

```python
import numpy as np
import concourse.bass as bass
from concourse import mybir
from contextlib import ExitStack

F32 = mybir.dt.float32
F32R = mybir.dt.float32r
U8 = mybir.dt.uint8
I32 = mybir.dt.int32
ALU = mybir.AluOpType
ACT = mybir.ActivationFunctionType
AX = mybir.AxisListType

P = 128
LAYERS = 2
DM, KT = 1024, 8
TP, TS = 256, 64
T = TP + TS
SEQS, STEP = 8, 8
TOK_TILES = [(0, 128), (128, 128), (256, 64)]
FF = 2816
FT = FF // P
HD, NH, KVH, GROUP = 64, 8, 2, 4
PAGE, NPAGES = 128, 2
PAST = PAGE * NPAGES
HG = 4
PD = 256
EPS = 1e-6
NEG = -1e30
TAKEN = -3e38
SENTINEL = 3e38
TOPK_P, TOPK_S = TP // 4, (PAST + STEP) // 4
ROUNDS_P = TOPK_P // 8
ROUNDS_S = -(-TOPK_S // 8)
PADS = ROUNDS_S * 8 - TOPK_S
KEYS_S = PAST + TS
CHUNK = 128
LEVELS = [1, 2, 4, 8, 16, 32, 64]

C_Q, C_K, C_V, C_IQ, C_IK, C_IW = 0, 512, 640, 768, 1280, 1344
C_HQ, C_HF, C_HI, C_HG = 1352, 1864, 2376, 2888

LOADS = []
for t in range(FT):
    LOADS.append(("gateup1", t, 1))
for j in range(KT):
    LOADS.append(("down1", j, 1))
for kind, count, tiles in (("iq", 2, 2), ("kv", 1, 3), ("ikiw", 1, 3), ("hf", 2, 2), ("hq", 2, 2),
                           ("q", 2, 2), ("hi", 2, 3), ("hgate", 2, 2), ("out", 4, 2)):
    for i in range(count):
        LOADS.append((kind, i, tiles))
for t in range(FT):
    LOADS.append(("gateup2", t, 1))
for j in range(KT):
    LOADS.append(("down2", j, 1))
for i in range(4):
    LOADS.append(("ple", i, 2))
assert len(LOADS) % 2 == 0
LOAD_AT = {(k, i): n for n, (k, i, _) in enumerate(LOADS)}
TILES_BEFORE = [sum(x[2] for x in LOADS[:n]) for n in range(len(LOADS) + 1)]
TILES = TILES_BEFORE[-1]
SLOT = FT * P


def tile_at(kind, i, k=0):
    return TILES_BEFORE[LOAD_AT[kind, i]] + k


def dmas_of(kind):
    return {"gateup1": 2, "gateup2": 2, "iq": 4, "q": 4, "out": 3, "ple": 2}.get(kind, 1)


SPLIT_KINDS = ("gateup1", "down1", "out", "gateup2", "down2", "ple")
assert FT % 2 == 0 and KT % 2 == 0


def split_size(n):
    return {"gateup": 2 * KT * P, "down": FT * P, "out": KT * 2 * P, "ple": (KT + 2) * 2 * P}[LOADS[n][0].rstrip("12")]


def splits_before(n):
    return sum(LOADS[m][0] in SPLIT_KINDS for m in range(n))


def dma_count_before(n):
    return sum(16 * dmas_of(LOADS[m][0]) for m in range(n % 2, n, 2))


def DMAS(n):
    return dmas_of(LOADS[n][0])


def _order(names):
    return {name: n for n, name in enumerate(names)}


AUXD = _order(["r_tok", "rot_iq0", "rot_iq1", "rot_iq2", "rot_iq3", "iwT", "iwrow", "score_s",
               "rot_q0", "rot_q1", "rot_q2", "rot_q3", "state0", "state1"]
              + ["ms_o"] + [f"state_s{h}{c}" for h in range(HG) for c in "ab"]
              + [f"r_o{h}" for h in range(HG)] + ["pv1", "pvs", "pv0"])
AUXA = _order(["p0", "p1"] + [f"kpages{k}" for k in range(4)] + [f"ipages{k}" for k in range(4)]
              + ["kT", "ikT", "key0", "key1", "key2"] + [f"o{h}" for h in range(HG)]
              + ["pT1_00", "pT1_01", "pT1_10", "pT1_11", "pTs0", "pTs1", "pTs2", "pT0_00", "pT0_01"])
SOFT = {1: 1, "samples": 2, 0: 3}
LEVEL_BIG, _n = [], 10 + 3
for _h in LEVELS:
    LEVEL_BIG.append(list(range(_n, _n + (3 if 2 * _h <= STEP else 2))))
    _n = LEVEL_BIG[-1][-1] + 1
BIG = {"idx": 0, "levels": 10, "att": _n, "att_s": _n + 4, "att0": _n + 8}


def BIGD_BEFORE(n):
    return n - BIG["levels"]


EV = {"score1": 1, "score0": 2}
MIX_LAST = {kind: tile_at(kind, *last) - tile_at("iq", 0) + 1 for kind, last in (
    ("kv", (0, 2)), ("ikiw", (0, 2)), ("hf", (1, 1)), ("hq", (1, 1)), ("hi", (1, 2)), ("hgate", (1, 1)))}
HGD = {"f": 1, "silu": 2, "scan": 3}


def level_view(t, h):
    if 2 * h <= STEP:
        v = t[:, :, :].rearrange("p g (n two s) -> p (g n) two s", two=2, s=h)
        return v[:, :, 0, :], v[:, :, 1, :]
    v = t[:, :, 0:TP].rearrange("p g (n two s) -> p g n two s", two=2, s=h)
    return v[:, :, :, 0, :], v[:, :, :, 1, :]


def constants():
    f = np.float32
    pos = np.concatenate([np.arange(TP), np.tile(PAST + np.arange(STEP), SEQS)]).astype(f)
    half = HD // 2
    inv = (f(10000.0) ** (-np.arange(half, dtype=f) / f(half))).astype(f)
    ang = (pos[:, None] * inv[None, :]).astype(f).astype(np.float64)
    cos, sin = np.cos(ang).astype(f), np.sin(ang).astype(f)
    c = {}
    c["cos_f"] = np.tile(cos.T, (4, 1))
    c["sin_f"] = np.tile(sin.T, (4, 1))
    tok = np.zeros((2, P, 3, half), f)
    for i, (a, n) in enumerate(TOK_TILES):
        tok[0, :n, i], tok[1, :n, i] = cos[a:a + n], sin[a:a + n]
    c["cos_t"], c["sin_t"] = tok[0].reshape(P, -1), tok[1].reshape(P, -1)
    rot = np.zeros((P, P), f)
    for m in range(P):
        if m % HD < half:
            rot[m + half, m] = -1
        else:
            rot[m - half, m] = 1
    c["rotate"] = rot
    c["identity"] = np.eye(P, dtype=f)
    c["mean_model"] = np.full((P, P), 1.0 / DM, f)
    c["mean_head"] = np.full((P, P), 1.0 / P, f)
    s, t = np.arange(P)[:, None], np.arange(P)[None, :]
    c["level_masks"] = np.stack(
        [((s // (2 * h) == t // (2 * h)) & (s % (2 * h) < h) & (t % (2 * h) >= h)) for h in LEVELS],
        1).astype(f).reshape(P, -1)
    fill = np.zeros((P, 256), f)
    fill[:, 128:] = np.where(t > s, f(NEG), f(0))
    c["causal"] = fill
    a, b = np.arange(TS)[:, None], np.arange(TS)[None, :]
    c["causal_s"] = np.where((a // STEP == b // STEP) & (b % STEP <= a % STEP), f(0), f(NEG)).astype(f)
    spread = np.zeros((TS, 4, P), f)
    for pair in range(4):
        for r in range(P):
            spread[(2 * pair + r // 64) * STEP + r % STEP, pair, r] = 1
    c["spread"] = spread.reshape(TS, -1)
    c["own_token"] = spread.transpose(2, 1, 0).reshape(P, -1).copy()
    head = np.zeros((NH, P), f)
    for r in range(P):
        head[(r % 64) // STEP, r] = 1
    c["head_row"] = head
    reset = np.ones((P, T), f)
    reset[:, 0:TP:CHUNK] = 0
    reset[:, TP::STEP] = 0
    c["carry"] = reset
    own = np.zeros((TS, SEQS), f)
    for r in range(TS):
        own[r, r // STEP] = 1
    c["own_seq"] = own
    return c


EARLY = ["identity", "mean_model"]


def tables():
    c = constants()
    masks = c.pop("level_masks")
    early = np.concatenate([c[n] for n in EARLY], 1)
    late = np.concatenate([np.pad(a, ((0, P - a.shape[0]), (0, 0))) for n, a in c.items() if n not in EARLY], 1)
    return {"early": early, "late": late, "level_masks": masks}


def laid_out(inputs):
    arrays = {name: np.ascontiguousarray(inputs[name]) for name in _INS if name not in _ROWS}
    arrays["rows_a"] = np.concatenate([np.asarray(inputs[n]).reshape(LAYERS * KT, P) for n in _NORMS])
    arrays["rows_b"] = np.concatenate([np.asarray(inputs[n]).reshape(-1, P) for n in ("hg_lb_logits", "hg_norm")])
    arrays.update(tables())
    return arrays


class Signal:

    def __init__(self, nc, ctx, name, totals):
        self.sem = ctx.enter_context(nc.semaphore(name))
        self.name = name
        self.before, self.each, _ = totals.get(name, (0, 0, 0))
        self.seen = [0, 0, 0]

    def at(self, layer, n):
        assert self.each == 0 or self.before + n >= 1, (self.name, n)
        return layer * self.each + (self.before + n)


class Counts:

    def __init__(self):
        self.in_layer, self.times = 0, 1

    def inc(self, sig, by=1):
        sig.seen[self.in_layer] += by * self.times
        return sig.sem, by


def build(nc, A, O, totals):
    ctx = ExitStack()
    counts = Counts()
    signals = {}

    def sig(name):
        signals[name] = Signal(nc, ctx, name, totals)
        return signals[name]

    def once(s):
        return counts.inc(s, 1)

    def dma(s):
        return counts.inc(s, 16)

    with ctx:
        pool_pages = A["cache_k"].shape[1]
        base = -(-nc.sbuf_base // 32) * 32
        cursor = [base]

        def place(name, shape, dt=F32, at=None):
            size = int(np.prod(shape[1:])) * (1 if dt == U8 else 4)
            size = -(-size // 32) * 32
            off = at
            if at is None:
                off = cursor[0]
                cursor[0] += size
            return nc.alloc_sbuf_tensor_at(name, list(shape), dt, offset=off)

        x = place("x", [P, KT, T])
        u_at = cursor[0]
        u = place("u", [P, KT, T])
        slots = [place(f"slot{i}", [P, SLOT]) for i in range(2)]
        consts = constants()
        late = [n for n in consts if n not in EARLY and n != "level_masks"]
        early_table, late_table = (place(name, [P, sum(consts[n].shape[1] for n in names)])
                                   for name, names in (("early_table", EARLY), ("late_table", late)))
        C = {}
        for table, names in ((early_table, EARLY), (late_table, late)):
            at = 0
            for n in names:
                rows, columns = consts[n].shape
                C[n] = table[0:rows, at:at + columns]
                at += columns
        for n, parts in (("cos_t", 3), ("sin_t", 3), ("spread", 4), ("own_token", 4)):
            C[n] = C[n].rearrange("p (a b) -> p a b", a=parts)
        identity, mean_model, mean_head, rotate = (C[n] for n in ("identity", "mean_model", "mean_head", "rotate"))
        cos_f, sin_f, cos_t, sin_t = (C[n] for n in ("cos_f", "sin_f", "cos_t", "sin_t"))
        causal, causal_s, spread, own_token = (C[n] for n in ("causal", "causal_s", "spread", "own_token"))
        head_row, carry, own_seq = (C[n] for n in ("head_row", "carry", "own_seq"))
        level_masks = place("level_masks", [P, len(LEVELS), P], U8)
        gains = place("gains", [P, 8, LAYERS, KT])
        small = place("small", [P, 10])
        bounds = place("bounds", [P, LAYERS, HG])
        bounds_tmp = place("bounds_tmp", [P, 5, HG])
        gain = place("gain", [P, 8, KT])
        bound = place("bound", [P, 3, HG])
        pT_at = cursor[0]
        pT = place("pT", [P, 2, T])
        pT_lo = place("pT_lo", [P, 2, T], F32R, at=pT_at)
        pT_hi = place("pT_hi", [P, 2, T], F32R)
        r_pre, r_post = place("r_pre", [P, T]), place("r_post", [P, T])
        inv_pre, inv_post = r_pre, r_post
        sq = place("sq", [P, 4, T])
        sumsq = place("sumsq", [P, T])
        ffn_small = cursor[0]
        kT, ikT = place("kT", [P, T]), place("ikT", [P, T])
        rope_tmp = place("rope_tmp", [P, 2, T])
        iw_mask = place("iw_mask", [P, 4, TS])
        score0, score1 = place("score0", [P, 128]), place("score1", [P, 256])
        score_s = place("score_s", [TS, PADS + KEYS_S])
        assert cursor[0] - ffn_small >= 4 * 6 * T
        kv_tok = place("kv_tok", [P, 3, 256])
        ik_tok, iw_tok = place("ik_tok", [P, 3, 128]), place("iw_tok", [P, 3, NH])
        r_tok = place("r_tok", [P, 3])
        iwT = place("iwT", [NH, TS])
        top8 = place("top8", [P, 8])
        peak, total = place("peak", [P, 3, NH]), place("total", [P, 3, NH])
        mixed_at = cursor[0]
        mixed_lo = place("mixed_lo", [P, KT, T], F32R)
        shared = cursor[0]
        hidden_hi, hidden_lo = (place(f"hidden_{a}", [P, FT, T], F32R) for a in ("hi", "lo"))
        y = place("y", [P, KT, T])
        hidden_tmp = place("hidden_tmp", [P, 2, T])
        slot_hi = [place(f"slot{i}_hi", [P, SLOT], F32R) for i in range(2)]
        slot_lo1_at = cursor[0] + 4 * SLOT
        slot_lo = [place(f"slot{i}_lo", [P, SLOT], F32R) for i in range(2)]
        gate_in = place("gate_in", [P, 2, T], at=ffn_small)
        gate_out = place("gate_out", [P, 2, T], at=ffn_small + 4 * 2 * T)
        up_out = place("up_out", [P, 2, T], at=ffn_small + 4 * 4 * T)
        u_hi = place("u_hi", [P, KT, T], F32R, at=u_at)
        u_lo = place("u_lo", [P, KT, T], F32R, at=mixed_at)
        ffn_end = cursor[0]
        tokens = place("tokens", [P, 3, DM], at=shared)
        rows_a = place("rows_a", [P, P], at=shared + 4 * 3 * DM)
        rows_b = place("rows_b", [10, P], at=shared + 4 * (3 * DM + P))
        masks_in = place("masks_in", [P, len(LEVELS), P], at=shared + 4 * (3 * DM + 2 * P))
        cursor[0] = shared
        hk, hb, hq = (place(n, [P, HG, T]) for n in ("hk", "hb", "hq"))
        v_tok = place("v_tok", [P, 3, 512])
        att_p, att_s = place("att_p", [P, 2, HG, P]), place("att_s", [TS, HG, TS])
        work_at = cursor[0]
        decay = [place(f"decay{i}", [P, HG, T]) for i in range(2)]
        scaled = [place(f"scaled{i}", [P, HG, T]) for i in range(2)]
        iq_at = cursor[0]
        iq, iq_s = place("iq", [P, 4, TP]), place("iq_s", [P, SEQS, 4, STEP])
        q, q_s = place("q", [P, 4, TP]), place("q_s", [P, SEQS, 4, STEP])
        cache_at = cursor[0]
        k_pages, i_pages = place("k_pages", [P, 16, P]), place("i_pages", [P, 16, 2, HD])
        v_pages = place("v_pages", [P, 16, P])
        kT_past, ikT_past = place("kT_past", [P, 16, P]), place("ikT_past", [P, 16, P])
        state = place("state", [P, SEQS, HG, P])
        s_end = place("s_end", [P, HG, P])
        assert max(cursor[0], ffn_end) <= nc.sbuf_usable_end, (cursor[0], ffn_end)
        mixed_hi = place("mixed_hi", [P, KT, T], F32R, at=shared + 4 * 2 * HG * T)
        out_size = split_size(LOAD_AT["out", 0])
        past_at = cache_at + 4 * 3 * 16 * P
        out_hi = [place(f"out{i}_hi", [P, out_size], F32R, at=at) for i, at in enumerate((work_at, past_at))]
        out_lo = [place(f"out{i}_lo", [P, out_size], F32R, at=at)
                  for i, at in enumerate((work_at + 4 * out_size, slot_lo1_at))]
        p_tok = place("p_tok", [P, 3, PD], at=work_at)
        relu_p = place("relu_p", [P, NH, 256], at=work_at)
        relu_s = place("relu_s", [P, 4, KEYS_S], at=work_at + 4 * 2 * HG * T)
        probs = place("probs", [P, NH, 256], at=work_at)
        probsT = place("probsT", [P, 2, NH, P], at=work_at + 4 * 2 * HG * T)
        probs_0 = place("probs_0", [P, NH, 128], at=past_at + 4 * 16 * P)
        probsT_0 = place("probsT_0", [P, 1, NH, P], at=past_at + 4 * (16 * P + NH * P))
        probs, probsT = {1: probs, 0: probs_0}, {1: probsT, 0: probsT_0}
        hgate = place("hgate", [P, HG, T], at=iq_at)
        raw_iq = place("raw_iq", [P, 4, T], at=work_at + 4 * 2 * HG * T)
        raw_q = place("raw_q", [P, 4, T], at=work_at + 4 * 3 * HG * T)
        rope_tok = place("rope_tok", [P, 4, 3 * 2 * 32], at=work_at + 4 * 3 * HG * T)
        s_mid = place("s_mid", [P, HG, P], at=cache_at + 4 * 7 * HG * P)
        key_tok = place("key_tok", [P, 3, HG, P], at=cache_at)
        v_own = place("v_own", [TS, 2, SEQS, P], at=cache_at + 4 * 3 * HG * P)
        probs_s = place("probs_s", [P, 4, KEYS_S], at=shared + 4 * HG * T)
        probsT_s = place("probsT_s", [P, 3, 4, P], at=cache_at)
        o_hg = place("o_hg", [P, HG, T], at=shared)

        def parts_of(n):
            hi, lo = (out_hi, out_lo) if LOADS[n][0] == "out" else (slot_hi, slot_lo)
            return hi[n % 2][:, 0:split_size(n)], lo[n % 2][:, 0:split_size(n)]

        ps = ctx.enter_context(nc.psum_tensor("ps", [P, 8, 512], F32))

        late_in = sig("late_in")
        constants_in, early_in = sig("constants_in"), sig("early_in")
        tokens_in = sig("tokens_in")
        slot_in = [sig("slot0_in"), sig("slot1_in")]
        caches_in, states_in, embeddings_in = sig("caches_in"), sig("states_in"), sig("embeddings_in")
        y_scaled = sig("y_scaled")
        slot_hi_ready, slot_lo_ready = sig("slot_hi_ready"), sig("slot_lo_ready")
        u_lo_ready = sig("u_lo_ready")
        squarex_ready, squarex_added = sig("squarex_ready"), sig("squarex_added")
        hidden_hi_ready = sig("hidden_hi_ready")
        pT_hi_ready, pT_lo_ready = sig("pT_hi_ready"), sig("pT_lo_ready")
        tile_done = sig("tile_done")
        pair_read = sig("pair_read")
        mix_read = sig("mix_read")
        turned = sig("turned")
        turned_read = sig("turned_read")
        setup_done = sig("setup_done")
        bounds_exp = sig("bounds_exp")
        x_ready = sig("x_ready")
        u_ready = sig("u_ready")
        gain_ready = sig("gain_ready")
        msx_ready = sig("msx_ready")
        invx_ready, r_pre_ready = sig("invx_ready"), sig("r_pre_ready")
        square_ready, square_added, ms_ready = sig("square_ready"), sig("square_added"), sig("ms_ready")
        inv_ready, r_post_ready = sig("inv_ready"), sig("r_post_ready")
        gate_scaled, gate_acted, hidden_ready = sig("gate_scaled"), sig("gate_acted"), sig("hidden_ready")
        ple_y_ready = sig("ple_y_ready")
        auxd_done, auxd_read = sig("auxd_done"), sig("auxd_read")
        auxa_done, auxa_read = sig("auxa_done"), sig("auxa_read")
        big_done = sig("big_done")
        big_read_act, big_read_dve = sig("big_read_act"), sig("big_read_dve")
        scored = sig("scored")
        roped = sig("roped")
        relu_ready = sig("relu_ready")
        iw_ready = sig("iw_ready")
        hg_exp, hg_dve = sig("hg_exp"), sig("hg_dve")
        diff_ready, decay_ready, scaled_ready = sig("diff_ready"), sig("decay_ready"), sig("scaled_ready")
        att_ready = sig("att_ready")
        v_own_ready = sig("v_own_ready")
        o_ready, inv_o_ready, r_o_ready = sig("o_ready"), sig("inv_o_ready"), sig("r_o_ready")
        state_decayed, states_done = sig("state_decayed"), sig("states_done")
        masked, exped, normed = sig("masked"), sig("exped"), sig("normed")
        attended = sig("attended")
        stored = sig("stored")
        y_stored = sig("y_stored")
        final_turned, final_copied = sig("final_turned"), sig("final_copied")
        passed = sig("passed")
        dve_steps, act_steps, pool_steps = sig("dve_steps"), sig("act_steps"), sig("pool_steps")

        block = ctx.enter_context(nc.Block())
        N_CONST = 1

        def apart(eng):
            eng.sem_inc(passed.sem, 1)


        def mix_bank_of(n):
            return 2 + n if n in (2, 3) else n % 2

        def ple_bank(j):
            return 2 * (j % 3)

        Y_BY_DVE = 3
        ADDS = KT - 2

        def sums_before(j):
            return max(1, j - 4)

        class Chain:

            def __init__(self, eng, s):
                self.eng, self.sig, self.layer, self.n = eng, s, None, 0

            def enter(self, layer):
                self.layer, self.n = layer, 0

            def add(self, ins):
                ins.then_inc(*once(self.sig))
                self.n += 1

            def settle(self, but=0):
                if self.layer is None:
                    self.eng.wait_ge(self.sig.sem, self.n)
                else:
                    self.eng.wait_ge(self.sig.sem, self.sig.at(self.layer, self.n - but))
                    apart(self.eng)

            def __call__(self, ins):
                self.add(ins)
                self.settle()

        @block.sync
        def _(sp):
            counts.in_layer = 0
            def load(L, n, parts, i=None):
                before = n - 2 if i is None else n
                if LOADS[before][0] in SPLIT_KINDS:
                    v = slot_lo_ready.at(L, splits_before(before) + 1 if before >= 0 else before + 1)
                    sp.wait_ge(slot_lo_ready.sem, v if i is None else v + (i * 2 - 2))
                else:
                    sp.wait_ge(tile_done.sem, tile_done.at(L, TILES_BEFORE[n - 1]))
                apart(sp)
                for dst, src in parts:
                    sp.dma_start(dst, src).then_inc(*dma(slot_in[n % 2]))

            def w(name, L):
                return A[name][bass.ds(L, 1)]

            def cols(name, L, at, n, kt=KT):
                return w(name, L)[:, :, at:at + n].rearrange("a (k p) n -> p (a k) n", p=P)

            def ffn(L, which):
                g, up, down = f"w_f{which}_gate", f"w_f{which}_up", f"w_f{which}_down"
                n0 = LOAD_AT[f"gateup{which}", 0]

                def gateup(half, at, i=None):
                    n = n0 + half
                    s = slots[n % 2][:, 0:2 * KT * P].rearrange("p (a k n) -> p a k n", a=2, k=KT)
                    load(L, n, [
                        (s[:, a], w(name, L)[:, :, at].rearrange("a (k p) n -> p (a k) n", p=P))
                        for a, name in enumerate((g, up))], i)

                for half in range(2):
                    gateup(half, slice(half * P, half * P + P))
                counts.times = FT // 2 - 1
                with sp.Fori(1, FT // 2) as i:
                    for half in range(2):
                        gateup(half, bass.ds(i * (2 * P) + half * P, P), i)
                n0 = LOAD_AT[f"down{which}", 0]
                counts.times = KT // 2
                with sp.Fori(0, KT // 2) as i:
                    for half in range(2):
                        n = n0 + half
                        s = slots[n % 2][:, :].rearrange("p (f n) -> p f n", f=FT)
                        at = bass.ds(i * (2 * P) + half * P, P)
                        load(L, n, [(s, w(down, L)[:, :, at].rearrange("a (f p) n -> p (a f) n", p=P))],
                             i)
                counts.times = 1

            sp.dma_start(tokens[:, 0:2, :], A["x_prompt"].rearrange("a (t p) d -> p (a t) d", p=P)
                         ).then_inc(*dma(tokens_in))
            sp.dma_start(tokens[0:TS, 2, :], A["x_sample"].rearrange("b t d -> (b t) d")
                         ).then_inc(*dma(tokens_in))
            sp.dma_start(early_table[:, :], A["early"]).then_inc(*dma(early_in))
            sp.dma_start(rows_a[:, :], A["rows_a"]).then_inc(*dma(early_in))
            sp.dma_start(rows_b[:, :], A["rows_b"]).then_inc(*dma(early_in))
            counts.in_layer = 1
            with sp.Fori(0, LAYERS) as L:
                ffn(L, 1)
                def mix_load(kind, i, parts):
                    load(L, LOAD_AT[kind, i], parts)

                def slot_of(kind, i, width):
                    return slots[LOAD_AT[kind, i] % 2][:, 0:KT * width].rearrange("p (k n) -> p k n", k=KT)

                def head_pairs(kind, at):
                    for i in range(2):
                        dst = slot_of(kind, i, 256).rearrange("p k (j g n) -> p j g k n", j=2, g=2)
                        mix_load(kind, i, [
                            (dst[:, j, g], cols("w_in", L, at + g * 256 + (2 * i + j) * HD, HD))
                            for j in range(2) for g in range(2)])

                head_pairs("iq", C_IQ)
                pages = [sp.value_load(A["page_table"][b:b + 1, n:n + 1], min_val=0, max_val=pool_pages - 1)
                         for b in range(SEQS) for n in range(NPAGES)]
                sp.wait_ge(x_ready.sem, x_ready.at(L, KT))
                apart(sp)
                pool_k = w("cache_k", L).rearrange("a n t h d -> (a n) t (h d)")
                pool_v = w("cache_v", L).rearrange("a n t h d -> (a n) t (h d)")
                pool_i = w("cache_idx_k", L).rearrange("a n t d -> (a n) t d")
                sp.dma_start(p_tok[:, 0:2, :], w("p_prompt", L).rearrange("l a (t p) d -> p (l a t) d", p=P)
                             ).then_inc(*dma(embeddings_in))
                sp.dma_start(p_tok[0:TS, 2, :], w("p_sample", L).rearrange("l b t d -> (l b t) d")
                             ).then_inc(*dma(embeddings_in))

                for n in range(16):
                    sp.dma_start(k_pages[:, n, :], pool_k[bass.ds(pages[n], 1)].rearrange("a t d -> t (a d)")
                                 ).then_inc(*dma(caches_in))
                mix_load("kv", 0, [(slot_of("kv", 0, 256), cols("w_in", L, C_K, 256))])
                for n in range(16):
                    for twice in range(2):
                        sp.dma_start(i_pages[:, n, twice, :],
                                     pool_i[bass.ds(pages[n], 1)].rearrange("a t d -> t (a d)")
                                     ).then_inc(*dma(caches_in))
                mix_load("ikiw", 0, [(slot_of("ikiw", 0, 72), cols("w_in", L, C_IK, 72))])
                for kind, at in (("hf", C_HF), ("hq", C_HQ)):
                    for i in range(2):
                        mix_load(kind, i, [(slot_of(kind, i, 256), cols("w_in", L, at + 256 * i, 256))])
                head_pairs("q", C_Q)
                for n in range(16):
                    sp.dma_start(v_pages[:, n, :], pool_v[bass.ds(pages[n], 1)].rearrange("a t d -> t (a d)")
                                 ).then_inc(*dma(states_in))
                st = w("state_hgrn", L).rearrange("l b h d e -> d (l b) h e")
                for b in range(0, SEQS, 2):
                    sp.dma_start(state[:, b:b + 2], st[:, b:b + 2]).then_inc(*dma(states_in))
                for kind, at in (("hi", C_HI), ("hgate", C_HG)):
                    for i in range(2):
                        mix_load(kind, i, [(slot_of(kind, i, 256), cols("w_in", L, at + 256 * i, 256))])
                wo = w("w_out", L)
                for i in range(4):
                    dst = slot_of("out", i, 256)
                    c = slice(256 * i, 256 * i + 256)
                    mix_load("out", i, [
                        (dst[0:64, 0:4], wo[:, 0:256, c].rearrange("a (j d) n -> d (a j) n", d=HD)),
                        (dst[64:128, 0:4], wo[:, 256:512, c].rearrange("a (j d) n -> d (a j) n", d=HD)),
                        (dst[:, 4:8], wo[:, 512:1024, c].rearrange("a (h e) n -> e (a h) n", e=P))])
                ffn(L, 2)
                for i in range(4):
                    s = slots[LOAD_AT["ple", i] % 2][:, 0:(KT + 2) * 256].rearrange("p (k n) -> p k n", k=KT + 2)
                    mix_load("ple", i, [(s[:, 0:KT], cols("w_ple_gate", L, 256 * i, 256)),
                                        (s[:, KT:], cols("w_ple_proj", L, 256 * i, 256))])
            counts.in_layer = 2
            sp.wait_ge(final_copied.sem, 6)
            yt = tokens
            sp.dma_start(O["y_prompt"].rearrange("a (t p) d -> p (a t) d", p=P), yt[:, 0:2, :]
                         ).then_inc(*dma(y_stored))
            sp.dma_start(O["y_sample"].rearrange("b t d -> (b t) d"), yt[0:TS, 2, :]
                         ).then_inc(*dma(y_stored))
            sp.wait_ge(y_stored.sem, 32)
            sp.wait_ge(stored.sem, stored.at(LAYERS - 1, 16 * 8))

        @block.gpsimd
        def _(pool):
            counts.in_layer = 0
            ch = Chain(pool, pool_steps)
            ch(pool.memset(kv_tok[:, :, :], 0.0))
            ch(pool.memset(ik_tok[:, :, :], 0.0))
            pool.wait_ge(constants_in.sem, 16 * N_CONST)

            def squares_of_x(L, stage):
                pool.wait_ge(ms_ready.sem, ms_ready.at(L, stage))
                apart(pool)
                add_squares(L, stage, squarex_ready, squarex_added, sumsq, ADDS)

            def add_squares(L, stage, ready, added, total, adds):
                for j in range(1, adds + 1):
                    pool.wait_ge(ready.sem, ready.at(L, stage * KT + j + 1))
                    apart(pool)
                    if j > 1:
                        pool.wait_ge(added.sem, added.at(L, stage * adds + j - 1))
                        apart(pool)
                    first = sq[:, 0, :] if j == 1 else total[:, :]
                    pool.tensor_tensor(total[:, :], first, sq[:, j % 4, :], ALU.add).then_inc(*once(added))

            def scale_y(L, stage):
                pool.wait_ge(r_post_ready.sem, r_post_ready.at(L, stage + 1))
                apart(pool)
                for j in range(Y_BY_DVE, KT):
                    pool.tensor_tensor(y[:, j, :], y[:, j, :], r_post[:, :], ALU.mult
                                       ).then_inc(*once(y_scaled))

            def hidden_rest(L, which):
                m = FT * (which - 1)
                counts.times = FT // 2
                with pool.Fori(0, FT // 2) as i:
                    for half in range(2):
                        pool.wait_ge(gate_acted.sem, gate_acted.at(L, m + half + 1) + i * 2)
                        apart(pool)
                        pool.wait_ge(pair_read.sem, pair_read.at(L, m + half + 1) + i * 2)
                        apart(pool)
                        ch.add(pool.tensor_tensor(hidden_tmp[:, half, :], gate_out[:, half, :],
                                                  up_out[:, half, :], ALU.mult))
                        pool.wait_ge(hidden_hi_ready.sem, hidden_hi_ready.at(L, m + half + 1) + i * 2)
                        apart(pool)
                        pool.wait_ge(pool_steps.sem, pool_steps.at(L, ch.n) + i * 2)
                        apart(pool)
                        at = bass.ds(i * 2 + half, 1)
                        pool.tensor_tensor(hidden_lo[:, at, :].rearrange("p a t -> p (a t)"),
                                           hidden_tmp[:, half, :],
                                           hidden_hi[:, at, :].bitcast(F32).rearrange("p a t -> p (a t)"),
                                           ALU.subtract).then_inc(*once(hidden_ready))
                counts.times = 1
                ch.n += 2 * (FT // 2 - 1)

            def squares_of_y(L, stage):
                pool.wait_ge(msx_ready.sem, msx_ready.at(L, stage + 1))
                apart(pool)
                add_squares(L, stage, square_ready, square_added, sumsq, ADDS)

            def rope_tokens(tile, dst_heads, heads):
                v = tile.rearrange("p t (h two c) -> p t h two c", h=heads, two=2)
                a, b = v[:, :, :, 0, :], v[:, :, :, 1, :]
                n = 3 * heads * 32
                tmp = [rope_tok[:, i, 0:n].rearrange("p (t h c) -> p t h c", t=3, h=heads) for i in range(4)]
                for h in range(heads):
                    pool_ops = ((0, a, cos_t), (1, b, sin_t), (2, b, cos_t), (3, a, sin_t))
                    for i, src, tab in pool_ops:
                        ch.add(pool.tensor_tensor(tmp[i][:, :, h, :], src[:, :, h, :], tab[:, :, :], ALU.mult))
                ch.settle()
                for h in range(heads):
                    ch.add(pool.tensor_tensor(a[:, :, h, :], tmp[0][:, :, h, :], tmp[1][:, :, h, :], ALU.subtract))
                    ch.add(pool.tensor_tensor(b[:, :, h, :], tmp[2][:, :, h, :], tmp[3][:, :, h, :], ALU.add))
                ch.settle()

            def store(L, dst, src, rearrange):
                pool.dma_start(dst, src).then_inc(*dma(stored))

            counts.in_layer = 1
            with pool.Fori(0, LAYERS) as L:
                ch.enter(L)
                squares_of_x(L, 0)
                hidden_rest(L, 1)
                squares_of_y(L, 0)
                pool.wait_ge(late_in.sem, 16)
                scale_y(L, 0)
                squares_of_x(L, 1)
                pool.wait_ge(mix_read.sem, mix_read.at(L, MIX_LAST["kv"]))
                apart(pool)
                rope_tokens(kv_tok[:, :, 0:128], None, 2)
                pool.wait_ge(mix_read.sem, mix_read.at(L, MIX_LAST["ikiw"]))
                apart(pool)
                rope_tokens(ik_tok[:, :, 0:64], None, 1)
                pool.tensor_copy(ik_tok[:, :, 64:128], ik_tok[:, :, 0:64]).then_inc(*once(roped))
                pool.wait_ge(roped.sem, roped.at(L, 1))
                apart(pool)
                for name, src in (("k", kv_tok[:, :, 0:128]), ("v", kv_tok[:, :, 128:256]),
                                  ("idx_k", ik_tok[:, :, 0:64])):
                    d = O[f"{name}_prompt"][bass.ds(L, 1)]
                    e = O[f"{name}_sample"][bass.ds(L, 1)]
                    if name == "idx_k":
                        d = d.rearrange("l a (t p) d -> p (l a t) d", p=P)
                        e = e.rearrange("l b t d -> (l b t) d")
                    else:
                        d = d.rearrange("l a (t p) h d -> p (l a t) (h d)", p=P)
                        e = e.rearrange("l b t h d -> (l b t) (h d)")
                    pool.dma_start(d, src[:, 0:2]).then_inc(*dma(stored))
                    pool.dma_start(e, src[0:TS, 2]).then_inc(*dma(stored))
                pool.wait_ge(hg_dve.sem, hg_dve.at(L, HGD["scan"]))
                apart(pool)
                for n, h in enumerate(LEVELS):
                    if n >= 2:
                        pool.wait_ge(scaled_ready.sem, scaled_ready.at(L, n - 1))
                        apart(pool)
                    src, dst = level_view(hb, h), level_view(decay[n % 2], h)
                    ref = src[0][:, :, h - 1:h] if 2 * h <= STEP else src[0][:, :, :, h - 1:h]
                    ref = ref.to_broadcast(list(src[1].shape))
                    pool.tensor_tensor(dst[1], src[1], ref, ALU.subtract)
                    pool.tensor_tensor(dst[0], ref, src[0], ALU.subtract).then_inc(*once(diff_ready))
                n = len(LEVELS)
                pool.wait_ge(scaled_ready.sem, scaled_ready.at(L, n))
                apart(pool)
                for a, b in (((0, TP), CHUNK), ((TP, T), STEP)):
                    for hh in range(HG):
                        v = hb[:, hh, a[0]:a[1]].rearrange("p (c s) -> p c s", s=b)
                        d = decay[1][:, hh, a[0]:a[1]].rearrange("p (c s) -> p c s", s=b)
                        ins = pool.tensor_tensor(d, v[:, :, b - 1:b].to_broadcast(list(v.shape)), v, ALU.subtract)
                ins.then_inc(*once(diff_ready))
                pool.wait_ge(mix_read.sem, mix_read.at(L, MIX_LAST["hi"]))
                apart(pool)
                def own_values(h):
                    vv = v_tok[0:TS, 2, h * P:(h + 1) * P].rearrange("p (a e) -> p a e", a=1)
                    oo = own_seq[:, :].rearrange("p (b a) -> p b a", a=1)
                    pool.tensor_tensor(v_own[:, h % 2], vv.to_broadcast([TS, SEQS, P]),
                                       oo.to_broadcast([TS, SEQS, P]), ALU.mult).then_inc(*once(v_own_ready))

                pool.wait_ge(auxa_done.sem, auxa_done.at(L, AUXA["ipages3"] + 1))
                apart(pool)
                own_values(0)
                own_values(1)
                for h in range(HG):
                    pool.wait_ge(auxa_done.sem, auxa_done.at(L, AUXA[f"o{h}"] + 1))
                    apart(pool)
                    last = decay[0][:, h, TP + STEP - 1::STEP].rearrange("p (b a) -> p b a", a=1)
                    pool.tensor_tensor(state[:, :, h, :], state[:, :, h, :], last.to_broadcast([P, SEQS, P]),
                                       ALU.mult).then_inc(*once(state_decayed))
                for h in (2, 3):
                    pool.wait_ge(auxd_done.sem, auxd_done.at(L, AUXD[f"state_s{h - 2}b"] + 1))
                    apart(pool)
                    own_values(h)
                pool.wait_ge(states_done.sem, states_done.at(L, 1))
                apart(pool)
                pool.dma_start(O["hgrn_prompt"][bass.ds(L, 1)].rearrange("l a h d e -> d (l a h) e"),
                               s_end[:, :, :]).then_inc(*dma(stored))
                pool.wait_ge(states_done.sem, states_done.at(L, 2))
                apart(pool)
                pool.dma_start(O["hgrn_sample"][bass.ds(L, 1)].rearrange("l b h d e -> d (l b h) e"),
                               state[:, :, :, :].rearrange("p b h e -> p (b h) e")).then_inc(*dma(stored))
                squares_of_y(L, 1)
                scale_y(L, 1)
                squares_of_x(L, 2)
                hidden_rest(L, 2)
                squares_of_y(L, 2)
                scale_y(L, 2)
                squares_of_x(L, 3)
                squares_of_y(L, 3)
                scale_y(L, 3)
            counts.in_layer = 2

        @block.scalar
        def _(act):
            counts.in_layer = 0
            ch = Chain(act, act_steps)
            act.wait_ge(tokens_in.sem, 32)
            act.dma_start(masks_in[:, :, :], A["level_masks"].rearrange("p (a b) -> p a b", a=len(LEVELS))
                          ).then_inc(*dma(constants_in))
            act.wait_ge(bounds_exp.sem, 1)
            act.activation(bounds_tmp[:, 1, :], bounds_tmp[:, 1, :], ACT.Exp)
            act.activation(bounds_tmp[:, 2, :], bounds_tmp[:, 2, :], ACT.Exp).then_inc(*once(bounds_exp))
            act.wait_ge(slot_in[0].sem, 32)
            act.dma_start(late_table[:, :], A["late"]).then_inc(*dma(late_in))
            act.wait_ge(constants_in.sem, 16 * N_CONST)

            def make_u(L, stage, norm):
                dst = u if stage == 1 else u_hi
                for j in range(KT):
                    act.wait_ge(x_ready.sem, x_ready.at(L, stage * KT + j + 1 - KT))
                    apart(act)
                    if j == 0:
                        act.wait_ge(gain_ready.sem, gain_ready.at(L, 1))
                        apart(act)
                    act.activation(dst[:, j, :], x[:, j, :], ACT.Copy, scale=gain[:, norm, j:j + 1]
                                   ).then_inc(*once(u_ready))
                    if j >= 4:
                        act.wait_ge(squarex_added.sem, squarex_added.at(L, stage * ADDS + sums_before(j)))
                        apart(act)
                    act.activation(sq[:, j % 4, :], x[:, j, :], ACT.Square).then_inc(*once(squarex_ready))

            def split_hi(L, n, i=None):
                size = split_size(n)
                full = slot_in[n % 2]
                value = full.at(L, dma_count_before(n) + 16 * DMAS(n))
                act.wait_ge(full.sem, value if i is None else value + i * (16 * DMAS(n)))
                apart(act)
                act.activation(parts_of(n)[0], slots[n % 2][:, 0:size], ACT.Copy
                               ).then_inc(*once(slot_hi_ready))

            def root(L, n, ready, inv, dst, out):
                act.wait_ge(ready.sem, ready.at(L, n))
                act.activation(dst, inv, ACT.Sqrt).then_inc(*once(out))

            def tiles_out(L, kind, stage):
                per = dict(down1=1, out=2, down2=1)[kind]
                for j in range(KT):
                    act.wait_ge(tile_done.sem, tile_done.at(L, tile_at(kind, j // per, j % per) + 1))
                    apart(act)
                    if kind != "out" and j + 2 < KT or kind == "down2" and j + 2 == KT:
                        split_hi(L, LOAD_AT[kind, j] + 2)
                    if j >= 4:
                        act.wait_ge(square_added.sem, square_added.at(L, stage * ADDS + sums_before(j)))
                        apart(act)
                    if j < KT - 1:
                        act.activation(y[:, j, :], ps[:, 4 + j % 2, 0:T], ACT.Copy)
                    act.activation(sq[:, j % 4, :], ps[:, 4 + j % 2, 0:T], ACT.Square
                                   ).then_inc(*once(square_ready))
                    if kind == "out" and j in (1, 3):
                        split_hi(L, LOAD_AT["out", j // 2 + 2])
                    if kind == "out" and j == KT - 2:
                        split_hi(L, LOAD_AT["gateup2", 0])
                    if j == KT - 1:
                        act.activation(y[:, j, :], ps[:, 4 + j % 2, 0:T], ACT.Copy)

            def ple_square(L, j):
                act.wait_ge(pair_read.sem, pair_read.at(L, 2 * FT + j + 1))
                apart(act)
                if j >= 4:
                    act.wait_ge(square_added.sem, square_added.at(L, 3 * ADDS + sums_before(j)))
                act.activation(sq[:, j % 4, :], y[:, j, :], ACT.Square).then_inc(*once(square_ready))

            def soft(L, t):
                keys = 256 if t else 128
                act.wait_ge(masked.sem, masked.at(L, SOFT[t]))
                apart(act)
                for h in range(NH):
                    ins = act.activation(probs[t][:, h, 0:keys], probs[t][:, h, 0:keys], ACT.Exp,
                                         bias=peak[:, t, h:h + 1], scale=HD ** -0.5,
                                         accum_out=total[:, t, h:h + 1])
                ins.then_inc(*once(exped))

            def ffn(L, which):
                m = FT * (which - 1)
                n0 = LOAD_AT[f"gateup{which}", 0]
                t0 = tile_at(f"gateup{which}", 0)

                def split_next(n, i=None):
                    v = tile_done.at(L, t0 + n + 1)
                    act.wait_ge(tile_done.sem, v if i is None else v + i * 2)
                    apart(act)
                    split_hi(L, n0 + n + 2, i)

                def gate(n, i=None):
                    v = gate_scaled.at(L, m + n + 1)
                    act.wait_ge(gate_scaled.sem, v if i is None else v + i * 2)
                    act.activation(gate_out[:, n % 2, :], gate_in[:, n % 2, :], ACT.Silu
                                   ).then_inc(*once(gate_acted))

                split_next(0)
                s = 1 if which == 1 else 3
                root(L, s, invx_ready, inv_pre[:, :], r_pre[:, :], r_pre_ready)
                gate(0)
                split_next(1)
                gate(1)
                counts.times = FT // 2 - 2
                with act.Fori(1, FT // 2 - 1) as i:
                    for n in range(2):
                        split_next(n, i)
                        gate(n, i)
                counts.times = 1
                for n in (FT - 2, FT - 1):
                    split_next(n)
                    gate(n)

            def auxa(L, name, dst, src, func=ACT.Copy, done=None):
                k = AUXA[name]
                act.wait_ge(auxa_done.sem, auxa_done.at(L, k + 1))
                apart(act)
                act.activation(dst, src(ps[:, (3, 6)[k % 2], :]), func).then_inc(*once(auxa_read))

            counts.in_layer = 1
            with act.Fori(0, LAYERS) as L:
                ch.enter(L)
                split_hi(L, 0)
                make_u(L, 0, 0)
                split_hi(L, 1)
                ffn(L, 1)
                tiles_out(L, "down1", 0)
                root(L, 1, inv_ready, inv_post[:, :], r_post[:, :], r_post_ready)
                make_u(L, 1, 2)
                root(L, 2, invx_ready, inv_pre[:, :], r_pre[:, :], r_pre_ready)
                for k in range(2):
                    auxa(L, f"p{k}", pT[:, k, :], lambda b: b[:, 0:T])
                act.wait_ge(auxa_read.sem, auxa_read.at(L, AUXA["p1"] + 1))
                apart(act)
                act.activation(pT_hi[:, :, :], pT[:, :, :], ACT.Copy).then_inc(*once(pT_hi_ready))
                for k in range(4):
                    auxa(L, f"kpages{k}", kT_past[:, 4 * k:4 * k + 4, :],
                         lambda b: b.rearrange("p (n t) -> p n t", n=4))
                for k in range(4):
                    auxa(L, f"ipages{k}", ikT_past[:, 4 * k:4 * k + 4, :],
                         lambda b: b.rearrange("p (n t) -> p n t", n=4))
                act.wait_ge(mix_read.sem, mix_read.at(L, MIX_LAST["hf"]))
                act.activation(hb[:, :, :], hk[:, :, :], ACT.Sigmoid).then_inc(*once(hg_exp))
                auxa(L, "kT", kT[:, :], lambda b: b[:, 0:T])
                auxa(L, "ikT", ikT[:, :], lambda b: b[:, 0:T])
                act.wait_ge(mix_read.sem, mix_read.at(L, MIX_LAST["hq"]))
                act.activation(scaled[1][:, :, :], hq[:, :, :], ACT.Silu).then_inc(*once(hg_exp))
                for n in range(4):
                    g, j = n % 2, n // 2 * 2
                    act.wait_ge(big_done.sem, big_done.at(L, BIG["idx"] + n + 1))
                    apart(act)
                    act.activation(relu_p[:, 4 * g + j:4 * g + j + 2, :],
                                   ps[:, 4 + n % 2, :].rearrange("p (h k) -> p h k", h=2),
                                   ACT.Relu, scale=HD ** -0.5).then_inc(*once(big_read_act))
                act.wait_ge(scored.sem, scored.at(L, EV["score1"]))
                for n in range(2):
                    act.wait_ge(big_done.sem, big_done.at(L, BIG["idx"] + 5 + n))
                    apart(act)
                    act.activation(relu_p[:, 4 * n:4 * n + 4, 0:128],
                                   ps[:, 4 + n % 2, :].rearrange("p (h k) -> p h k", h=4),
                                   ACT.Relu, scale=HD ** -0.5).then_inc(*once(big_read_act))
                for n in range(4):
                    act.wait_ge(big_done.sem, big_done.at(L, BIG["idx"] + 7 + n))
                    apart(act)
                    act.activation(relu_s[:, n, :], ps[:, 4 + n % 2, 0:KEYS_S],
                                   ACT.Relu, scale=HD ** -0.5).then_inc(*once(big_read_act))
                act.wait_ge(hg_dve.sem, hg_dve.at(L, HGD["f"]))
                apart(act)
                act.wait_ge(scored.sem, scored.at(L, EV["score0"]))
                act.activation(decay[0][:, :, :], hb[:, :, :], ACT.Ln).then_inc(*once(hg_exp))
                act.wait_ge(auxd_done.sem, auxd_done.at(L, AUXD["score_s"] + 1))
                apart(act)
                for n, h in enumerate(LEVELS):
                    act.wait_ge(diff_ready.sem, diff_ready.at(L, n + 1))
                    c = T if 2 * h <= STEP else TP
                    act.activation(decay[n % 2][:, :, 0:c], decay[n % 2][:, :, 0:c], ACT.Exp
                                   ).then_inc(*once(decay_ready))
                n = len(LEVELS)
                act.wait_ge(scaled_ready.sem, scaled_ready.at(L, n))
                act.activation(decay[0][:, :, :], hb[:, :, :], ACT.Exp).then_inc(*once(decay_ready))
                act.wait_ge(diff_ready.sem, diff_ready.at(L, n + 1))
                act.activation(decay[1][:, :, :], decay[1][:, :, :], ACT.Exp).then_inc(*once(decay_ready))
                for n in range(3):
                    m = TOK_TILES[n][1]
                    auxa(L, f"key{n}", key_tok[0:m, n, :, :],
                         lambda b, m=m: b[0:m, :].rearrange("p (h d) -> p h d", h=HG))
                for h in range(HG):
                    k = AUXA[f"o{h}"]
                    act.wait_ge(auxa_done.sem, auxa_done.at(L, k + 1))
                    apart(act)
                    bank = ps[:, (3, 6)[k % 2], 0:T]
                    ch.add(act.activation(o_hg[:, h, :], bank, ACT.Copy))
                    act.activation(scaled[1][:, h, :], bank, ACT.Square).then_inc(*once(auxa_read))
                act.wait_ge(inv_o_ready.sem, inv_o_ready.at(L, 1))
                act.activation(decay[1][:, 0, :], decay[1][:, 0, :], ACT.Sqrt).then_inc(*once(r_o_ready))
                soft(L, 1)
                act.wait_ge(masked.sem, masked.at(L, SOFT["samples"]))
                apart(act)
                for pair in range(4):
                    ins = act.activation(probs_s[:, pair, :], probs_s[:, pair, :], ACT.Exp,
                                         bias=peak[:, 2, pair:pair + 1], scale=HD ** -0.5,
                                         accum_out=total[:, 2, pair:pair + 1])
                ins.then_inc(*once(exped))
                soft(L, 0)
                for k in range(2):
                    for g in range(2):
                        auxa(L, f"pT1_{k}{g}", probsT[1][:, k, 4 * g:4 * g + 4, :],
                             lambda b: b.rearrange("p (h t) -> p h t", h=4))
                act.wait_ge(mix_read.sem, mix_read.at(L, MIX_LAST["hgate"]))
                act.activation(hgate[:, :, :], hgate[:, :, :], ACT.Silu).then_inc(*once(hg_exp))
                for k in range(3):
                    m = TOK_TILES[k][1]
                    auxa(L, f"pTs{k}", probsT_s[0:m, k, :, :],
                         lambda b, m=m: b[0:m, :].rearrange("p (n t) -> p n t", n=4))
                for g in range(2):
                    auxa(L, f"pT0_0{g}", probsT[0][:, 0, 4 * g:4 * g + 4, :],
                         lambda b: b.rearrange("p (h t) -> p h t", h=4))
                act.wait_ge(auxd_done.sem, auxd_done.at(L, AUXD["pv1"] + 1))
                apart(act)
                split_hi(L, LOAD_AT["out", 0])
                act.wait_ge(stored.sem, stored.at(L, 16 * 8))
                apart(act)
                split_hi(L, LOAD_AT["out", 1])
                tiles_out(L, "out", 1)
                root(L, 2, inv_ready, inv_post[:, :], r_post[:, :], r_post_ready)
                make_u(L, 2, 4)
                split_hi(L, LOAD_AT["gateup2", 1])
                ffn(L, 2)
                tiles_out(L, "down2", 2)
                root(L, 3, inv_ready, inv_post[:, :], r_post[:, :], r_post_ready)
                make_u(L, 3, 6)
                split_hi(L, LOAD_AT["ple", 1])
                root(L, 4, invx_ready, inv_pre[:, :], r_pre[:, :], r_pre_ready)
                for j in range(KT):
                    act.wait_ge(gate_scaled.sem, gate_scaled.at(L, 2 * FT + j + 1))
                    act.activation(gate_out[:, j % 2, :], gate_in[:, j % 2, :], ACT.Sigmoid
                                   ).then_inc(*once(gate_acted))
                    if j in (1, 3):
                        split_hi(L, LOAD_AT["ple", j // 2 + 2])
                    if j:
                        ple_square(L, j - 1)
                ple_square(L, KT - 1)
                root(L, 4, inv_ready, inv_post[:, :], r_post[:, :], r_post_ready)
            counts.in_layer = 2

        @block.vector
        def _(dve):
            counts.in_layer = 0
            ch = Chain(dve, dve_steps)
            for s in (tile_done, slot_lo_ready):
                dve.sem_inc(*counts.inc(s, 2))
            for k in range(KT):
                dve.wait_ge(turned.sem, k + 1)
                dve.tensor_copy(x[:, k, :], ps[:, k, 0:T]).then_inc(*once(turned_read))
            dve.wait_ge(turned.sem, KT + 1)
            dve.tensor_copy(gains[:, :, :, :].rearrange("p a l k -> p (a l k)"), ps[:, 0, 320:448]
                            ).then_inc(*once(turned_read))
            dve.wait_ge(turned.sem, KT + 2)
            dve.tensor_copy(small[:, :], ps[:, 1, 320:330]).then_inc(*once(turned_read))
            dve.wait_ge(turned_read.sem, KT + 2)
            for a in (1, 5):
                ch(dve.tensor_scalar(gains[:, a], gains[:, a], 0.5, None, ALU.mult))
            lg = small[:, 0:8].rearrange("p (l h) -> p l h", l=LAYERS)
            ch(dve.tensor_tensor(bounds_tmp[:, 0, :], lg[:, 0], lg[:, 1], ALU.max))
            ch(dve.tensor_tensor(bounds_tmp[:, 1, :], lg[:, 0], bounds_tmp[:, 0, :], ALU.subtract))
            dve.tensor_tensor(bounds_tmp[:, 2, :], lg[:, 1], bounds_tmp[:, 0, :], ALU.subtract
                              ).then_inc(*once(bounds_exp))
            dve.wait_ge(bounds_exp.sem, 2)
            ch(dve.tensor_tensor(bounds_tmp[:, 3, :], bounds_tmp[:, 1, :], bounds_tmp[:, 2, :], ALU.add))
            ch(dve.reciprocal(bounds_tmp[:, 4, :], bounds_tmp[:, 3, :]))
            for a in (1, 2):
                ch(dve.tensor_tensor(bounds_tmp[:, a, :], bounds_tmp[:, a, :], bounds_tmp[:, 4, :], ALU.mult))
            ch(dve.tensor_tensor(bounds_tmp[:, 3, :], bounds_tmp[:, 1, :], bounds_tmp[:, 2, :], ALU.add))
            ch(dve.tensor_tensor(bounds[:, 0, :], bounds_tmp[:, 1, :], bounds_tmp[:, 1, :], ALU.subtract))
            ch(dve.tensor_tensor(bounds[:, 1, :], bounds_tmp[:, 3, :], bounds_tmp[:, 1, :], ALU.subtract))
            for s in (pair_read, mix_read, square_ready, hidden_ready,
                      auxd_read, auxa_read):
                dve.sem_inc(*counts.inc(s, 2))
            for s in (msx_ready, ms_ready):
                dve.sem_inc(*once(s))
            dve.sem_inc(*counts.inc(x_ready, KT))
            dve.wait_ge(constants_in.sem, 16 * N_CONST)
            ch(dve.tensor_copy(level_masks[:, :, :], masks_in[:, :, :]))
            dve.sem_inc(*once(setup_done))

            def norm_in(L, stage):
                dve.wait_ge(msx_ready.sem, msx_ready.at(L, stage + 1))
                ch(dve.tensor_scalar(inv_pre[:, :], ps[:, 7, 0:T], EPS, None, ALU.add))
                dve.reciprocal(inv_pre[:, :], inv_pre[:, :]).then_inc(*once(invx_ready))

            def split_lo(L, n, i=None):
                size = split_size(n)
                v = slot_hi_ready.at(L, splits_before(n) + 1)
                dve.wait_ge(slot_hi_ready.sem, v if i is None else v + i * 2)
                apart(dve)
                hi, lo = parts_of(n)
                dve.tensor_tensor(lo, slots[n % 2][:, 0:size], hi.bitcast(F32), ALU.subtract
                                  ).then_inc(*once(slot_lo_ready))

            def rest_of_u(L, stage, norm, j):
                dve.wait_ge(u_ready.sem, u_ready.at(L, stage * KT + j + 1))
                apart(dve)
                dve.scalar_tensor_tensor(out=u_lo[:, j, :], in0=x[:, j, :], scalar=gain[:, norm, j:j + 1],
                                         in1=u_hi[:, j, :].bitcast(F32), op0=ALU.mult, op1=ALU.subtract
                                         ).then_inc(*once(u_lo_ready))

            def norm_out(L, stage, norm, u_norm=None):
                dve.wait_ge(ms_ready.sem, ms_ready.at(L, stage + 1))
                ch(dve.tensor_scalar(inv_post[:, :], ps[:, 6, 0:T], EPS, None, ALU.add))
                dve.reciprocal(inv_post[:, :], inv_post[:, :]).then_inc(*once(inv_ready))
                dve.wait_ge(r_post_ready.sem, r_post_ready.at(L, stage + 1))
                apart(dve)

                def add(j):
                    dve.scalar_tensor_tensor(out=x[:, j, :], in0=y[:, j, :], scalar=gain[:, norm, j:j + 1],
                                             in1=x[:, j, :], op0=ALU.mult, op1=ALU.add
                                             ).then_inc(*once(x_ready))

                for j in range(Y_BY_DVE):
                    ch.add(dve.tensor_tensor(y[:, j, :], y[:, j, :], r_post[:, :], ALU.mult))
                for j in range(KT):
                    if j < Y_BY_DVE:
                        ch.settle(Y_BY_DVE - 1 - j)
                    else:
                        dve.wait_ge(y_scaled.sem, y_scaled.at(L, stage * (KT - Y_BY_DVE) + j - Y_BY_DVE + 1))
                        apart(dve)
                    add(j)
                    if u_norm is not None and j:
                        rest_of_u(L, stage + 1, u_norm, j - 1)
                if u_norm is not None:
                    rest_of_u(L, stage + 1, u_norm, KT - 1)

            def ffn(L, which):
                m = FT * (which - 1)
                t0 = tile_at(f"gateup{which}", 0)
                n0 = LOAD_AT[f"gateup{which}", 0]

                def at(sig, n, i):
                    v = sig.at(L, n)
                    return v if i is None else v + i * 2

                def step(n, i=None, split=True):
                    h = n % 2
                    dve.wait_ge(tile_done.sem, at(tile_done, t0 + n + 1, i))
                    apart(dve)
                    dve.wait_ge(hidden_ready.sem, at(hidden_ready, m + n - 1, i))
                    apart(dve)
                    dve.tensor_tensor(gate_in[:, h, :], ps[:, 2 * h, 0:T], r_pre[:, :], ALU.mult
                                      ).then_inc(*once(gate_scaled))
                    dve.tensor_tensor(up_out[:, h, :], ps[:, 2 * h + 1, 0:T], r_pre[:, :], ALU.mult
                                      ).then_inc(*once(pair_read))
                    if split:
                        split_lo(L, n0 + n + 2, i)
                    dve.wait_ge(pair_read.sem, at(pair_read, m + n + 1, i))
                    apart(dve)
                    dve.wait_ge(gate_acted.sem, at(gate_acted, m + n + 1, i))
                    apart(dve)
                    if i is None:
                        tile = hidden_hi[:, n, :]
                    else:
                        tile = hidden_hi[:, bass.ds(i * 2 + h, 1), :].rearrange("p a t -> p (a t)")
                    dve.tensor_tensor(tile, gate_out[:, h, :], up_out[:, h, :], ALU.mult
                                      ).then_inc(*once(hidden_hi_ready))

                split_lo(L, n0 + 2)
                dve.wait_ge(r_pre_ready.sem, r_pre_ready.at(L, 1 if which == 1 else 3))
                apart(dve)
                step(0, split=False)
                step(1)
                counts.times = FT // 2 - 2
                with dve.Fori(1, FT // 2 - 1) as i:
                    step(0, i)
                    step(1, i)
                counts.times = 1
                step(FT - 2)
                step(FT - 1)
                for j in range(2, KT):
                    split_lo(L, LOAD_AT[f"down{which}", j])
                if which == 2:
                    split_lo(L, LOAD_AT["ple", 0])

            def mix_tile(L, kind, i, k):
                n = tile_at(kind, i, k)
                dve.wait_ge(tile_done.sem, tile_done.at(L, n + 1))
                apart(dve)
                return ps[:, mix_bank_of(n - tile_at("iq", 0)), :]

            def auxd(L, name):
                k = AUXD[name]
                dve.wait_ge(auxd_done.sem, auxd_done.at(L, k + 1))
                apart(dve)
                return ps[:, (2, 7)[k % 2], :]

            def mark(name, ins):
                ins.then_inc(*once(scored))
                assert totals == {} or scored.seen[1] == EV[name], (name, scored.seen)

            def own(s, L, n):
                dve.wait_ge(s.sem, s.at(L, n))
                apart(dve)

            def rope_feature(L, raw, dst, dst_s, j, name):
                bank = auxd(L, name)
                ch.add(dve.tensor_tensor(rope_tmp[:, 0, :], bank[:, 0:T], sin_f[:, :], ALU.mult))
                ch.add(dve.tensor_tensor(rope_tmp[:, 1, :], raw[:, j, :], cos_f[:, :], ALU.mult))
                ch.settle()
                dve.tensor_tensor(dst[:, j, :], rope_tmp[:, 0, 0:TP], rope_tmp[:, 1, 0:TP], ALU.add)
                a, b = (rope_tmp[:, n, TP:T].rearrange("p (b t) -> p b t", b=SEQS) for n in range(2))
                dve.tensor_tensor(dst_s[:, :, j, :], a, b, ALU.add).then_inc(*once(auxd_read))
                own(auxd_read, L, AUXD[name] + 1)

            def top_rounds(score, rounds, m):
                for _ in range(rounds):
                    ch(dve.max(top8[0:m, :], score))
                    ch(dve.match_replace(score, top8[0:m, :], score, TAKEN))

            def top_mask(score):
                ch(dve.tensor_scalar(score, score, TAKEN / 2, NEG, ALU.is_gt, ALU.mult))

            counts.in_layer = 1
            with dve.Fori(0, LAYERS) as L:
                ch.enter(L)
                own(x_ready, L, 0)
                ch.add(dve.tensor_copy(gain[:, :, :], gains[:, :, bass.ds(L, 1), :].rearrange("p a l k -> p a (l k)")))
                ch.add(dve.tensor_copy(bound[:, 0, :], bounds[:, bass.ds(L, 1), :].rearrange("p l h -> p (l h)")))
                ch.add(dve.tensor_copy(bound[:, 2, 0:1], small[:, bass.ds(L + 8, 1)]))
                ch.settle()
                dve.tensor_scalar(bound[:, 1, :], bound[:, 0, :], -1.0, 1.0, ALU.mult, ALU.add
                                  ).then_inc(*once(gain_ready))
                split_lo(L, 0)
                for j in range(KT):
                    rest_of_u(L, 0, 0, j)
                split_lo(L, 1)
                norm_in(L, 0)
                ffn(L, 1)
                dve.wait_ge(late_in.sem, 16)
                norm_out(L, 0, 1)
                norm_in(L, 1)
                dve.wait_ge(r_pre_ready.sem, r_pre_ready.at(L, 2))
                apart(dve)

                def feature_tile(kind, i, k, dst):
                    bank = mix_tile(L, kind, i, k)
                    dve.tensor_tensor(dst[:, 2 * i + k, :], bank[:, 0:T], r_pre[:, :], ALU.mult
                                      ).then_inc(*once(mix_read))

                def tile_no(kind, i, k):
                    return tile_at(kind, i, k) - tile_at("iq", 0) + 1

                feature_tile("iq", 0, 0, raw_iq)
                feature_tile("iq", 0, 1, raw_iq)
                feature_tile("iq", 1, 0, raw_iq)
                feature_tile("iq", 1, 1, raw_iq)
                bank = auxd(L, "r_tok")
                dve.tensor_copy(r_tok[:, 0:2], bank[:, 0:2])
                dve.tensor_copy(r_tok[0:TS, 2:3], bank[0:TS, 2:3]).then_inc(*once(auxd_read))
                own(auxd_read, L, AUXD["r_tok"] + 1)
                for t, (_, m) in enumerate(TOK_TILES):
                    bank = mix_tile(L, "kv", 0, t)
                    dve.tensor_scalar(kv_tok[0:m, t, :], bank[0:m, 0:256], r_tok[0:m, t:t + 1], None, ALU.mult
                                      ).then_inc(*once(mix_read))
                    rope_feature(L, raw_iq, iq, iq_s, t, f"rot_iq{t}")
                rope_feature(L, raw_iq, iq, iq_s, 3, "rot_iq3")
                for t, (_, m) in enumerate(TOK_TILES):
                    bank = mix_tile(L, "ikiw", 0, t)
                    ch.add(dve.tensor_scalar(iw_tok[0:m, t, :], bank[0:m, 64:72], r_tok[0:m, t:t + 1],
                                             NH ** -0.5, ALU.mult, ALU.mult))
                    dve.tensor_scalar(ik_tok[0:m, t, 0:64], bank[0:m, 0:64], r_tok[0:m, t:t + 1], None, ALU.mult
                                      ).then_inc(*once(mix_read))
                for i in range(2):
                    for k in range(2):
                        feature_tile("hf", i, k, hk)
                bank = auxd(L, "iwT")
                dve.tensor_copy(iwT[:, :], bank[0:NH, 0:TS]).then_inc(*once(auxd_read))
                bank = auxd(L, "iwrow")
                dve.tensor_tensor(iw_mask[:, :, :],
                                  bank[:, 0:TS].rearrange("p (a t) -> p a t", a=1).to_broadcast([P, 4, TS]),
                                  own_token[:, :, :], ALU.mult).then_inc(*once(auxd_read))
                dve.wait_ge(hg_exp.sem, hg_exp.at(L, 1))
                apart(dve)
                for h in range(HG):
                    ch.add(dve.tensor_scalar(hb[:, h, :], hb[:, h, :], bound[:, 1, h:h + 1], bound[:, 0, h:h + 1],
                                             ALU.mult, ALU.add))
                ch.settle()
                dve.tensor_scalar(hk[:, :, :], hb[:, :, :], -1.0, 1.0, ALU.mult, ALU.add).then_inc(*once(hg_dve))
                assert hg_dve.seen[1] == HGD["f"]
                for i in range(2):
                    for k in range(2):
                        feature_tile("hq", i, k, hq)
                fills = {1: (score1, causal[:, 0:256], 256), 0: (score0, causal[:, 128:256], 128)}
                for t in (1, 0):
                    score, fill, keys = fills[t]
                    order = [0, 1, 4, 5, 2, 3, 6, 7] if t else range(NH)
                    for m, h in enumerate(order):
                        n = BIG["idx"] + (m // 2 + 1 if t else 5 + m // 4)
                        if m % (2 if t else 4) == 0:
                            dve.wait_ge(big_read_act.sem, big_read_act.at(L, n))
                            apart(dve)
                        ins = dve.scalar_tensor_tensor(out=score[:, :], in0=relu_p[:, h, 0:keys],
                                                       scalar=iw_tok[:, t, h:h + 1],
                                                       in1=fill if m == 0 else score[:, :],
                                                       op0=ALU.mult, op1=ALU.add)
                        if m == NH - 1:
                            mark(f"score{t}", ins)
                            own(scored, L, EV[f"score{t}"])
                        else:
                            ch(ins)
                bank = auxd(L, "score_s")
                ch.add(dve.memset(score_s[:, 0:PADS], SENTINEL))
                ch.add(dve.tensor_copy(score_s[:, PADS:PADS + PAST], bank[0:TS, 0:PAST]))
                dve.tensor_tensor(score_s[:, PADS + PAST:], bank[0:TS, PAST:KEYS_S], causal_s[:, :], ALU.add
                                  ).then_inc(*once(auxd_read))
                own(auxd_read, L, AUXD["score_s"] + 1)
                dve.wait_ge(hg_exp.sem, hg_exp.at(L, 2))
                apart(dve)
                dve.tensor_scalar(hq[:, :, :], scaled[1][:, :, :], P ** -0.5, None, ALU.mult
                                  ).then_inc(*once(hg_dve))
                own(hg_dve, L, HGD["silu"])
                dve.wait_ge(hg_exp.sem, hg_exp.at(L, 3))
                apart(dve)
                for h in range(HG):
                    ins = dve.tensor_tensor_scan(hb[:, h, :], carry[:, :], decay[0][:, h, :], 0.0, ALU.mult, ALU.add)
                ins.then_inc(*once(hg_dve))
                assert hg_dve.seen[1] == HGD["scan"]
                assert ROUNDS_P == 8
                for i in range(2):
                    for k in range(2):
                        feature_tile("q", i, k, raw_q)
                        top_rounds(score1[:, :], 2, P)
                top_mask(score1[:, :])
                for n in range(6):
                    i, t = n // 3, n % 3
                    m = TOK_TILES[t][1]
                    bank = mix_tile(L, "hi", i, t)
                    dve.tensor_scalar(v_tok[0:m, t, 256 * i:256 * i + 256], bank[0:m, 0:256],
                                      r_tok[0:m, t:t + 1], None, ALU.mult).then_inc(*once(mix_read))
                    if n < 4:
                        top_rounds(score0[:, :], 2, P)
                        rope_feature(L, raw_q, q, q_s, n, f"rot_q{n}")
                    elif n == 4:
                        ch(dve.tensor_tensor(score1[:, :], score1[:, :], causal[:, 0:256], ALU.add))
                        top_mask(score0[:, :])
                        ch(dve.tensor_tensor(score0[:, :], score0[:, :], causal[:, 128:256], ALU.add))
                    else:
                        top_rounds(score_s[:, :], 2, TS)

                def big(n):
                    dve.wait_ge(big_done.sem, big_done.at(L, n + 1))
                    apart(dve)
                    return ps[:, 4 + n % 2, :]

                n = BIG["levels"]
                for c in range(2):
                    b = big(n)
                    dve.tensor_tensor(att_p[:, c], b.rearrange("p (h t) -> p h t", h=HG),
                                      identity[:, :].rearrange("p (a t) -> p a t", a=1).to_broadcast([P, HG, P]),
                                      ALU.mult).then_inc(*once(big_read_dve))
                    n += 1
                b = big(n)
                dve.tensor_tensor(att_s[:, :, :], b[0:TS, 0:HG * TS].rearrange("p (h t) -> p h t", h=HG),
                                  identity[0:TS, 0:TS].rearrange("p (a t) -> p a t", a=1).to_broadcast([TS, HG, TS]),
                                  ALU.mult).then_inc(*once(big_read_dve))
                n += 1

                def products(lv):
                    h = LEVELS[lv]
                    dve.wait_ge(decay_ready.sem, decay_ready.at(L, lv + 1))
                    apart(dve)
                    if lv >= 2:
                        dve.wait_ge(big_done.sem, big_done.at(L, LEVEL_BIG[lv - 2][-1] + 1))
                        apart(dve)
                    e, s = level_view(decay[lv % 2], h), level_view(scaled[lv % 2], h)
                    a, b = level_view(hk, h), level_view(hq, h)
                    dve.tensor_tensor(s[0], a[0], e[0], ALU.mult)
                    dve.tensor_tensor(s[1], b[1], e[1], ALU.mult).then_inc(*once(scaled_ready))

                def keep(lv):
                    own(big_read_dve, L, BIGD_BEFORE(LEVEL_BIG[lv][0]))
                    for c, k in enumerate(LEVEL_BIG[lv]):
                        b = big(k)
                        if c < 2:
                            m = level_masks[:, lv, :].rearrange("p (a t) -> p a t", a=1).to_broadcast([P, HG, P])
                            dve.copy_predicated(att_p[:, c], m, b.rearrange("p (h t) -> p h t", h=HG)
                                                ).then_inc(*once(big_read_dve))
                        else:
                            m = level_masks[0:TS, lv, 0:TS].rearrange("p (a t) -> p a t", a=1)
                            dve.copy_predicated(att_s[:, :, :], m.to_broadcast([TS, HG, TS]),
                                                b[0:TS, 0:HG * TS].rearrange("p (h t) -> p h t", h=HG)
                                                ).then_inc(*once(big_read_dve))

                products(0)
                for lv in range(len(LEVELS)):
                    if lv + 1 < len(LEVELS):
                        products(lv + 1)
                    keep(lv)
                own(big_read_dve, L, BIGD_BEFORE(BIG["att"]))
                nl = len(LEVELS)
                dve.wait_ge(decay_ready.sem, decay_ready.at(L, nl + 1))
                apart(dve)
                ch(dve.tensor_tensor(hq[:, :, :], hq[:, :, :], decay[0][:, :, :], ALU.mult))
                dve.wait_ge(decay_ready.sem, decay_ready.at(L, nl + 2))
                apart(dve)
                dve.tensor_tensor(scaled[0][:, :, :], hk[:, :, :], decay[1][:, :, :], ALU.mult
                                  ).then_inc(*once(att_ready))
                own(att_ready, L, 1)
                feature_tile("hgate", 0, 0, hgate)
                bank = auxd(L, "state0")
                dve.tensor_copy(s_mid[:, :, :].rearrange("p h e -> p (h e)"), bank).then_inc(*once(auxd_read))
                own(auxd_read, L, AUXD["state0"] + 1)
                bank = auxd(L, "state1")
                for h in range(HG):
                    ins = dve.scalar_tensor_tensor(out=s_end[:, h, :], in0=s_mid[:, h, :],
                                                   scalar=decay[0][:, h, TP - 1:TP],
                                                   in1=bank[:, h * P:(h + 1) * P], op0=ALU.mult, op1=ALU.add)
                ins.then_inc(*once(auxd_read))
                own(auxd_read, L, AUXD["state1"] + 1)
                dve.sem_inc(*once(states_done))
                feature_tile("hgate", 0, 1, hgate)
                top_rounds(score_s[:, :], ROUNDS_S - 2, TS)
                top_mask(score_s[:, :])
                dve.tensor_tensor(score_s[:, PADS + PAST:], score_s[:, PADS + PAST:], causal_s[:, :], ALU.add
                                  ).then_inc(*once(att_ready))
                own(att_ready, L, 2)
                feature_tile("hgate", 1, 0, hgate)
                bank = auxd(L, "ms_o")
                dve.tensor_scalar(decay[1][:, 0, :], bank[:, 0:T], EPS, float(P) ** -2, ALU.add, ALU.mult
                                  ).then_inc(*once(auxd_read))
                for h in range(HG):
                    dve.wait_ge(state_decayed.sem, state_decayed.at(L, h + 1))
                    apart(dve)
                    for half in range(2):
                        bank = auxd(L, f"state_s{h}{'ab'[half]}")
                        v = state[:, 4 * half:4 * half + 4, h, :]
                        dve.tensor_tensor(v, v, bank.rearrange("p (b e) -> p b e", b=4), ALU.add
                                          ).then_inc(*once(auxd_read))
                    if h == 2:
                        dve.reciprocal(decay[1][:, 0, :], decay[1][:, 0, :]).then_inc(*once(inv_o_ready))
                own(auxd_read, L, AUXD["state_s3b"] + 1)
                dve.sem_inc(*once(states_done))
                for h in range(HG):
                    bank = auxd(L, f"r_o{h}")
                    dve.scalar_tensor_tensor(out=o_hg[:, h, :], in0=o_hg[:, h, :], scalar=bound[:, 2, 0:1],
                                             in1=bank[:, 0:T], op0=ALU.mult, op1=ALU.mult
                                             ).then_inc(*once(auxd_read))

                def mask_scores(t):
                    score, _, keys = fills[t]
                    per = 512 // keys
                    b0 = BIG["att"] if t else BIG["att0"]
                    order = [(0, 0), (1, 0), (0, 2), (1, 2)] if t else [(0, 0), (1, 0)]
                    for k, (g, j) in enumerate(order):
                        b = big(b0 + k)
                        for a in range(per):
                            h = 4 * g + j + a
                            ins = dve.tensor_tensor_reduce(probs[t][:, h, 0:keys], b[:, a * keys:(a + 1) * keys],
                                                           score[:, :], 1.0, TAKEN, ALU.add, ALU.max,
                                                           peak[:, t, h:h + 1])
                        ins.then_inc(*once(big_read_dve))
                    own(big_read_dve, L, BIGD_BEFORE(b0 + len(order)))
                    dve.tensor_scalar(peak[:, t, :], peak[:, t, :], -(HD ** -0.5), None, ALU.mult
                                      ).then_inc(*once(masked))

                def normalise(t):
                    keys = fills[t][2]
                    dve.wait_ge(exped.sem, exped.at(L, SOFT[t]))
                    apart(dve)
                    ch(dve.reciprocal(total[:, t, :], total[:, t, :]))
                    for h in range(NH):
                        ins = dve.tensor_scalar(probs[t][:, h, 0:keys], probs[t][:, h, 0:keys], total[:, t, h:h + 1],
                                                None, ALU.mult)
                    ins.then_inc(*once(normed))

                def keep_attended(name, t0, m):
                    bank = auxd(L, name)
                    out = bank.rearrange("p (j t) -> p j t", j=4)
                    ch(dve.tensor_copy(mixed_hi[:, 0:4, t0:t0 + m], out))
                    dve.tensor_tensor(mixed_lo[:, 0:4, t0:t0 + m], out,
                                      mixed_hi[:, 0:4, t0:t0 + m].bitcast(F32), ALU.subtract
                                      ).then_inc(*once(auxd_read))

                mask_scores(1)
                for pair in range(4):
                    b = big(BIG["att_s"] + pair)
                    dve.tensor_copy(probs_s[:, pair, :], b[:, 0:KEYS_S]).then_inc(*once(big_read_dve))
                own(big_read_dve, L, BIGD_BEFORE(BIG["att_s"] + 4))
                ch(dve.tensor_reduce(peak[:, 2, 0:4], probs_s[:, :, :], AX.X, ALU.max))
                dve.tensor_scalar(peak[:, 2, 0:4], peak[:, 2, 0:4], -(HD ** -0.5), None, ALU.mult
                                  ).then_inc(*once(masked))
                mask_scores(0)
                feature_tile("hgate", 1, 1, hgate)
                normalise(1)
                dve.wait_ge(exped.sem, exped.at(L, SOFT["samples"]))
                apart(dve)
                ch(dve.reciprocal(total[:, 2, 0:4], total[:, 2, 0:4]))
                for pair in range(4):
                    ins = dve.tensor_scalar(probs_s[:, pair, :], probs_s[:, pair, :], total[:, 2, pair:pair + 1],
                                            None, ALU.mult)
                ins.then_inc(*once(normed))
                normalise(0)
                keep_attended("pv1", 128, 128)
                own(auxd_read, L, AUXD["r_o3"] + 1)
                dve.wait_ge(hg_exp.sem, hg_exp.at(L, 4))
                apart(dve)
                ch(dve.tensor_tensor(o_hg[:, :, :], o_hg[:, :, :], hgate[:, :, :], ALU.mult))
                ch(dve.tensor_copy(mixed_hi[:, 4:8, :], o_hg[:, :, :]))
                dve.tensor_tensor(mixed_lo[:, 4:8, :], o_hg[:, :, :], mixed_hi[:, 4:8, :].bitcast(F32),
                                  ALU.subtract).then_inc(*once(attended))
                split_lo(L, LOAD_AT["out", 0])
                split_lo(L, LOAD_AT["out", 1])
                bank = auxd(L, "pvs").rearrange("p (b g j t) -> p j b g t", b=SEQS, g=2, j=4)
                for g in range(2):
                    rows = slice(64 * g, 64 * g + 64)
                    dst = mixed_hi[rows, 0:4, TP:T].rearrange("p j (b t) -> p j b t", b=SEQS)
                    ch.add(dve.tensor_copy(dst, bank[rows, :, :, g, :]))
                ch.settle()
                for g in range(2):
                    rows = slice(64 * g, 64 * g + 64)
                    hi, lo = (a.rearrange("p j (b t) -> p j b t", b=SEQS)
                              for a in (mixed_hi[rows, 0:4, TP:T].bitcast(F32), mixed_lo[rows, 0:4, TP:T]))
                    ins = dve.tensor_tensor(lo, bank[rows, :, :, g, :], hi, ALU.subtract)
                ins.then_inc(*once(auxd_read))
                keep_attended("pv0", 0, 128)
                own(auxd_read, L, AUXD["pv0"] + 1)
                dve.sem_inc(*once(attended))
                split_lo(L, LOAD_AT["out", 2])
                split_lo(L, LOAD_AT["out", 3])
                split_lo(L, LOAD_AT["gateup2", 0])
                norm_out(L, 1, 3, 4)
                split_lo(L, LOAD_AT["gateup2", 1])
                norm_in(L, 2)
                dve.wait_ge(pT_hi_ready.sem, pT_hi_ready.at(L, 1))
                apart(dve)
                dve.tensor_tensor(pT_lo[:, :, :], pT[:, :, :], pT_hi[:, :, :].bitcast(F32), ALU.subtract
                                  ).then_inc(*once(pT_lo_ready))
                ffn(L, 2)
                norm_out(L, 2, 5, 6)
                norm_in(L, 3)
                split_lo(L, LOAD_AT["ple", 1])
                dve.wait_ge(r_pre_ready.sem, r_pre_ready.at(L, 4))
                apart(dve)
                for j in range(KT):
                    b = ple_bank(j)
                    dve.wait_ge(tile_done.sem, tile_done.at(L, tile_at("ple", j // 2, j % 2) + 1))
                    dve.tensor_tensor(gate_in[:, j % 2, :], ps[:, b, 0:T], r_pre[:, :], ALU.mult
                                      ).then_inc(*once(gate_scaled))
                    dve.wait_ge(gate_acted.sem, gate_acted.at(L, 2 * FT + j + 1))
                    dve.tensor_tensor(y[:, j, :], ps[:, b + 1, 0:T], gate_out[:, j % 2, :], ALU.mult
                                      ).then_inc(*once(pair_read))
                    if j in (1, 3):
                        split_lo(L, LOAD_AT["ple", j // 2 + 2])
                norm_out(L, 3, 7)
            counts.in_layer = 2
            for n in range(6):
                dve.wait_ge(final_turned.sem, n + 1)
                t, half = n // 2, n % 2
                m = TOK_TILES[t][1]
                dve.tensor_copy(tokens[0:m, t, 512 * half:512 * half + 512], ps[0:m, n, :]
                                ).then_inc(*once(final_copied))

        @block.tensor
        def _(pe):
            counts.in_layer = 0
            pe.wait_ge(tokens_in.sem, 32)
            pe.wait_ge(early_in.sem, 16 * 3)
            for k in range(KT):
                for t, (a, m) in enumerate(TOK_TILES):
                    ins = pe.transpose(ps[:, k, a:a + m], tokens[0:m, t, k * P:(k + 1) * P], identity[0:m, 0:m])
                ins.then_inc(*once(turned))
            pe.wait_ge(turned_read.sem, 1)
            pe.transpose(ps[:, 0, 320:448], rows_a[:, :], identity[:, :]).then_inc(*once(turned))
            pe.wait_ge(turned_read.sem, 2)
            pe.transpose(ps[:, 1, 320:330], rows_b[:, :], identity[0:10, 0:10]).then_inc(*once(turned))
            pe.wait_ge(turned_read.sem, KT + 2)
            pe.wait_ge(setup_done.sem, 1)

            def wait(s, value):
                pe.wait_ge(s.sem, value)
                apart(pe)

            def slot_full(L, n, i=None):
                full = slot_in[n % 2]
                value = full.at(L, dma_count_before(n) + 16 * DMAS(n))
                if i is not None:
                    value = value + i * (16 * DMAS(n))
                pe.wait_ge(full.sem, value)

            def mean_x(L, stage):
                wait(squarex_added, squarex_added.at(L, (stage + 1) * ADDS))
                pe.matmul(ps[:, 7, 0:T], mean_model[:, :], sumsq[:, :], start=True, stop=False)
                wait(squarex_ready, squarex_ready.at(L, (stage + 1) * KT))
                pe.matmul(ps[:, 7, 0:T], mean_model[:, :], sq[:, (KT - 1) % 4, :], start=False, stop=True
                          ).then_inc(*once(msx_ready))

            def mean_y(L, stage):
                wait(square_added, square_added.at(L, (stage + 1) * ADDS))
                pe.matmul(ps[:, 6, 0:T], mean_model[:, :], sumsq[:, :], start=True, stop=False)
                wait(square_ready, square_ready.at(L, (stage + 1) * KT))
                pe.matmul(ps[:, 6, 0:T], mean_model[:, :], sq[:, (KT - 1) % 4, :], start=False, stop=True
                          ).then_inc(*once(ms_ready))

            def product(bank, weights, rhs, last=None):
                n = len(rhs)
                for k in range(n):
                    ins = pe.matmul(bank, weights(k), rhs[k], start=(k == 0), stop=(k == n - 1))
                if last is not None:
                    ins.then_inc(*last)

            def product_split(bank, hi, lo, rhs_hi, rhs_lo, last=None, first=0, end=None):
                n = len(rhs_hi)
                for k in range(first, n if end is None else end):
                    pe.matmul(bank, hi(k), rhs_hi[k], start=(k == 0), stop=False)
                    pe.matmul(bank, hi(k), rhs_lo[k], start=False, stop=False)
                    ins = pe.matmul(bank, lo(k), rhs_hi[k], start=False, stop=(k == n - 1))
                if last is not None:
                    ins.then_inc(*last)

            def us(a=0, b=T):
                return [u[:, k, a:b] for k in range(KT)]

            def ffn(L, which, stage):
                n0 = LOAD_AT[f"gateup{which}", 0]
                m = FT * (which - 1)

                u_parts = [[t[:, k, :] for k in range(KT)] for t in (u_hi, u_lo)]

                def tile(half, i=None):
                    v = slot_lo_ready.at(L, splits_before(n0) + half + 1)
                    pe.wait_ge(slot_lo_ready.sem, v if i is None else v + i * 2)
                    apart(pe)
                    hi, lo = (t[(n0 + half) % 2][:, 0:2 * KT * P].rearrange("p (a k n) -> p a k n", a=2, k=KT)
                              for t in (slot_hi, slot_lo))
                    v = pair_read.at(L, m + half - 1)
                    pe.wait_ge(pair_read.sem, v if i is None else v + i * 2)
                    parts = (ps[:, 2 * half, 0:T], lambda k: hi[:, 0, k, :], lambda k: lo[:, 0, k, :], *u_parts)
                    up = (ps[:, 2 * half + 1, 0:T], lambda k: hi[:, 1, k, :], lambda k: lo[:, 1, k, :], *u_parts)
                    if half == 0 and i is None:
                        for k in range(KT):
                            wait(u_lo_ready, u_lo_ready.at(L, stage // 2 * KT + k + 1))
                            product_split(*parts, first=k, end=k + 1)
                            product_split(*up, once(tile_done) if k == KT - 1 else None, first=k, end=k + 1)
                        return
                    if half == 1 and i is None:
                        product_split(*parts, end=KT // 2)
                        mean_x(L, stage)
                        product_split(*parts, first=KT // 2)
                    else:
                        product_split(*parts)
                    product_split(*up, once(tile_done))

                tile(0)
                tile(1)
                apart(pe)
                counts.times = FT // 2 - 1
                with pe.Fori(1, FT // 2) as i:
                    for half in range(2):
                        tile(half, i)
                counts.times = 1
                n0 = LOAD_AT[f"down{which}", 0]
                wait(hidden_ready, hidden_ready.at(L, m + FT - 2))
                y0 = (0 if which == 1 else 2) * KT
                counts.times = KT // 2
                with pe.Fori(0, KT // 2) as i:
                    for half in range(2):
                        pe.wait_ge(slot_lo_ready.sem,
                                   slot_lo_ready.at(L, splits_before(n0) + half + 1) + i * 2)
                        apart(pe)
                        hi, lo = (t[(n0 + half) % 2][:, :].rearrange("p (f n) -> p f n", f=FT)
                                  for t in (slot_hi, slot_lo))
                        pe.wait_ge(square_ready.sem, square_ready.at(L, y0 + half - 1) + i * 2)
                        parts = (ps[:, 4 + half, 0:T], lambda k: hi[:, k, :], lambda k: lo[:, k, :],
                                 [hidden_hi[:, k, :] for k in range(FT)],
                                 [hidden_lo[:, k, :] for k in range(FT)])
                        product_split(*parts, end=FT - 2)
                        if half == 0:
                            wait(hidden_ready, hidden_ready.at(L, m + FT))
                        product_split(*parts, once(tile_done), first=FT - 2)
                counts.times = 1
                mean_y(L, 0 if which == 1 else 2)

            def mix_bank(L, n):
                if n < 2 or n >= 4:
                    wait(mix_read, mix_read.at(L, n - 1))
                return ps[:, mix_bank_of(n), :]

            base = tile_at("iq", 0)

            def feature_tile(L, kind, i, k):
                if k == 0:
                    slot_full(L, LOAD_AT[kind, i])
                    apart(pe)
                bank = mix_bank(L, tile_at(kind, i, k) - base)
                s = slots[LOAD_AT[kind, i] % 2][:, 0:KT * 256].rearrange("p (k n) -> p k n", k=KT)
                product(bank[:, 0:T], lambda c: s[:, c, 128 * k:128 * k + 128], us(), once(tile_done))

            def token_tiles(L, kind, i, width, after=None):
                slot_full(L, LOAD_AT[kind, i])
                apart(pe)
                s = slots[LOAD_AT[kind, i] % 2][:, 0:KT * width].rearrange("p (k n) -> p k n", k=KT)
                for t, (a, m) in enumerate(TOK_TILES):
                    bank = mix_bank(L, tile_at(kind, i, t) - base)
                    product(bank[0:m, 0:width], lambda c: u[:, c, a:a + m],
                            [s[:, c, :] for c in range(KT)], once(tile_done))
                    if after is not None:
                        after(t)

            def rotation(L, what, raw, j):
                bank = auxd(L, f"rot_{what}{j}")
                if j == 0:
                    wait(mix_read, mix_read.at(L, tile_at(what, 1, 1) - base + 1))
                pe.matmul(bank[:, 0:T], rotate[:, :], raw[:, j, :], start=True, stop=True
                          ).then_inc(*once(auxd_done))

            def aux(L, table, name, done, read):
                k = table[name]
                wait(read, read.at(L, k - 1))
                return ps[:, ((2, 7) if table is AUXD else (3, 6))[k % 2], :]

            def auxd(L, name):
                return aux(L, AUXD, name, auxd_done, auxd_read)

            def auxa(L, name):
                return aux(L, AUXA, name, auxa_done, auxa_read)

            def big(L, n):
                return ps[:, 4 + n % 2, :]

            def sample_scores(bank, queries, new, past, b, start):
                for g in range(2):
                    rows = slice(64 * g, 64 * g + 64)
                    out = bank[64 * (b % 2) + 32 * g:64 * (b % 2) + 32 * g + 32]
                    lhs = queries[rows, b].rearrange("p j t -> p (j t)")
                    pe.matmul(out[:, 0:PAST], lhs,
                              past[rows, 2 * b:2 * b + 2, :].rearrange("p n t -> p (n t)"),
                              start=start, stop=True, skip_group_check=True)
                    ins = pe.matmul(out[:, PAST:KEYS_S], lhs, new[rows, TP:T], start=start, stop=True,
                                    skip_group_check=True)
                return ins

            counts.in_layer = 1
            with pe.Fori(0, LAYERS) as L:
                ffn(L, 1, 0)
                pe.wait_ge(late_in.sem, 16)
                slot_full(L, LOAD_AT["iq", 0])
                apart(pe)
                banks = [mix_bank(L, k) for k in range(2)]
                s = slots[LOAD_AT["iq", 0] % 2][:, 0:KT * 256].rearrange("p (k n) -> p k n", k=KT)
                for c in range(KT):
                    wait(u_ready, u_ready.at(L, KT + c + 1))
                    for k in range(2):
                        ins = pe.matmul(banks[k][:, 0:T], s[:, c, 128 * k:128 * k + 128], u[:, c, :],
                                        start=(c == 0), stop=(c == KT - 1))
                        if c == KT - 1:
                            ins.then_inc(*once(tile_done))
                mean_x(L, 1)
                feature_tile(L, "iq", 1, 0)
                feature_tile(L, "iq", 1, 1)
                wait(r_pre_ready, r_pre_ready.at(L, 2))
                bank = auxd(L, "r_tok")
                for t, (a, m) in enumerate(TOK_TILES):
                    ins = pe.matmul(bank[0:m, t:t + 1], r_pre[0:1, a:a + m], identity[0:1, 0:1],
                                    start=True, stop=True)
                ins.then_inc(*once(auxd_done))
                wait(embeddings_in, embeddings_in.at(L, 32))
                for k in range(2):
                    bank = auxa(L, f"p{k}")
                    for t, (a, m) in enumerate(TOK_TILES):
                        ins = pe.transpose(bank[:, a:a + m], p_tok[0:m, t, k * P:(k + 1) * P], identity[0:m, 0:m])
                    ins.then_inc(*once(auxa_done))
                token_tiles(L, "kv", 0, 256, lambda t: rotation(L, "iq", raw_iq, t))
                rotation(L, "iq", raw_iq, 3)
                token_tiles(L, "ikiw", 0, 72)
                wait(caches_in, caches_in.at(L, 16 * 48))
                for src, name in ((k_pages[:, :, :], "kpages"),
                                  (i_pages[:, :, :, :].rearrange("p n a d -> p n (a d)"), "ipages")):
                    for k in range(4):
                        bank = auxa(L, f"{name}{k}")
                        for n in range(4):
                            ins = pe.transpose(bank[:, n * P:(n + 1) * P], src[:, 4 * k + n, :], identity[:, :])
                        ins.then_inc(*once(auxa_done))
                for i in range(2):
                    for k in range(2):
                        feature_tile(L, "hf", i, k)
                wait(roped, roped.at(L, 1))
                for name, src in (("kT", kv_tok), ("ikT", ik_tok)):
                    bank = auxa(L, name)
                    for t, (a, m) in enumerate(TOK_TILES):
                        ins = pe.transpose(bank[:, a:a + m], src[0:m, t, 0:P], identity[0:m, 0:m])
                    ins.then_inc(*once(auxa_done))
                bank = auxd(L, "iwT")
                pe.transpose(bank[0:NH, 0:TS], iw_tok[0:TS, 2, :], identity[0:TS, 0:TS]
                             ).then_inc(*once(auxd_done))
                wait(auxd_read, auxd_read.at(L, AUXD["iwT"] + 1))
                bank = auxd(L, "iwrow")
                pe.matmul(bank[:, 0:TS], head_row[:, :], iwT[:, :], start=True, stop=True
                          ).then_inc(*once(auxd_done))
                for i in range(2):
                    for k in range(2):
                        feature_tile(L, "hq", i, k)
                wait(auxa_read, auxa_read.at(L, AUXA["ikT"] + 1))
                n = BIG["idx"]

                for kk, q0, order in ((256, 128, [(0, 0), (1, 0), (0, 2), (1, 2)]), (128, 0, [(0, 0), (1, 0)])):
                    for g, j in order:
                        if n >= BIG["idx"] + 2:
                            wait(big_read_act, big_read_act.at(L, n - BIG["idx"] - 1))
                        bank = big(L, n)
                        for a in range(512 // kk):
                            ins = pe.matmul(bank[:, a * kk:(a + 1) * kk],
                                            iq[64 * g:64 * g + 64, j + a, q0:q0 + 128],
                                            ikT[64 * g:64 * g + 64, 0:kk], start=True, stop=True)
                        ins.then_inc(*once(big_done))
                        n += 1
                for pair in range(4):
                    wait(big_read_act, big_read_act.at(L, n - BIG["idx"] - 1))
                    bank = big(L, n)
                    for b2 in range(2):
                        b = 2 * pair + b2
                        ins = sample_scores(bank, iq_s, ikT, ikT_past, b, True)
                    ins.then_inc(*once(big_done))
                    n += 1
                bank = auxd(L, "score_s")
                wait(auxd_read, auxd_read.at(L, AUXD["iwrow"] + 1))
                for pair in range(4):
                    wait(big_read_act, big_read_act.at(L, 7 + pair))
                    ins = pe.matmul(bank[0:TS, 0:KEYS_S], iw_mask[:, pair, :], relu_s[:, pair, :],
                                    start=(pair == 0), stop=(pair == 3))
                ins.then_inc(*once(auxd_done))
                for i in range(2):
                    for k in range(2):
                        feature_tile(L, "q", i, k)
                token_tiles(L, "hi", 0, 256, lambda t: rotation(L, "q", raw_q, t))
                token_tiles(L, "hi", 1, 256, lambda t: rotation(L, "q", raw_q, 3) if t == 0 else None)
                n = BIG["levels"]
                wait(hg_dve, hg_dve.at(L, HGD["scan"]))

                use = [n]

                def chunk(c, a, b):
                    n = use[0]
                    use[0] += 1
                    if n - BIG["levels"] >= 2:
                        wait(big_read_dve, big_read_dve.at(L, BIGD_BEFORE(n - 1)))
                    bank = big(L, n)
                    t0, m = TOK_TILES[c]
                    for h in range(HG):
                        ins = pe.matmul(bank[0:m, h * m:(h + 1) * m], a[:, h, t0:t0 + m], b[:, h, t0:t0 + m],
                                        start=True, stop=True)
                    ins.then_inc(*once(big_done))

                for c in range(3):
                    chunk(c, hk, hq)
                for lv, h in enumerate(LEVELS):
                    wait(scaled_ready, scaled_ready.at(L, lv + 1))
                    for c in range(3 if 2 * h <= STEP else 2):
                        assert use[0] == LEVEL_BIG[lv][c]
                        chunk(c, scaled[lv % 2], scaled[lv % 2])
                feature_tile(L, "hgate", 0, 0)
                wait(att_ready, att_ready.at(L, 1))
                for t, (a, m) in enumerate(TOK_TILES):
                    bank = auxa(L, f"key{t}")
                    for h in range(HG):
                        ins = pe.transpose(bank[0:m, h * P:(h + 1) * P], scaled[0][:, h, a:a + m], identity[:, :])
                    ins.then_inc(*once(auxa_done))
                for t in range(2):
                    wait(auxa_read, auxa_read.at(L, AUXA[f"key{t}"] + 1))
                    bank = auxd(L, f"state{t}")
                    for h in range(HG):
                        ins = pe.matmul(bank[:, h * P:(h + 1) * P], key_tok[:, t, h, :],
                                        v_tok[:, t, h * P:(h + 1) * P], start=True, stop=True)
                    ins.then_inc(*once(auxd_done))
                feature_tile(L, "hgate", 0, 1)
                wait(states_in, states_in.at(L, 16 * 20))
                wait(auxd_read, auxd_read.at(L, AUXD["state0"] + 1))
                for h in range(HG):
                    bank = auxa(L, f"o{h}")
                    v = lambda t, m: v_tok[0:m, t, h * P:(h + 1) * P]
                    pe.matmul(bank[:, 0:128], v(0, P), att_p[:, 0, h, :], start=True, stop=True)
                    pe.matmul(bank[:, 128:256], v(1, P), att_p[:, 1, h, :], start=True, stop=False)
                    pe.matmul(bank[:, 128:256], s_mid[:, h, :], hq[:, h, 128:256], start=False, stop=True)
                    pe.matmul(bank[:, TP:T], v(2, TS), att_s[:, h, :], start=True, stop=True,
                              skip_group_check=True)
                    for b in range(SEQS):
                        ins = pe.matmul(bank[:, TP + b * STEP:TP + (b + 1) * STEP], state[:, b, h, :],
                                        hq[:, h, TP + b * STEP:TP + (b + 1) * STEP], start=False,
                                        stop=True, skip_group_check=True)
                    ins.then_inc(*once(auxa_done))
                feature_tile(L, "hgate", 1, 0)
                bank = auxd(L, "ms_o")
                for h in range(HG):
                    wait(auxa_read, auxa_read.at(L, AUXA[f"o{h}"] + 1))
                    ins = pe.matmul(bank[32 * h:32 * h + 32, 0:T], mean_head[:, 0:32], scaled[1][:, h, :],
                                    start=True, stop=True)
                ins.then_inc(*once(auxd_done))
                wait(auxa_read, auxa_read.at(L, AUXA["key2"] + 1))
                for h in range(HG):
                    wait(v_own_ready, v_own_ready.at(L, h + 1))
                    for half in range(2):
                        bank = auxd(L, f"state_s{h}{'ab'[half]}")
                        pe.matmul(bank, key_tok[0:TS, 2, h, :],
                                  v_own[:, h % 2, 4 * half:4 * half + 4, :].rearrange("p b e -> p (b e)"),
                                  start=True, stop=True).then_inc(*once(auxd_done))
                wait(r_o_ready, r_o_ready.at(L, 1))
                for h in range(HG):
                    bank = auxd(L, f"r_o{h}")
                    pe.matmul(bank[:, 0:T], mean_head[32 * h:32 * h + 1, :], decay[1][32 * h:32 * h + 1, 0, :],
                              start=True, stop=True).then_inc(*once(auxd_done))

                def att_scores(t):
                    n = BIG["att"] if t else BIG["att0"]
                    kk, q0 = (256, 128) if t else (128, 0)
                    for g, j in ([(0, 0), (1, 0), (0, 2), (1, 2)] if t else [(0, 0), (1, 0)]):
                        wait(big_read_dve, big_read_dve.at(L, BIGD_BEFORE(n - 1)))
                        bank = big(L, n)
                        for a in range(512 // kk):
                            ins = pe.matmul(bank[:, a * kk:(a + 1) * kk],
                                            q[64 * g:64 * g + 64, j + a, q0:q0 + 128],
                                            kT[64 * g:64 * g + 64, 0:kk], start=True, stop=True)
                        ins.then_inc(*once(big_done))
                        n += 1

                def turn_probs(t, keys):
                    for k in range(keys):
                        for g in range(2):
                            bank = auxa(L, f"pT{t}_{k}{g}")
                            for a in range(4):
                                ins = pe.transpose(bank[:, a * P:(a + 1) * P],
                                                   probs[t][:, 4 * g + a, k * P:(k + 1) * P], identity[:, :])
                            ins.then_inc(*once(auxa_done))

                def weigh(t, keys):
                    bank = auxd(L, f"pv{t}")
                    for k in range(keys):
                        wait(auxa_read, auxa_read.at(L, AUXA[f"pT{t}_{k}1"] + 1))
                        for g in range(2):
                            ins = pe.matmul(bank[64 * g:64 * g + 64, :], kv_tok[:, k, 128 + 64 * g:192 + 64 * g],
                                            probsT[t][:, k, 4 * g:4 * g + 4, :].rearrange("p h t -> p (h t)"),
                                            start=(k == 0), stop=(k == keys - 1))
                    ins.then_inc(*once(auxd_done))

                assert use[0] == BIG["att"]
                att_scores(1)
                for pair in range(4):
                    n = BIG["att_s"] + pair
                    wait(big_read_dve, big_read_dve.at(L, BIGD_BEFORE(n - 1)))
                    wait(att_ready, att_ready.at(L, 2))
                    bank = big(L, n)
                    pe.matmul(bank[:, 0:KEYS_S], spread[:, pair, :], score_s[:, PADS:], start=True, stop=True,
                              skip_group_check=True)
                    for b2 in range(2):
                        b = 2 * pair + b2
                        ins = sample_scores(bank, q_s, kT, kT_past, b, False)
                    ins.then_inc(*once(big_done))
                att_scores(0)
                feature_tile(L, "hgate", 1, 1)
                wait(normed, normed.at(L, SOFT[1]))
                turn_probs(1, 2)
                weigh(1, 2)
                wait(normed, normed.at(L, SOFT["samples"]))
                for k, (a, m) in enumerate(TOK_TILES):
                    bank = auxa(L, f"pTs{k}")
                    for pair in range(4):
                        ins = pe.transpose(bank[0:m, pair * P:(pair + 1) * P], probs_s[:, pair, a:a + m],
                                           identity[:, :])
                    ins.then_inc(*once(auxa_done))
                wait(normed, normed.at(L, SOFT[0]))
                turn_probs(0, 1)
                wait(auxa_read, auxa_read.at(L, AUXA["pTs2"] + 1))
                bank = auxd(L, "pvs")
                pe.matmul(bank, kv_tok[0:TS, 2, 128:256], probsT_s[0:TS, 2, :, :].rearrange("p n t -> p (n t)"),
                          start=True, stop=True, skip_group_check=True)
                for b in range(SEQS):
                    out = bank[:, 64 * b:64 * b + 64]
                    c = slice(64 * (b % 2), 64 * (b % 2) + 64)
                    for k in range(2):
                        ins = pe.matmul(out, v_pages[:, 2 * b + k, :], probsT_s[:, k, b // 2, c],
                                        start=False, stop=True, skip_group_check=True)
                ins.then_inc(*once(auxd_done))
                weigh(0, 1)
                wait(attended, attended.at(L, 2))
                for i in range(4):
                    n = LOAD_AT["out", i]
                    wait(slot_lo_ready, slot_lo_ready.at(L, splits_before(n) + 1))
                    hi, lo = (t.rearrange("p (k n) -> p k n", k=KT) for t in parts_of(n))
                    for k in range(2):
                        wait(square_ready, square_ready.at(L, KT + 2 * i + k - 1))
                        c128 = slice(128 * k, 128 * k + 128)
                        product_split(ps[:, 4 + k, 0:T], lambda c: hi[:, c, c128], lambda c: lo[:, c, c128],
                                      *([t[:, c, :] for c in range(KT)] for t in (mixed_hi, mixed_lo)),
                                      once(tile_done))
                mean_y(L, 1)
                ffn(L, 2, 2)
                wait(pT_lo_ready, pT_lo_ready.at(L, 1))
                for i in range(4):
                    n = LOAD_AT["ple", i]
                    wait(slot_lo_ready, slot_lo_ready.at(L, splits_before(n) + 1))
                    hi, lo = (t[n % 2][:, 0:split_size(n)].rearrange("p (k n) -> p k n", k=KT + 2)
                              for t in (slot_hi, slot_lo))
                    parts = [[t[:, c, :] for c in range(KT)] for t in (u_hi, u_lo)]
                    p_parts = [[t[:, c, :] for c in range(2)] for t in (pT_hi, pT_lo)]

                    def gate(k, **part):
                        c128 = slice(128 * k, 128 * k + 128)
                        product_split(ps[:, ple_bank(2 * i + k), 0:T], lambda c: hi[:, c, c128],
                                      lambda c: lo[:, c, c128], *parts, **part)

                    def embedding(k):
                        c128 = slice(128 * k, 128 * k + 128)
                        wait(pair_read, pair_read.at(L, 2 * FT + max(0, 2 * i + k - 2)))
                        product_split(ps[:, ple_bank(2 * i + k) + 1, 0:T], lambda c: hi[:, KT + c, c128],
                                      lambda c: lo[:, KT + c, c128], *p_parts)

                    if i == 0:
                        embedding(0)
                        embedding(1)
                        for c in range(KT):
                            wait(u_lo_ready, u_lo_ready.at(L, 2 * KT + c + 1))
                            for k in range(2):
                                gate(k, first=c, end=c + 1, last=once(tile_done) if c == KT - 1 else None)
                        mean_x(L, 3)
                        continue
                    for k in range(2):
                        embedding(k)
                        gate(k, last=once(tile_done))
                mean_y(L, 3)
            counts.in_layer = 2
            pe.wait_ge(x_ready.sem, x_ready.at(LAYERS, 0))
            for n in range(6):
                t, half = n // 2, n % 2
                a, m = TOK_TILES[t]
                for k in range(4):
                    ins = pe.transpose(ps[0:m, n, k * P:(k + 1) * P], x[:, 4 * half + k, a:a + m], identity[:, :])
                ins.then_inc(*once(final_turned))

    return {n: tuple(s.seen) for n, s in signals.items()}


_INS = ["x_prompt", "x_sample", "p_prompt", "p_sample", "cache_k", "cache_v", "cache_idx_k", "state_hgrn",
        "page_table", "n_f1_pre", "n_f1_post", "w_f1_gate", "w_f1_up", "w_f1_down", "n_mix_pre", "n_mix_post",
        "w_in", "hg_lb_logits", "hg_norm", "w_out", "n_f2_pre", "n_f2_post", "w_f2_gate", "w_f2_up", "w_f2_down",
        "n_ple_pre", "n_ple_post", "w_ple_proj", "w_ple_gate"]
_NORMS = ["n_f1_pre", "n_f1_post", "n_mix_pre", "n_mix_post", "n_f2_pre", "n_f2_post", "n_ple_pre", "n_ple_post"]
_ROWS = _NORMS + ["hg_lb_logits", "hg_norm"]
_OUTS = [("y_prompt", (1, TP, DM)), ("y_sample", (SEQS, STEP, DM)),
         ("k_prompt", (LAYERS, 1, TP, KVH, HD)), ("v_prompt", (LAYERS, 1, TP, KVH, HD)),
         ("idx_k_prompt", (LAYERS, 1, TP, HD)), ("hgrn_prompt", (LAYERS, 1, HG, P, P)),
         ("k_sample", (LAYERS, SEQS, STEP, KVH, HD)), ("v_sample", (LAYERS, SEQS, STEP, KVH, HD)),
         ("idx_k_sample", (LAYERS, SEQS, STEP, HD)), ("hgrn_sample", (LAYERS, SEQS, HG, P, P))]


def declared(nc, arrays):
    A = {name: nc.dram_tensor(f"in_{name}", a.shape, mybir.dt.from_np(a.dtype), kind="ExternalInput").ap()
         for name, a in arrays.items()}
    O = {name: nc.dram_tensor(f"out_{name}", shape, F32, kind="ExternalOutput").ap() for name, shape in _OUTS}
    return A, O


def kernel(**inputs):
    import concourse.bacc as _bacc
    from concourse.bass_utils import run_bass_kernel_spmd as _run

    arrays = laid_out(inputs)
    totals = {}
    for _ in range(2):
        nc = _bacc.Bacc("TRN2", target_bir_lowering=False, num_devices=1)
        totals = build(nc, *declared(nc, arrays), totals)
    r = _run(nc, [{f"in_{k}": v for k, v in arrays.items()}], core_ids=[0])
    return tuple(r.results[0][f"out_{name}"] for name, _ in _OUTS)
```
